# Optimizing a Trainium2 kernel written in Bass

```python
import jax, jax.numpy as jnp
from jax import lax
import numpy as np

D_MODEL = 1024
BATCH = 1
SEQ = 512
DEPTH = 2
DEC_BATCH = 8
DEC_SEQ = 1
PAST_LEN = 2048
PAGE_SIZE = 128

N_MIXERS = 2
N_MLA_LAYERS = (DEPTH + 1) // 2
N_POOL_LAYERS = DEPTH // 2
EPS = 1e-6
N_HEADS = 8
QK_NOPE_DIM = 128
QK_ROPE_DIM = 64
V_HEAD_DIM = 128
Q_LORA_RANK = 384
KV_LORA_RANK = 256
CACHE_ROW = KV_LORA_RANK + QK_ROPE_DIM
ROPE_THETA = 10000.0
ATTN_SCALE = (QK_NOPE_DIM + QK_ROPE_DIM) ** -0.5
Q_BLOCK = 128
POOL_WINDOWS = (2, 4, 8, 16)
POOL_GROUPS = len(POOL_WINDOWS)
POOL_GROUP_DIM = D_MODEL // POOL_GROUPS
POOL_STATE_LEN = max(POOL_WINDOWS) - 1
PEER_HEADS = 8
PEER_N_KEYS = 128
PEER_N_EXPERTS = PEER_N_KEYS * PEER_N_KEYS
PEER_TOPK = 16
PEER_QUERY_DIM = 256
PEER_HALF = PEER_QUERY_DIM // 2
PEER_BLOCK = 128
PAGE_POOL_NUM = 5
PAGE_POOL_DEN = 4

kernel_name = 'hybrid_mla_pool_peer_adaln_step'

def rmsnorm(x, g):
    xf = x.astype(jnp.float32)
    y = xf * lax.rsqrt(jnp.mean(xf * xf, axis=-1, keepdims=True) + EPS)
    return (y * g.astype(jnp.float32)).astype(x.dtype)

def modulate(h, shift, scale):
    return h * (1 + scale[:, None, :]) + shift[:, None, :]

def adaln(c, w, b):
    return jnp.split(jax.nn.silu(c) @ w + b, 6, axis=-1)

def rope_tables(pos):
    inv = ROPE_THETA ** (-jnp.arange(0, QK_ROPE_DIM, 2, dtype=jnp.float32) / QK_ROPE_DIM)
    ang = pos.astype(jnp.float32)[:, None] * inv[None, :]
    return jnp.cos(ang), jnp.sin(ang)

def apply_rope(x, cos, sin):
    xf = x.astype(jnp.float32)
    x1, x2 = xf[..., :QK_ROPE_DIM // 2], xf[..., QK_ROPE_DIM // 2:]
    return jnp.concatenate([x1 * cos - x2 * sin, x1 * sin + x2 * cos], -1).astype(x.dtype)

def mla_project(h, pos, w_in, g_q_lat, g_kv_lat, w_uq, g_qn_nope, g_qn_rope, g_kn_rope):
    b, t, _ = h.shape
    z = h @ w_in
    cq = rmsnorm(z[..., :Q_LORA_RANK], g_q_lat)
    lat = rmsnorm(z[..., Q_LORA_RANK:Q_LORA_RANK + KV_LORA_RANK], g_kv_lat)
    cos, sin = rope_tables(pos)
    kr = apply_rope(rmsnorm(z[..., Q_LORA_RANK + KV_LORA_RANK:], g_kn_rope), cos, sin)
    q = (cq @ w_uq).reshape(b, t, N_HEADS, QK_NOPE_DIM + QK_ROPE_DIM)
    qn = rmsnorm(q[..., :QK_NOPE_DIM], g_qn_nope)
    qr = apply_rope(rmsnorm(q[..., QK_NOPE_DIM:], g_qn_rope), cos[:, None], sin[:, None])
    return qn, qr, lat, kr

def key_nope(lat, w_uk, g_kn_nope):
    return rmsnorm(jnp.einsum('...c,chd->...hd', lat, w_uk), g_kn_nope)

def mla_attend(qn, qr, kn, kr, lat, q_pos, k_pos, w_uv):
    s = (jnp.einsum('bqhd,bkhd->bhqk', qn, kn, preferred_element_type=jnp.float32)
         + jnp.einsum('bqhr,bkr->bhqk', qr, kr, preferred_element_type=jnp.float32)) * ATTN_SCALE
    s = jnp.where(k_pos[None, None, None, :] <= q_pos[None, None, :, None], s, -jnp.inf)
    p = jax.nn.softmax(s, axis=-1).astype(lat.dtype)
    ctx = jnp.einsum('bhqk,bkc->bqhc', p, lat)
    return jnp.einsum('bqhc,chv->bqhv', ctx, w_uv)

def mla_prompt(h, pos, w_in, g_q_lat, g_kv_lat, w_uq, w_uk, w_uv,
               g_qn_nope, g_qn_rope, g_kn_nope, g_kn_rope, w_out):
    b, s, _ = h.shape
    qn, qr, lat, kr = mla_project(h, pos, w_in, g_q_lat, g_kv_lat, w_uq, g_qn_nope, g_qn_rope, g_kn_rope)
    kn = key_nope(lat, w_uk, g_kn_nope)
    nqb = s // Q_BLOCK
    qn_b = qn.reshape(b, nqb, Q_BLOCK, N_HEADS, QK_NOPE_DIM).transpose(1, 0, 2, 3, 4)
    qr_b = qr.reshape(b, nqb, Q_BLOCK, N_HEADS, QK_ROPE_DIM).transpose(1, 0, 2, 3, 4)
    qp_b = pos.reshape(nqb, Q_BLOCK)

    def block(args):
        qn_i, qr_i, qp_i = args
        return mla_attend(qn_i, qr_i, kn, kr, lat, qp_i, pos, w_uv)

    o = lax.map(block, (qn_b, qr_b, qp_b))
    o = o.transpose(1, 0, 2, 3, 4).reshape(b, s, N_HEADS * V_HEAD_DIM)
    return o @ w_out, jnp.concatenate([lat, kr], -1)

def mla_sample(h, pos, cache, page_table, w_in, g_q_lat, g_kv_lat, w_uq, w_uk, w_uv,
               g_qn_nope, g_qn_rope, g_kn_nope, g_kn_rope, w_out):
    b, t, _ = h.shape
    qn, qr, lat, kr = mla_project(h, pos, w_in, g_q_lat, g_kv_lat, w_uq, g_qn_nope, g_qn_rope, g_kn_rope)
    new_rows = jnp.concatenate([lat, kr], -1)

    def one_seq(args):
        qn_i, qr_i, pages, rows_i = args
        past = cache[pages].reshape(-1, CACHE_ROW)
        rows = jnp.concatenate([past, rows_i.astype(past.dtype)], 0)
        lat_i, kr_i = rows[:, :KV_LORA_RANK], rows[:, KV_LORA_RANK:]
        kn_i = key_nope(lat_i, w_uk, g_kn_nope)
        k_pos = jnp.arange(rows.shape[0])
        return mla_attend(qn_i[None], qr_i[None], kn_i[None], kr_i[None], lat_i[None],
                          pos, k_pos, w_uv)[0]

    o = lax.map(one_seq, (qn, qr, page_table, new_rows))
    return o.reshape(b, t, N_HEADS * V_HEAD_DIM) @ w_out, new_rows

def pool_mixer(h, prefix, pos, w_pool, scale):
    b, t, _ = h.shape
    p = prefix.shape[1]
    ext = jnp.concatenate([prefix.astype(h.dtype), h], 1)
    extf = ext.astype(jnp.float32)
    cs = jnp.concatenate([jnp.zeros((b, 1, D_MODEL), jnp.float32), jnp.cumsum(extf, axis=1)], 1)
    end = cs[:, p + 1:p + 1 + t]
    parts = []
    for gi, w in enumerate(POOL_WINDOWS):
        ch = slice(gi * POOL_GROUP_DIM, (gi + 1) * POOL_GROUP_DIM)
        start = cs[:, p + 1 - w:p + 1 - w + t, ch]
        cnt = jnp.minimum(pos + 1, w).astype(jnp.float32)[None, :, None]
        parts.append((end[..., ch] - start) / cnt)
    d = (jnp.concatenate(parts, -1) - extf[:, p:]).astype(h.dtype)
    d = d.reshape(b, t, POOL_GROUPS, POOL_GROUP_DIM)
    y = jnp.einsum('btgc,gce->btge', d, w_pool).reshape(b, t, D_MODEL) * scale
    return y, ext[:, -POOL_STATE_LEN:]

def peer(h, w_q, subkeys, u, v):
    shp = h.shape
    flat = h.reshape(-1, D_MODEL)
    n = flat.shape[0]
    pad = (-n) % PEER_BLOCK
    blocks = jnp.pad(flat, ((0, pad), (0, 0))).reshape(-1, PEER_BLOCK, D_MODEL)

    def block(xb):
        q = (xb @ w_q).reshape(PEER_BLOCK, PEER_HEADS, 2, PEER_HALF)
        s = jnp.einsum('thpc,hpnc->thpn', q, subkeys).astype(jnp.float32)
        vals, idx = lax.top_k(s, PEER_TOPK)
        cand = (vals[:, :, 0, :, None] + vals[:, :, 1, None, :]).reshape(
            PEER_BLOCK, PEER_HEADS, PEER_TOPK * PEER_TOPK)
        best, ci = lax.top_k(cand, PEER_TOPK)
        i1 = jnp.take_along_axis(idx[:, :, 0], ci // PEER_TOPK, axis=-1)
        i2 = jnp.take_along_axis(idx[:, :, 1], ci % PEER_TOPK, axis=-1)
        e = (i1 * PEER_N_KEYS + i2).reshape(PEER_BLOCK, PEER_HEADS * PEER_TOPK)
        g = jax.nn.softmax(best, axis=-1).reshape(PEER_BLOCK, PEER_HEADS * PEER_TOPK)
        a = jax.nn.gelu(jnp.einsum('td,tkd->tk', xb, u[e]), approximate=False)
        return jnp.einsum('tk,tkd->td', (g * a).astype(xb.dtype), v[e])

    y = lax.map(block, blocks).reshape(-1, D_MODEL)[:n]
    return y.reshape(shp)

def setup_inputs(seed: int = 0) -> dict:
    key = jax.random.key(seed)
    ks = jax.random.split(key, 28)
    f32 = jnp.float32

    def nrm(k, shape, s):
        return jax.random.normal(k, shape, f32) * s

    def gain(k, shape):
        return 1.0 + 0.05 * jax.random.normal(k, shape, f32)

    n_pages = PAST_LEN // PAGE_SIZE
    n_used = DEC_BATCH * n_pages
    n_phys = (n_used * PAGE_POOL_NUM + PAGE_POOL_DEN - 1) // PAGE_POOL_DEN
    page_table = jax.random.permutation(ks[6], n_phys)[:n_used].reshape(DEC_BATCH, n_pages).astype(jnp.int32)
    L, A, P = DEPTH, N_MLA_LAYERS, N_POOL_LAYERS
    qk = QK_NOPE_DIM + QK_ROPE_DIM
    return {
        'x_prompt': nrm(ks[0], (BATCH, SEQ, D_MODEL), 1.0),
        'x_sample': nrm(ks[1], (DEC_BATCH, DEC_SEQ, D_MODEL), 1.0),
        'c_prompt': nrm(ks[2], (BATCH, D_MODEL), 1.0),
        'c_sample': nrm(ks[3], (DEC_BATCH, D_MODEL), 1.0),
        'cache_mla': nrm(ks[4], (A, n_phys, PAGE_SIZE, CACHE_ROW), 1.0),
        'state_pool': nrm(ks[5], (P, DEC_BATCH, POOL_STATE_LEN, D_MODEL), 1.0),
        'page_table': page_table,
        'norm_mix': gain(ks[7], (L, D_MODEL)),
        'norm_ffn': gain(ks[8], (L, D_MODEL)),
        'w_ada': nrm(ks[9], (L, D_MODEL, 6 * D_MODEL), 0.5 * D_MODEL ** -0.5),
        'b_ada': nrm(ks[10], (L, 6 * D_MODEL), 0.02),
        'w_mla_in': nrm(ks[11], (A, D_MODEL, Q_LORA_RANK + KV_LORA_RANK + QK_ROPE_DIM), D_MODEL ** -0.5),
        'g_q_lat': gain(ks[12], (A, Q_LORA_RANK)),
        'g_kv_lat': gain(ks[13], (A, KV_LORA_RANK)),
        'w_uq': nrm(ks[14], (A, Q_LORA_RANK, N_HEADS * qk), Q_LORA_RANK ** -0.5),
        'w_uk': nrm(ks[15], (A, KV_LORA_RANK, N_HEADS, QK_NOPE_DIM), KV_LORA_RANK ** -0.5),
        'w_uv': nrm(ks[16], (A, KV_LORA_RANK, N_HEADS, V_HEAD_DIM), KV_LORA_RANK ** -0.5),
        'g_qn_nope': gain(ks[17], (A, QK_NOPE_DIM)),
        'g_qn_rope': gain(ks[18], (A, QK_ROPE_DIM)),
        'g_kn_nope': gain(ks[19], (A, QK_NOPE_DIM)),
        'g_kn_rope': gain(ks[20], (A, QK_ROPE_DIM)),
        'w_mla_out': nrm(ks[21], (A, N_HEADS * V_HEAD_DIM, D_MODEL), (N_HEADS * V_HEAD_DIM) ** -0.5),
        'w_pool': nrm(ks[22], (P, POOL_GROUPS, POOL_GROUP_DIM, POOL_GROUP_DIM), POOL_GROUP_DIM ** -0.5),
        'pool_scale': gain(ks[23], (P, D_MODEL)),
        'w_peer_q': nrm(ks[24], (L, D_MODEL, PEER_HEADS * PEER_QUERY_DIM), D_MODEL ** -0.5),
        'peer_subkeys': nrm(ks[25], (L, PEER_HEADS, 2, PEER_N_KEYS, PEER_HALF), PEER_HALF ** -0.5),
        'peer_u': nrm(ks[26], (L, PEER_N_EXPERTS, D_MODEL), D_MODEL ** -0.5),
        'peer_v': nrm(ks[27], (L, PEER_N_EXPERTS, D_MODEL), PEER_HEADS ** -0.5),
    }

def reference(x_prompt, x_sample, c_prompt, c_sample, cache_mla, state_pool, page_table,
              norm_mix, norm_ffn, w_ada, b_ada, w_mla_in, g_q_lat, g_kv_lat, w_uq, w_uk, w_uv,
              g_qn_nope, g_qn_rope, g_kn_nope, g_kn_rope, w_mla_out, w_pool, pool_scale,
              w_peer_q, peer_subkeys, peer_u, peer_v):
    pos_p = jnp.arange(x_prompt.shape[1])
    pos_s = PAST_LEN + jnp.arange(x_sample.shape[1])
    xp, xs = x_prompt, x_sample
    rows_p, rows_s, pst_p, pst_s = [], [], [], []
    for l in range(DEPTH):
        sp = adaln(c_prompt, w_ada[l], b_ada[l])
        ss = adaln(c_sample, w_ada[l], b_ada[l])
        hp = modulate(rmsnorm(xp, norm_mix[l]), sp[0], sp[1])
        hs = modulate(rmsnorm(xs, norm_mix[l]), ss[0], ss[1])
        i = l // N_MIXERS
        if l % N_MIXERS == 0:
            mw = (w_mla_in[i], g_q_lat[i], g_kv_lat[i], w_uq[i], w_uk[i], w_uv[i],
                  g_qn_nope[i], g_qn_rope[i], g_kn_nope[i], g_kn_rope[i], w_mla_out[i])
            mp, r_p = mla_prompt(hp, pos_p, *mw)
            ms, r_s = mla_sample(hs, pos_s, cache_mla[i], page_table, *mw)
            rows_p.append(r_p)
            rows_s.append(r_s)
        else:
            zero_prefix = jnp.zeros((hp.shape[0], POOL_STATE_LEN, D_MODEL), hp.dtype)
            mp, st_p = pool_mixer(hp, zero_prefix, pos_p, w_pool[i], pool_scale[i])
            ms, st_s = pool_mixer(hs, state_pool[i], pos_s, w_pool[i], pool_scale[i])
            pst_p.append(st_p)
            pst_s.append(st_s)
        xp = xp + sp[2][:, None, :] * mp
        xs = xs + ss[2][:, None, :] * ms
        hp = modulate(rmsnorm(xp, norm_ffn[l]), sp[3], sp[4])
        hs = modulate(rmsnorm(xs, norm_ffn[l]), ss[3], ss[4])
        xp = xp + sp[5][:, None, :] * peer(hp, w_peer_q[l], peer_subkeys[l], peer_u[l], peer_v[l])
        xs = xs + ss[5][:, None, :] * peer(hs, w_peer_q[l], peer_subkeys[l], peer_u[l], peer_v[l])
    return (xp, xs, jnp.stack(rows_p), jnp.stack(rows_s), jnp.stack(pst_p), jnp.stack(pst_s))


_drawn_inputs = setup_inputs


def setup_inputs(seed=0):
    import zlib

    import numpy as np

    out = dict(_drawn_inputs(seed))
    spreads = {}
    factors = {'cache_mla': 4.049,
     'norm_ffn': 2.857,
     'g_q_lat': 8.0,
     'g_qn_nope': 8.0,
     'g_qn_rope': 8.0,
     'g_kn_nope': 8.0,
     'pool_scale': 3.859}
    for name, (base, spread) in spreads.items():
        noise = np.random.default_rng([zlib.crc32(name.encode()), seed]).standard_normal(out[name].shape)
        drawn = base * np.exp(spread * noise) if base else spread * noise
        out[name] = __import__('jax').numpy.asarray(drawn.astype(out[name].dtype))
    for name, factor in factors.items():
        out[name] = (out[name] * factor).astype(out[name].dtype)
    return out
```

```python
from contextlib import ExitStack

import numpy as np

import concourse.bass as bass
from concourse import mybir

F32 = mybir.dt.float32
U32 = mybir.dt.uint32
I32 = mybir.dt.int32
ALU = mybir.AluOpType
ACT = mybir.ActivationFunctionType
AX_X = mybir.AxisListType.X

P = 128
D = 1024
DC = D // P
SEQ = 512
NT = SEQ // P
NS = 8
NC = NS + 1
PAST = 2048
PAGE = 128
NPG = PAST // PAGE
DEPTH = 2
EPS = 1e-6
NH = 8
NOPE, ROPE, VD = 128, 64, 128
QH = NOPE + ROPE
QL, KL = 384, 256
QLC, KLC = QL // P, KL // P
ROW = KL + ROPE
ZW = QL + KL + ROPE
SCALE = float(QH) ** -0.5
WINDOWS = (2, 4, 8, 16)
GD = D // 4
STATE = 15
PH = 8
NK = 128
TOPK = 16
PEER_HALF = 128
NQ = PH * 2
KK = PH * TOPK
NEG = -1.0e30
LOWEST = -3.0e38
GRP = 4
ADA = 6 * D


def shape_constants():
    inv = (10000.0 ** (-np.arange(0, ROPE, 2) / ROPE)).astype(np.float32)
    pos = np.concatenate([np.arange(SEQ), np.full(NS, PAST)]).astype(np.float32)
    ang = (pos[:, None] * inv[None, :]).astype(np.float32)
    cos, sin = np.cos(ang).astype(np.float32), np.sin(ang).astype(np.float32)
    rot = np.zeros((P, NT + 1, 2, ROPE), np.float32)
    for t in range(NT + 1):
        n = P if t < NT else NS
        rot[:n, t, 0] = np.tile(cos[t * P:t * P + n], 2)
        rot[:n, t, 1] = np.tile(sin[t * P:t * P + n], 2)
    i = np.arange(P)
    small = np.concatenate([
        np.eye(P), np.where(i[None, :] <= i[:, None], 0.0, NEG),
        (i[None, :] // TOPK == i[:, None]), (i[:, None] // TOPK == np.arange(NS)[None, :]),
        (i[:, None] % TOPK == np.arange(TOPK)[None, :]), np.tile(np.arange(TOPK), (P, 1)),
    ], axis=1).astype(np.float32)
    band = np.zeros((P, 4, 4, P), np.float32)
    for g, w in enumerate(WINDOWS):
        near = (i[:, None] <= i[None, :]) & (i[:, None] > i[None, :] - w)
        band[:, 0, g] = near / np.minimum(i + 1, w)[None, :] - np.eye(P)
        band[:, 1, g] = near / w - np.eye(P)
        band[:, 2, g] = (i[:, None] - P > i[None, :] - w) / w
        r = np.arange(NS * STATE)
        band[:NS * STATE, 3, g, :NS] = ((r[:, None] // STATE == np.arange(NS)) & (r[:, None] % STATE >= STATE - (w - 1))) / w
        band[:NS, 3, g, NS:2 * NS] = np.eye(NS) * (1.0 / w - 1.0)
    return {"rot": rot.reshape(P, -1), "small": small, "band": band.reshape(P, -1)}


def decoder_step(nc, T, O):
    ctx = ExitStack()
    with ctx:
        def sb(name, shape, dt=F32):
            return ctx.enter_context(nc.sbuf_tensor(name, shape, dt))

        sems = {}

        def sem(name):
            if name not in sems:
                sems[name] = ctx.enter_context(nc.semaphore(name))
            return sems[name]

        ada_rows = nc.dram_tensor("ada_rows", (DEPTH, NC, ADA), F32, kind="Internal").ap()

        W = 11904
        x_tok = sb("x_tok", [P, NT + 1, D])
        big = sb("big", [P, 16384])
        ring = sb("ring", [P, 8, D])
        mod_mix = sb("mod_mix", [P, 3, D])
        mod_smp = sb("mod_smp", [P, 3, D])
        hT = sb("hT", [P, DC * P])
        hbuf = sb("hbuf", [P, 3, D])
        work = sb("work", [P, W])
        small = sb("small", [P, 3 * P + NS + 2 * TOPK])
        tiny = sb("tiny", [P, 64])
        newton = sb("newton", [P, 48])
        ones = sb("ones", [P, P])
        ident = small[:, 0:P]
        causal = small[:, P:2 * P]
        sel = small[:, 2 * P:3 * P]
        selT = small[:, 3 * P:3 * P + NS]
        lane = small[:, 3 * P + NS:3 * P + NS + TOPK]
        iota = small[:, 3 * P + NS + TOPK:3 * P + NS + 2 * TOPK]

        pos = [0]

        def region(base, size, total):
            o = pos[0]
            pos[0] += size
            assert pos[0] <= total, (pos[0], total)
            return base[:, o:o + size]

        w_in = region(big, DC * ZW, 16384).rearrange("p (c n) -> p c n", c=DC)
        w_uq = region(big, QLC * NH * QH, 16384).rearrange("p (c n) -> p c n", c=QLC)
        w_uk = region(big, KLC * NH * NOPE, 16384).rearrange("p (c n) -> p c n", c=KLC)
        w_uv = region(big, KLC * NH * VD, 16384).rearrange("p (c n) -> p c n", c=KLC)
        w_ukT = region(big, NH * KL, 16384).rearrange("p (h n) -> p h n", h=NH)
        w_q = big[:, :].rearrange("p (c n) -> p c n", c=DC)
        w_ada = big[:, :].rearrange("p (s c n) -> p s c n", s=4, c=DC)
        w_out = ring[:, :, :]
        pos[0] = 0
        knT = region(work, NH * SEQ, W).rearrange("p (h n) -> p h n", h=NH)
        krT = region(work, SEQ, W)
        rows = region(work, (NT + 1) * ROW, W).rearrange("p (t n) -> p t n", t=NT + 1)
        latT = region(work, KLC * P, W).rearrange("p (c n) -> p c n", c=KLC)
        cqT = region(work, QLC * P, W).rearrange("p (c n) -> p c n", c=QLC)
        z = region(work, ZW, W)
        qs = region(work, NH * QH, W)
        qnT = region(work, NH * P, W)
        qrT = region(work, NH * P, W)
        pT = region(work, SEQ, W)
        ctxT = region(work, KLC * P, W)
        rot = sb("rot", [P, 2, ROPE])
        spare = mod_smp[:, :, :].rearrange("p m n -> p (m n)")
        gain_all = spare[:, 0:ZW + QH + NOPE]
        sq = spare[:, ZW + QH + NOPE:ZW + QH + NOPE + NH * QH]
        ks = hbuf[:, 1, :]
        oT = hbuf[:, 2, :]
        probs = hT[:, :].rearrange("p (b n) -> p b n", b=2)

        pos[0] = 0
        cached = region(work, (NPG + 1) * ROW, W).rearrange("p (g n) -> p g n", g=NPG + 1)
        cachedT = region(work, 2 * 3 * P, W).rearrange("p (b n) -> p b n", b=2)
        ksq = region(work, 2 * D, W).rearrange("p (b n) -> p b n", b=2)
        kss = region(work, NPG * NH, W)
        krn = region(work, NPG * NH, W)
        krt = region(work, NPG * NH, W)
        sc_s = region(work, (NPG + 1) * NH, W).rearrange("p (g h) -> p g h", g=NPG + 1)
        ps_s = region(work, (NPG + 1) * NH, W).rearrange("p (g h) -> p g h", g=NPG + 1)
        ctx_s = region(work, KLC * NH * NS, W).rearrange("p (c h s) -> p c h s", c=KLC, h=NH)
        oT_s = region(work, NH * NS, W)
        keep = sb("keep", [P, 256])
        own_dram = nc.dram_tensor("own_scores", (NS, NH), F32, kind="Internal").ap()
        zero = causal
        cact = hbuf[:, 2, 0:DC * NC].rearrange("p (c n) -> p c n", c=DC)

        def ada_bias(l):
            return work[0:NC, 0:ADA] if l == 0 else ring[0:NC, 0:6, :].rearrange("p a n -> p (a n)")
        q_abs = keep[:, 0:128].rearrange("p (c m) -> p c m", c=KLC)
        q_rot = keep[0:ROPE, 128:192]
        s_own = keep[0:1, 192:256]
        pages = sb("pages", [1, NS * NPG], mybir.dt.int32)

        pos[0] = 0
        mod_ffn = region(work, 3 * D, W).rearrange("p (m n) -> p m n", m=3)
        keysT = region(work, NQ * NK, W).rearrange("p (q n) -> p q n", q=NQ)
        qT = region(work, NQ * P, W)
        hits = qT
        sco = region(work, NQ * NK, W)
        cand = sco
        vals = region(work, NQ * TOPK, W)
        idx = region(work, NQ * TOPK, W).bitcast(U32)
        idxf = region(work, NQ * TOPK, W)
        best = region(work, KK, W)
        flat = region(work, KK, W).bitcast(U32)
        fhi = region(work, KK, W)
        flo = region(work, KK, W)
        e1 = region(work, KK, W)
        e2 = region(work, KK, W)
        expert = region(work, KK, W).bitcast(U32)
        gate = region(work, KK, W)
        turn = region(work, 2 * GRP, W).bitcast(U32).rearrange("p (b j) -> p b j", b=2)
        dots = region(work, GRP, W)
        acts = region(work, GRP, W)
        wts = region(work, GRP, W)
        diag = region(work, GRP * P, W).rearrange("p (j n) -> p j n", j=GRP)
        e_lane = region(work, PH, W).bitcast(U32)
        g_lane = region(work, PH, W)
        band = hits
        dT = sco
        state = mod_smp[:, 0, :]
        pool_gain = mod_smp[:, 1, :]
        w_pool = big[:, 0:DC * GD].rearrange("p (c n) -> p c n", c=DC)

        pb = [ctx.enter_context(nc.psum_tensor(f"bank{i}", [P, 512], F32)) for i in range(8)]

        units = [(l, t) for l in range(DEPTH) for t in range(NT + 1)]
        tokens = lambda t: P if t < NT else NS
        STEPS = KK // GRP
        SSTEPS = PH // GRP
        before = [0]
        for _, t in units:
            before.append(before[-1] + (STEPS if t < NT else SSTEPS))
        mla_order = [NT] + list(range(NT))

        class Turns:

            def __init__(self, eng, own):
                self.eng, self.own, self.n, self.given = eng, own, {}, {}

            def next(self, name, unit=1, times=1):
                self.n[name] = self.n.get(name, 0) + unit * times
                self.eng.wait_ge(sem(name), self.n[name])

            def done(self, ins, name=None):
                name = name or self.own
                self.given[name] = self.given.get(name, 0) + 1
                ins.then_inc(sem(name), 1)
                self.eng.wait_ge(sem(name), self.given[name])

        for name in ("x_in", "consts_in", "c_in", "b_in", "table_in", "mix_w_in", "out_w_in", "gains_in", "rot_in",
                     "mods_in", "keys_in", "query_w_in", "pool_in", "state_in", "rows_out", "own_out", "own_in",
                     "y_out", "state_out", "dve_step", "act_step", "idx_read", "slot_turn"):
            sem(name)
        block = ctx.enter_context(nc.Block())

        @block.sync
        def _(sp):
            w = Turns(sp, "sp")

            def ld(dst, src, name):
                sp.dma_start(dst, src).then_inc(sem(name), 16)

            ld(small[:, :], T["small"], "consts_in")
            ld(hbuf[:, 0, 0:DC * NC].rearrange("p (c n) -> p c n", c=DC), T["cT"].rearrange("(c p) n -> p c n", p=P), "c_in")
            ld(pages[:, :], T["page_table"].rearrange("(a s) g -> a (s g)", a=1), "table_in")
            for l in range(DEPTH):
                ld(ada_bias(l),
                   T["b_ada"][l].partition_broadcast(NC), "b_in")
            def store_ada(i):
                l, j = divmod(i, ADA // 512)
                ld(ada_rows[l, :, j * 512:(j + 1) * 512], mod_mix[0:NC, 0, i % 2 * 512:(i % 2 + 1) * 512], f"ada_out{i % 2}")

            for l in range(DEPTH):
                for j in range(ADA // 512):
                    i = l * (ADA // 512) + j
                    if i >= 4:
                        sp.wait_ge(sem("ada_ps"), i - 3)
                    ld(w_ada[:, i % 4], T["w_ada"][l].rearrange("(c p) n -> p c n", p=P)[:, :, j * 512:(j + 1) * 512],
                       f"ada_w_in{i % 4}")
                    if i == 3:
                        for t in range(NT):
                            ld(x_tok[:, t, :], T["x_prompt"][0, t * P:(t + 1) * P, :], "x_in")
                        ld(x_tok[0:NS, NT, :], T["x_sample"].rearrange("b s d -> (b s) d"), "x_in")
                    if i >= 2:
                        sp.wait_ge(sem("ada_row"), i - 1)
                        store_ada(i - 2)
            for i in (2 * ADA // 512 - 2, 2 * ADA // 512 - 1):
                sp.wait_ge(sem("ada_row"), i + 1)
                store_ada(i)
            for j in range(2):
                sp.wait_ge(sem(f"ada_out{j}"), 16 * (ADA // 512))

            def mods(dst, l, first, who, n, norm):
                for m, k in ((0, 1), (1, 0), (2, 2)):
                    cols = slice((first + k) * D, (first + k + 1) * D)
                    src = ada_rows[l, NC - 1, cols].partition_broadcast(n) if who == "prompt" else ada_rows[l, 0:NS, cols]
                    ld(dst[0:n, m, :], src, "mods_in")
                ld(hT[0:n, :], norm.partition_broadcast(n), "mods_in")

            sp.wait_ge(sem("ada_ps"), 2 * ADA // 512)
            for dst, src in ((w_in, T["w_mla_in"][0]), (w_uq, T["w_uq"][0]),
                             (w_uk, T["w_uk"][0].rearrange("c h d -> c (h d)")), (w_uv, T["w_uv"][0].rearrange("c h d -> c (h d)"))):
                ld(dst, src.rearrange("(c p) n -> p c n", p=P), "mix_w_in")
            ld(w_ukT, T["w_ukT"], "mix_w_in")
            mods(mod_smp, 0, 0, "sample", NS, T["norm_mix"][0])
            w.next("mods_set")
            mods(mod_mix, 0, 0, "prompt", P, T["norm_mix"][0])
            sp.wait_ge(sem("ada_row"), 2 * ADA // 512)
            ld(w_out, T["w_mla_out"][0].rearrange("(c p) n -> p c n", p=P), "out_w_in")
            w.next("h_ready")
            o = 0
            for a, size in (("g_q_lat", QL), ("g_kv_lat", KL), ("g_kn_rope", ROPE), ("g_qn_nope", NOPE), ("g_qn_rope", ROPE), ("g_kn_nope", NOPE)):
                ld(gain_all[:, o:o + size], T[a][0].partition_broadcast(P), "gains_in")
                o += size
            for n_, t in enumerate(mla_order):
                if n_:
                    w.next("qk_norm")
                ld(rot[:, :, :], T["rot"].rearrange("p (t a b) -> p t a b", t=NT + 1, a=2)[:, t], "rot_in")
                w.next("row_ready")
                n = tokens(t)
                if t < NT:
                    ld(O["rows_p"][0, 0, t * P:(t + 1) * P, :], rows[:, t, :], "rows_out")
                else:
                    ld(O["rows_s"].rearrange("l b s n -> (l b s) n"), rows[0:NS, NT, :], "rows_out")
                    w.next("own_ready")
                    ld(own_dram, tiny[0:NS, 40:48], "own_out")
            w.next("qk_norm")
            for t in range(NT):
                w.next("x_mixed")
            sp.wait_ge(sem("rows_out"), 16 * (NT + 1))
            sp.wait_ge(sem("own_out"), 16)
            ld(s_own, own_dram.rearrange("(a s) h -> a (s h)", a=1), "own_in")
            w.next("smp_clear")
            ld(mod_smp[0:NS, 2, :], ada_rows[0, 0:NS, 2 * D:3 * D], "mods_in")
            w.next("table_in", 16)
            with sp.Fori(0, NS) as r:
                sp.wait_ge(sem("ctx_ps"), r)
                for g in range(NPG):
                    page = sp.value_load(pages[0:1, bass.ds(r * NPG + g, 1)], min_val=0, max_val=T["cache_mla"].shape[1] - 1)
                    ld(cached[:, g, :], T["cache_mla"][0, bass.ds(page, 1)].rearrange("a p n -> (a p) n"), f"page_in{g}")
                ld(cached[0:1, NPG, 0:KL], O["rows_s"][0, bass.ds(r, 1), 0, 0:KL], f"page_in{NPG}")
            w.next("x_mixed")
            for l in range(DEPTH):
                if l:
                    w.next("x_routed")
                    ld(w_pool, T["w_pool"][0].rearrange("g (a p) n -> p (g a) n", p=P), "pool_in")
                    ld(band.rearrange("p (k n) -> p k n", k=16), T["band"].rearrange("p (k n) -> p k n", k=16), "pool_in")
                    mods(mod_mix, 1, 0, "prompt", P, T["norm_mix"][1])
                    ld(pool_gain, T["pool_scale"][0].partition_broadcast(P), "pool_in")
                    w.next("mods_set")
                    for t in range(NT):
                        w.next("x_mixed")
                    ld(O["pst_p"][0, 0], hbuf[P - STATE:P, (NT - 1) % 2, :], "state_out")
                    mods(mod_mix, 1, 0, "sample", NS, T["norm_mix"][1])
                    w.next("mods_set")
                    ld(state[0:NS * STATE], T["state_pool"].rearrange("l b r d -> (l b r) d"), "state_in")
                    ld(O["pst_s"][0, :, 0:STATE - 1, :], T["state_pool"][0, :, 1:STATE, :], "state_out")
                    w.next("x_mixed")
                    ld(O["pst_s"][0, :, STATE - 1, :], hbuf[0:NS, NT % 2, :], "state_out")
                ld(w_q, T["w_peer_q"][l].rearrange("(c p) n -> p c n", p=P), "query_w_in")
                ld(keysT, T["subkeysT"][l], "keys_in")
                mods(mod_ffn, l, 3, "prompt", P, T["norm_ffn"][l])
                w.next("mods_set")
                if l:
                    sp.wait_ge(sem("state_out"), 48)
                    sp.sem_inc(sem("hbuf_free"), 1)
                for t in range(1, NT + 1):
                    w.next("x_routed")
                    if t == NT:
                        mods(mod_smp, l, 3, "sample", NS, T["norm_ffn"][l])
                        w.next("mods_set")
                    if l:
                        ld(O["y_p"][0, (t - 1) * P:t * P, :], x_tok[:, t - 1, :], "y_out")
            w.next("x_routed")
            ld(O["y_s"].rearrange("b s d -> (b s) d"), x_tok[0:NS, NT, :], "y_out")
            sp.wait_ge(sem("y_out"), 16 * (NT + 1))

        @block.tensor
        def _(pe):
            w = Turns(pe, "pe")
            mm = pe.matmul

            w.next("consts_in", 16)
            w.next("c_act")
            for i in range(2 * ADA // 512):
                w.next(f"ada_w_in{i % 4}", 16)
                if i >= 2:
                    pe.wait_ge(sem("ada_row"), i - 1)
                for c in range(DC):
                    last = mm(pb[i % 2][0:NC, :], cact[:, c, :], w_ada[:, i % 4, c, :], start=(c == 0), stop=(c == DC - 1))
                last.then_inc(sem("ada_ps"), 1)

            def transpose_h(t, hb):
                n = tokens(t)
                w.next("h_ready")
                for c in range(DC):
                    k = c if n == NS else c % 4
                    last = pe.transpose(pb[4 + (c // 4 if n == P else 0)][:, k * n:k * n + n], hb[0:n, c * P:(c + 1) * P],
                                        ident[0:n, 0:n])
                last.then_inc(sem("hT_ps"), 1)

            for i, t in enumerate(mla_order):
                n = tokens(t)
                ht = lambda c: hT[:, c * n:(c + 1) * n]
                transpose_h(t, hbuf[:, 0, :])
                w.next("hT_ready")
                if i == 0:
                    w.next("mix_w_in", 16, 5)
                for half in range(2):
                    for c in range(DC):
                        last = mm(pb[half][0:n, 0:ZW // 2], ht(c), w_in[:, c, half * ZW // 2:(half + 1) * ZW // 2],
                                  start=(c == 0), stop=(c == DC - 1))
                last.then_inc(sem("z_ps"), 1)
                w.next("row_ready")
                for c in range(QLC):
                    pe.transpose(pb[6][:, c * n:(c + 1) * n], z[0:n, c * P:(c + 1) * P], ident[0:n, 0:n])
                for c in range(KLC):
                    pe.transpose(pb[7][:, c * n:(c + 1) * n], rows[0:n, t, c * P:(c + 1) * P], ident[0:n, 0:n])
                pe.transpose(pb[7][0:ROPE, KLC * n:KLC * n + n], rows[0:n, t, KL:ROW], ident[0:n, 0:n])\
                    .then_inc(sem("zT_ps"), 1)
                w.next("zT_ready")
                for b in range(3):
                    for c in range(QLC):
                        mm(pb[2 + b][0:n, :], cqT[:, c, 0:n], w_uq[:, c, b * 512:(b + 1) * 512], start=(c == 0), stop=(c == QLC - 1))
                for b in range(2):
                    for c in range(KLC):
                        last = mm(pb[b][0:n, :], latT[:, c, 0:n], w_uk[:, c, b * 512:(b + 1) * 512], start=(c == 0), stop=(c == KLC - 1))
                last.then_inc(sem("qk_ps"), 1)
                w.next("qk_norm")
                q3 = qs[0:n, :].rearrange("p (h d) -> p h d", h=NH)
                if t < NT:
                    for h in range(NH):
                        pe.transpose(pb[6 + h // 4][:, h % 4 * P:(h % 4 + 1) * P], q3[:, h, 0:NOPE], ident)
                        pe.transpose(pb[h // 4][0:ROPE, h % 4 * P:(h % 4 + 1) * P], q3[:, h, NOPE:QH], ident)
                        last = pe.transpose(pb[2 + h // 4][:, h % 4 * P:(h % 4 + 1) * P], ks[:, h * NOPE:(h + 1) * NOPE], ident)
                    last.then_inc(sem("qkT_ps"), 1)
                    w.next("qkT_ready")
                    keys = (t + 1) * P

                    def scores(h):
                        mm(pb[h % 2][:, 0:keys], qnT[:, h * P:(h + 1) * P], knT[:, h, 0:keys], start=True, stop=False)
                        mm(pb[h % 2][:, 0:keys], qrT[0:ROPE, h * P:(h + 1) * P], krT[0:ROPE, 0:keys], start=False, stop=True)\
                            .then_inc(sem("s_ps"), 1)

                    scores(0)
                    for h in range(NH):
                        if h + 1 < NH:
                            scores(h + 1)
                        w.next("p_norm")
                        for k in range(t + 1):
                            last = pe.transpose(pb[2][:, k * P:(k + 1) * P], probs[:, h % 2, k * P:(k + 1) * P], ident)
                        last.then_inc(sem("pT_ps"), 1)
                        w.next("pT_ready")
                        for c in range(KLC):
                            for k in range(t + 1):
                                last = mm(pb[3][:, c * P:(c + 1) * P], rows[:, k, c * P:(c + 1) * P], pT[:, k * P:(k + 1) * P],
                                          start=(k == 0), stop=(k == t))
                        last.then_inc(sem("cT_ps"), 1)
                        w.next("cT_ready")
                        for c in range(KLC):
                            last = mm(pb[4 + h // 4][:, h % 4 * P:(h % 4 + 1) * P], w_uv[:, c, h * VD:(h + 1) * VD],
                                      ctxT[:, c * P:(c + 1) * P], start=(c == 0), stop=(c == KLC - 1))
                    last.then_inc(sem("o_ps"), 1)
                    w.next("o_ready")
                    if t == 0:
                        w.next("out_w_in", 16)
                    for b in range(2):
                        for h in range(NH):
                            last = mm(pb[6 + b][:, :], oT[:, h * P:(h + 1) * P], w_out[:, h, b * 512:(b + 1) * 512],
                                      start=(h == 0), stop=(h == NH - 1))
                    last.then_inc(sem("mix_ps"), 1)
                else:
                    for h in range(NH):
                        pe.transpose(pb[6][:, h * NS:(h + 1) * NS], q3[:, h, 0:NOPE], ident[0:n, 0:n])
                        last = pe.transpose(pb[7][0:ROPE, h * NS:(h + 1) * NS], q3[:, h, NOPE:QH], ident[0:n, 0:n])
                    last.then_inc(sem("qkT_ps"), 1)
                    w.next("qkT_ready")
                    for c in range(KLC):
                        for h in range(NH):
                            last = mm(pb[2][:, (c * NH + h) * NS:(c * NH + h + 1) * NS], w_ukT[:, h, c * P:(c + 1) * P],
                                      qnT[:, h * NS:(h + 1) * NS], start=True, stop=True)
                    last.then_inc(sem("qa_ps"), 1)

            w.next("smp_clear")
            w.next("ones_set")
            with pe.Fori(0, NS) as r:
                def turn_page(g):
                    pe.wait_ge(sem(f"page_in{g}"), r * 16 + 16)
                    for c in range(KLC):
                        pe.transpose(pb[6 + g % 2][:, c * P:(c + 1) * P], cached[:, g, c * P:(c + 1) * P], ident)
                    pe.transpose(pb[6 + g % 2][0:ROPE, 2 * P:3 * P], cached[:, g, KL:ROW], ident).then_inc(sem("page_ps"), 1)

                turn_page(0)
                for g in range(NPG):
                    if g + 1 < NPG:
                        turn_page(g + 1)
                    pe.wait_ge(sem("pageT"), r * NPG + g + 1)
                    b = g % 2
                    for c in range(KLC):
                        mm(pb[4][:, g * 16:g * 16 + 8], cachedT[:, b, c * P:(c + 1) * P], q_abs[:, c, bass.ds(r * NH, NH)],
                           start=(c == 0), stop=(c == KLC - 1), skip_group_check=True)
                    mm(pb[4][:, g * 16 + 8:g * 16 + 16], cachedT[0:ROPE, b, 2 * P:3 * P], q_rot[:, bass.ds(r * NH, NH)],
                       start=True, stop=True, skip_group_check=True)
                    if g >= 2:
                        pe.wait_ge(sem("k_squares"), r * NPG + g - 1)
                    for half in range(2):
                        for c in range(KLC):
                            last = mm(pb[2 * b + half][:, :], cachedT[:, b, c * P:(c + 1) * P], w_uk[:, c, half * 512:(half + 1) * 512],
                                      start=(c == 0), stop=(c == KLC - 1))
                    last.then_inc(sem("kk_ps"), 1)
                pe.wait_ge(sem("s_max"), r + 1)
                pe.transpose(pb[5][0:NH, 0:P], tiny[:, 0:NH], ident).then_inc(sem("max_ps"), 1)
                pe.wait_ge(sem("max_diag"), r + 1)
                mm(pb[5][:, P:P + NH], ones[0:NH, :], tiny[0:NH, 16:16 + NH], start=True, stop=True).then_inc(sem("maxb_ps"), 1)
                pe.wait_ge(sem("p_sum"), r + 1)
                mm(pb[5][:, 144:144 + NH], ones[:, :], tiny[:, 24:24 + NH], start=True, stop=True)
                pe.wait_ge(sem(f"page_in{NPG}"), r * 16 + 16)
                for c in range(KLC):
                    for g in range(NPG + 1):
                        last = mm(pb[5][:, 160 + c * NH:160 + (c + 1) * NH], cached[:, g, c * P:(c + 1) * P], ps_s[:, g, :],
                                  start=(g == 0), stop=(g == NPG))
                last.then_inc(sem("ctx_ps"), 1)
            pe.wait_ge(sem("ctx_ready"), NS)
            for h in range(NH):
                for c in range(KLC):
                    last = mm(pb[0][:, h * NS:(h + 1) * NS], w_uv[:, c, h * VD:(h + 1) * VD], ctx_s[:, c, h, :],
                              start=(c == 0), stop=(c == KLC - 1))
            last.then_inc(sem("o_ps"), 1)
            w.next("o_ready")
            for b in range(2):
                for h in range(NH):
                    last = mm(pb[6 + b][0:NS, :], oT_s[:, h * NS:(h + 1) * NS], w_out[:, h, b * 512:(b + 1) * 512],
                              start=(h == 0), stop=(h == NH - 1))
            last.then_inc(sem("mix_ps"), 1)

            def pool(t):
                n = tokens(t)
                w.next("h_ready")
                if t == 0:
                    w.next("pool_in", 16, 3)
                if t == NT:
                    w.next("state_in", 16)
                hb = hbuf[:, t % 2, :]
                bd = band.rearrange("p (k g n) -> p k g n", k=4, g=4)
                for c in range(DC):
                    out = pb[c // 4 if n == P else 0][:, (c % 4 if n == P else c) * n:(c % 4 if n == P else c) * n + n]
                    ch = slice(c * P, (c + 1) * P)
                    if t == NT:
                        mm(out, state[0:NS * STATE, ch], bd[0:NS * STATE, 3, c // 2, 0:NS], start=True, stop=False)
                        last = mm(out, hb[0:NS, ch], bd[0:NS, 3, c // 2, NS:2 * NS], start=False, stop=True)
                    else:
                        if t:
                            mm(out, hbuf[:, (t - 1) % 2, ch], bd[:, 2, c // 2, :], start=True, stop=False)
                        last = mm(out, hb[:, ch], bd[:, min(t, 1), c // 2, :], start=(t == 0), stop=True)
                last.then_inc(sem("dT_ps"), 1)
                w.next("dT_ready")
                for g in range(4):
                    for a in range(2):
                        c = 2 * g + a
                        last = mm(pb[6 + g // 2][0:n, g % 2 * GD:(g % 2 + 1) * GD], dT[:, c * n:(c + 1) * n], w_pool[:, c, :],
                                  start=(a == 0), stop=(a == 1))
                last.then_inc(sem("mix_ps"), 1)

            def route(u):
                l, t = units[u]
                n = tokens(t)
                transpose_h(t, hbuf[:, u % 2, :])
                w.next("hT_ready")
                if t == 0:
                    w.next("query_w_in", 16)
                for q in range(NQ):
                    b, k = (q // 4, q % 4) if n == P else (0, q)
                    for c in range(DC):
                        last = mm(pb[b][:, k * n:(k + 1) * n], w_q[:, c, q * P:(q + 1) * P], hT[:, c * n:(c + 1) * n],
                                  start=(c == 0), stop=(c == DC - 1))
                    if q % 4 == 3:
                        last.then_inc(sem("qT_ps"), 1)
                w.next("qT_ready")
                if t == 0:
                    w.next("keys_in", 16)
                for q in range(NQ):
                    last = mm(pb[q // 4][0:n, q % 4 * NK:(q % 4 + 1) * NK], qT[:, q * n:(q + 1) * n], keysT[:, q, :],
                              start=True, stop=True)
                last.then_inc(sem("sco_ps"), 1)

            def experts(u, a, b):
                n = tokens(units[u][1])
                with pe.Fori(a, b) as r:
                    for j in range(GRP):
                        pe.wait_ge(sem("diag_set"), r * GRP + (before[u] * GRP + j + 1))
                        pe.wait_ge(sem(f"v_in{j}"), r * 16 + (before[u] + 1) * 16)
                        for half in range(2):
                            last = mm(pb[6 + half][0:n, :], diag[:, j, 0:n], ring[:, GRP + j, half * 512:(half + 1) * 512],
                                      start=False, stop=False, skip_group_check=True)
                        last.then_inc(sem("v_used"), 1)

            pe.sem_inc(sem("v_used"), GRP)
            for u, (l, t) in enumerate(units):
                n = tokens(t)
                if l and t == 0:
                    for k in range(NT + 1):
                        pool(k)
                route(u)
                if t == NT:
                    w.next("route_done")
                    for half in range(2):
                        mm(pb[half][:, :], sel[0:NS, :], hbuf[0:NS, u % 2, half * 512:(half + 1) * 512], start=True, stop=True)
                    mm(pb[2][:, 0:KK], sel[0:NS, :], e1[0:NS, :], start=True, stop=True)
                    mm(pb[2][:, KK:2 * KK], sel[0:NS, :], gate[0:NS, :], start=True, stop=True, skip_group_check=True)\
                        .then_inc(sem("lane_ps"), 1)
                w.next("y_free")
                for half in range(2):
                    mm(pb[6 + half][0:n, :], zero[:, 0:n], w_q[:, 0, half * 512:(half + 1) * 512],
                       start=True, stop=False, skip_group_check=True)
                experts(u, 0, before[u + 1] - before[u])
                mm(pb[7][0:n, 0:64], zero[:, 0:n], w_q[:, 0, 0:64], start=False, stop=True, skip_group_check=True)\
                    .then_inc(sem("y_ps"), 1)

        @block.scalar
        def _(act):
            w = Turns(act, "act_step")

            def copy(out, in_, name=None):
                w.done(act.activation(out, in_, ACT.Copy), name)

            w.next("c_in", 16)
            w.done(act.activation(hbuf[:, 1, 0:DC * NC], hbuf[:, 0, 0:DC * NC], ACT.Exp, scale=-1.0), "c_exp")

            def copy_hT(t):
                w.next("hT_ps")
                if tokens(t) == P:
                    copy(hT[:, 0:512], pb[4][:, :])
                    copy(hT[:, 512:1024], pb[5][:, :], "hT_ready")
                else:
                    copy(hT[:, 0:DC * NS], pb[4][:, 0:DC * NS], "hT_ready")

            for t in mla_order:
                n = tokens(t)
                copy_hT(t)
                w.next("z_ps")
                copy(z[0:n, 0:ZW // 2], pb[0][0:n, 0:ZW // 2])
                copy(z[0:n, ZW // 2:ZW], pb[1][0:n, 0:ZW // 2], "z_ready")
                w.next("zT_ps")
                copy(cqT[:, :, 0:n], pb[6][:, 0:QLC * n].rearrange("p (c n) -> p c n", c=QLC))
                if t < NT:
                    copy(krT[0:ROPE, t * P:(t + 1) * P], pb[7][0:ROPE, KLC * n:KLC * n + n])
                copy(latT[:, :, 0:n], pb[7][:, 0:KLC * n].rearrange("p (c n) -> p c n", c=KLC), "zT_ready")
                w.next("qk_ps")
                for b in range(3):
                    copy(qs[0:n, b * 512:(b + 1) * 512], pb[2 + b][0:n, :])
                copy(ks[0:n, 0:512], pb[0][0:n, :])
                copy(ks[0:n, 512:1024], pb[1][0:n, :], "qk_ready")
                w.next("qkT_ps")
                if t == NT:
                    copy(q_rot.rearrange("p (s h) -> p s h", s=NS), pb[7][0:ROPE, 0:64].rearrange("p (h s) -> p s h", h=NH))
                    copy(qnT[:, 0:64], pb[6][:, 0:64], "qkT_ready")
                    w.next("qa_ps")
                    for c in range(KLC):
                        copy(q_abs[:, c, :].rearrange("p (s h) -> p s h", s=NS),
                             pb[2][:, c * 64:(c + 1) * 64].rearrange("p (h s) -> p s h", h=NH), "qa_ready" if c else None)
                    continue
                for b in range(2):
                    copy(qnT[:, b * 512:(b + 1) * 512], pb[6 + b][:, :])
                    copy(qrT[0:ROPE, b * 512:(b + 1) * 512], pb[b][0:ROPE, :])
                    copy(knT[:, 4 * b:4 * b + 4, t * P:(t + 1) * P], pb[2 + b][:, :].rearrange("p (h n) -> p h n", h=4),
                         "qkT_ready" if b else None)
                keys = (t + 1) * P
                def soften(h):
                    w.next("s_neg")
                    w.done(act.activation(probs[:, h % 2, 0:keys], pb[h % 2][:, 0:keys], ACT.Exp, bias=tiny[:, 56 + h % 2:57 + h % 2],
                                          accum_out=tiny[:, 58 + h % 2:59 + h % 2]), "p_ready")
                soften(0)
                for h in range(NH):
                    if h + 1 < NH:
                        soften(h + 1)
                    w.next("pT_ps")
                    copy(pT[:, 0:keys], pb[2][:, 0:keys], "pT_ready")
                    w.next("cT_ps")
                    copy(ctxT[:, :], pb[3][:, 0:256], "cT_ready")
                w.next("o_ps")
                copy(oT[:, 0:512], pb[4][:, :])
                copy(oT[:, 512:1024], pb[5][:, :], "o_ready")

            w.next("smp_clear")
            with act.Fori(0, NS) as r:
                for g in range(NPG):
                    def square(k):
                        act.wait_ge(sem("kk_ps"), r * NPG + k + 1)
                        if k >= 2:
                            act.wait_ge(sem("k_sums"), r * NPG + k - 1)
                        for half in range(2):
                            last = act.activation(ksq[:, k % 2, half * 512:(half + 1) * 512], pb[2 * (k % 2) + half][:, :], ACT.Square)
                        last.then_inc(sem("k_squares"), 1)
                    act.wait_ge(sem("page_ps"), r * NPG + g + 1)
                    act.activation(cachedT[:, g % 2, 0:256], pb[6 + g % 2][:, 0:256], ACT.Copy)
                    act.activation(cachedT[0:ROPE, g % 2, 256:384], pb[6 + g % 2][0:ROPE, 256:384], ACT.Copy).then_inc(sem("pageT"), 1)
                    if g:
                        square(g - 1)
                square(NPG - 1)
                act.wait_ge(sem("s_shift"), r + 1)
                act.activation(ps_s[:, :, :], sc_s[:, :, :], ACT.Exp).then_inc(sem("ps_ready"), 1)
            w.next("o_ps")
            copy(oT_s[:, :], pb[0][:, 0:64], "o_ready")

            def route(u):
                l, t = units[u]
                n = tokens(t)
                copy_hT(t)
                for b in range(4):
                    w.next("qT_ps")
                    if n == P:
                        copy(qT[:, b * 512:(b + 1) * 512], pb[b][:, :], "qT_ready" if b == 3 else None)
                if n == NS:
                    copy(qT[:, 0:NQ * NS], pb[0][:, 0:NQ * NS], "qT_ready")
                w.next("sco_ps")
                for b in range(4):
                    copy(sco[0:n, b * 512:(b + 1) * 512], pb[b][0:n, :], "sco_ready" if b == 3 else None)
                w.next("best_neg")
                w.done(act.activation(gate[0:n, :], e2[0:n, :], ACT.Exp), "gate_exp")

            def experts(u, a, b):
                n = tokens(units[u][1])
                scale_rows = ident if n == P else selT
                with act.Fori(a, b) as r:
                    act.wait_ge(sem("dots_set"), r + (before[u] + 1))
                    act.activation(acts[:, :], dots[:, :], ACT.Gelu).then_inc(sem("acts_set"), 1)
                    act.wait_ge(sem("wts_set"), r + (before[u] + 1))
                    for j in range(GRP):
                        act.wait_ge(sem("v_used"), r * GRP + (before[u] * GRP + j + 1))
                        act.activation(diag[:, j, 0:n], scale_rows, ACT.Copy, scale=wts[:, j:j + 1]).then_inc(sem("diag_set"), 1)

            for u, (l, t) in enumerate(units):
                if l and t == 0:
                    for k in range(NT + 1):
                        w.next("dT_ps")
                        if k < NT:
                            copy(dT[:, 0:512], pb[0][:, :])
                            copy(dT[:, 512:1024], pb[1][:, :], "dT_ready")
                        else:
                            copy(dT[:, 0:DC * NS], pb[0][:, 0:DC * NS], "dT_ready")
                route(u)
                if t == NT:
                    w.next("lane_ps")
                    for half in range(2):
                        copy(hbuf[:, 2, half * 512:(half + 1) * 512], pb[half][:, :], "lane_hidden" if half else None)
                experts(u, 0, before[u + 1] - before[u])

        @block.gpsimd
        def _(pool):
            nc.gpsimd.memset(ones[:, :], 1.0).then_inc(sem("ones_set"), 1)
            for u, (l, t) in enumerate(units):
                pool.wait_ge(sem("expert_set"), u + 1)
                if u == 0:
                    pool.wait_ge(sem("mix_ps"), NT + 1)
                with pool.Fori(0, (before[u + 1] - before[u]) // 2) as r:
                    for half in range(2):
                        base = before[u] + half
                        pool.wait_ge(sem("u_used"), r * 2 * GRP + base * GRP)
                        pool.sem_inc(sem("slot_turn"), 1)
                        pool.wait_ge(sem("v_used"), r * 2 * GRP + base * GRP)
                        pool.sem_inc(sem("slot_turn"), 1)
                        src = expert if t < NT else e_lane
                        pool.tensor_copy(turn[:, half, :], src[:, bass.ds(r * 2 * GRP + half * GRP, GRP)]).then_inc(sem("turn_set"), 1)
                        pool.wait_ge(sem("turn_set"), r * 2 + (base + 1))
                        pool.sem_inc(sem("slot_turn"), 1)
                        for kind, table, used in (("u", T["peer_u"].rearrange("l e d -> (l e) d"), "u_used"),
                                                  ("v", T["peer_v"].rearrange("l e d -> (l e) d"), "v_used")):
                            for j in range(GRP):
                                pool.wait_ge(sem(used), r * 2 * GRP + (base * GRP + j + 1))
                                pool.sem_inc(sem("slot_turn"), 1)
                                pool.indirect_dma_start(ring[:, (GRP if kind == "v" else 0) + j, :], None, table,
                                                        bass.IndirectOffsetOnAxis(turn[:, half, j:j + 1], 0))\
                                    .then_inc(sem(f"{kind}_in{j}"), 16)

        @block.vector
        def _(dve):
            w = Turns(dve, "dve_step")
            d = w.done
            tt, ts, stt = dve.tensor_tensor, dve.tensor_scalar, dve.scalar_tensor_tensor

            w.next("c_exp")
            d(ts(hbuf[:, 1, 0:DC * NC], hbuf[:, 1, 0:DC * NC], 1.0, None, ALU.add))
            d(dve.reciprocal(hbuf[:, 1, 0:DC * NC], hbuf[:, 1, 0:DC * NC]))
            d(tt(cact.rearrange("p c n -> p (c n)"), hbuf[:, 0, 0:DC * NC], hbuf[:, 1, 0:DC * NC], ALU.mult), "c_act")
            w.next("b_in", 16, 2)
            for i in range(2 * ADA // 512):
                l, j = divmod(i, ADA // 512)
                w.next("ada_ps")
                if i >= 2:
                    dve.wait_ge(sem(f"ada_out{i % 2}"), 16 * (i // 2))
                bias = ada_bias(l)
                d(tt(mod_mix[0:NC, 0, i % 2 * 512:(i % 2 + 1) * 512], pb[i % 2][0:NC, :], bias[:, j * 512:(j + 1) * 512], ALU.add), "ada_row")

            def inverse_root(y, v, t, link):
                link(ts(y.bitcast(I32), v.bitcast(I32), -0.5, float(0x5F3759DF), ALU.mult, ALU.add))
                for _ in range(3):
                    link(tt(t, y, y, ALU.mult))
                    link(stt(t, t, -0.5, v, ALU.mult, ALU.mult))
                    link(stt(y, t, 1.5, y, ALU.add, ALU.mult))

            def set_mods(m, n):
                w.next("mods_in", 16, 4)
                d(stt(m[0:n, 0, :], m[0:n, 0, :], 1.0, hT[0:n, :], ALU.add, ALU.mult), "mods_set")

            def norm(xt, hb, m, n):
                d(stt(hb[0:n, :], xt[0:n, :], 1.0, xt[0:n, :], ALU.mult, ALU.mult, accum_out=tiny[0:n, 0:1]))
                d(ts(tiny[0:n, 1:2], tiny[0:n, 0:1], 1.0 / D, EPS, ALU.mult, ALU.add))
                inverse_root(tiny[0:n, 2:3], tiny[0:n, 1:2], newton[0:n, 0:1], d)
                d(stt(hb[0:n, :], xt[0:n, :], tiny[0:n, 2:3], m[0:n, 0, :], ALU.mult, ALU.mult))
                d(tt(hb[0:n, :], hb[0:n, :], m[0:n, 1, :], ALU.add), "h_ready")

            def add_mixed(t, gate_, name="x_mixed"):
                n = tokens(t)
                for b in range(2):
                    part = slice(b * 512, (b + 1) * 512)
                    d(tt(hT[0:n, part], pb[6 + b][0:n, :], gate_[0:n, part], ALU.mult))
                    d(tt(x_tok[0:n, t, part], x_tok[0:n, t, part], hT[0:n, part], ALU.add), name if b else None)

            w.next("x_in", 16, NT + 1)
            w.next("consts_in", 16)
            set_mods(mod_smp, NS)
            set_mods(mod_mix, P)
            gq, gkv, gkr = gain_all[:, 0:QL], gain_all[:, QL:QL + KL], gain_all[:, QL + KL:ZW]
            gqn, gqr, gkn = (gain_all[:, ZW:ZW + NOPE], gain_all[:, ZW + NOPE:ZW + QH], gain_all[:, ZW + QH:ZW + QH + NOPE])

            def rotate(out1, out2, m1, m2):
                half = ROPE // 2
                d(tt(out1, m1[..., 0:half], m2[..., half:ROPE], ALU.subtract))
                return tt(out2, m2[..., 0:half], m1[..., half:ROPE], ALU.add)

            for i, t in enumerate(mla_order):
                n = tokens(t)
                norm(x_tok[:, t, :], hbuf[:, 0, :], mod_smp if t == NT else mod_mix, n)
                if i == 0:
                    w.next("gains_in", 16, 6)
                    d(stt(gqn, gqn, SCALE, gkn, ALU.mult, ALU.mult))
                    d(ts(gqr, gqr, SCALE, None, ALU.mult))
                w.next("z_ready")
                for k, (a, b) in enumerate(((0, QL), (QL, QL + KL), (QL + KL, ZW))):
                    d(stt(sq[0:n, a:b], z[0:n, a:b], 1.0, z[0:n, a:b], ALU.mult, ALU.mult, accum_out=tiny[0:n, 4 + k:5 + k]))
                    d(ts(newton[0:n, 24 + k:25 + k], tiny[0:n, 4 + k:5 + k], 1.0 / (b - a), EPS, ALU.mult, ALU.add))
                inverse_root(tiny[0:n, 4:7], newton[0:n, 24:27], newton[0:n, 0:3], d)
                d(stt(z[0:n, 0:QL], z[0:n, 0:QL], tiny[0:n, 4:5], gq[0:n], ALU.mult, ALU.mult))
                d(stt(rows[0:n, t, 0:KL], z[0:n, QL:QL + KL], tiny[0:n, 5:6], gkv[0:n], ALU.mult, ALU.mult))
                d(stt(z[0:n, QL + KL:ZW], z[0:n, QL + KL:ZW], tiny[0:n, 6:7], gkr[0:n], ALU.mult, ALU.mult))
                w.next("rot_in", 16)
                for k in range(2):
                    d(tt(sq[0:n, k * ROPE:(k + 1) * ROPE], z[0:n, QL + KL:ZW], rot[0:n, k, :], ALU.mult))
                d(rotate(rows[0:n, t, KL:KL + ROPE // 2], rows[0:n, t, KL + ROPE // 2:ROW], sq[0:n, 0:ROPE], sq[0:n, ROPE:2 * ROPE]), "row_ready")
                w.next("qk_ready")
                q3 = qs[0:n, :].rearrange("p (h d) -> p h d", h=NH)
                s3 = sq[0:n, :].rearrange("p (h d) -> p h d", h=NH)
                k3 = ks[0:n, :].rearrange("p (h d) -> p h d", h=NH)
                d(tt(sq[0:n, :], qs[0:n, :], qs[0:n, :], ALU.mult))
                d(dve.tensor_reduce(tiny[0:n, 8:16], s3[:, :, 0:NOPE], AX_X, ALU.add))
                d(dve.tensor_reduce(tiny[0:n, 16:24], s3[:, :, NOPE:QH], AX_X, ALU.add))
                d(tt(sq[0:n, 0:D], ks[0:n, :], ks[0:n, :], ALU.mult))
                d(dve.tensor_reduce(tiny[0:n, 24:32], sq[0:n, 0:D].rearrange("p (h d) -> p h d", h=NH), AX_X, ALU.add))
                for a, width in ((8, NOPE), (16, ROPE), (24, NOPE)):
                    d(ts(newton[0:n, a + 16:a + 24], tiny[0:n, a:a + 8], 1.0 / width, EPS, ALU.mult, ALU.add))
                inverse_root(tiny[0:n, 8:32], newton[0:n, 24:48], newton[0:n, 0:24], d)

                def heads(a, width):
                    return tiny[0:n, a:a + 8].unsqueeze(2).to_broadcast([n, NH, width])

                def over_heads(g, width):
                    return g[0:n, :].unsqueeze(1).to_broadcast([n, NH, width])

                d(tt(q3[:, :, 0:NOPE], q3[:, :, 0:NOPE], heads(8, NOPE), ALU.mult))
                d(tt(q3[:, :, 0:NOPE], q3[:, :, 0:NOPE], over_heads(gqn, NOPE), ALU.mult))
                d(tt(q3[:, :, NOPE:QH], q3[:, :, NOPE:QH], heads(16, ROPE), ALU.mult))
                d(tt(q3[:, :, NOPE:QH], q3[:, :, NOPE:QH], over_heads(gqr, ROPE), ALU.mult))
                m = [sq[0:n, k * 512:(k + 1) * 512].rearrange("p (h d) -> p h d", h=NH) for k in range(2)]
                for k in range(2):
                    d(tt(m[k], q3[:, :, NOPE:QH], rot[0:n, k, :].unsqueeze(1).to_broadcast([n, NH, ROPE]), ALU.mult))
                d(rotate(q3[:, :, NOPE:NOPE + 32], q3[:, :, NOPE + 32:QH], m[0], m[1]))
                d(tt(k3, k3, heads(24, NOPE), ALU.mult), "qk_norm")
                if t == NT:
                    d(tt(sq[0:n, 0:D].rearrange("p (h d) -> p h d", h=NH), q3[:, :, 0:NOPE], k3, ALU.mult))
                    d(dve.tensor_reduce(tiny[0:n, 32:40], sq[0:n, 0:D].rearrange("p (h d) -> p h d", h=NH), AX_X, ALU.add))
                    d(tt(sq[0:n, 0:512].rearrange("p (h d) -> p h d", h=NH), q3[:, :, NOPE:QH],
                         rows[0:n, NT, KL:ROW].unsqueeze(1).to_broadcast([n, NH, ROPE]), ALU.mult))
                    d(dve.tensor_reduce(tiny[0:n, 40:48], sq[0:n, 0:512].rearrange("p (h d) -> p h d", h=NH), AX_X, ALU.add))
                    d(tt(tiny[0:n, 40:48], tiny[0:n, 40:48], tiny[0:n, 32:40], ALU.add), "own_ready")
                    continue
                keys = (t + 1) * P
                def row_max(h):
                    w.next("s_ps")
                    b = pb[h % 2]
                    d(tt(b[:, t * P:keys], b[:, t * P:keys], causal, ALU.add))
                    d(dve.tensor_reduce(tiny[:, 60:61], b[:, 0:keys], AX_X, ALU.max))
                    d(ts(tiny[:, 56 + h % 2:57 + h % 2], tiny[:, 60:61], -1.0, None, ALU.mult), "s_neg")
                row_max(0)
                for h in range(NH):
                    if h + 1 < NH:
                        row_max(h + 1)
                    w.next("p_ready")
                    d(dve.reciprocal(tiny[:, 61:62], tiny[:, 58 + h % 2:59 + h % 2]))
                    d(ts(probs[:, h % 2, 0:keys], probs[:, h % 2, 0:keys], tiny[:, 61:62], None, ALU.mult), "p_norm")
                w.next("mix_ps")
                add_mixed(t, mod_mix[:, 2, :])

            d(dve.memset(sc_s[:, :, :], LOWEST))
            d(dve.memset(cached[:, NPG, :], 0.0), "smp_clear")
            w.next("own_in", 16)
            d(dve.memset(zero, 0.0), "zero_set")
            LINKS = 16
            with dve.Fori(0, NS) as r:
                at = [0]

                def e(ins, name=None):
                    if name is None:
                        at[0] += 1
                        ins.then_inc(sem("smp_step"), 1)
                        dve.wait_ge(sem("smp_step"), r * LINKS + at[0])
                    else:
                        ins.then_inc(sem(name), 1)
                        dve.wait_ge(sem(name), r + 1)

                for g in range(NPG):
                    dve.wait_ge(sem("k_squares"), r * NPG + g + 1)
                    dve.tensor_reduce(kss[:, g * NH:(g + 1) * NH], ksq[:, g % 2, :].rearrange("p (h d) -> p h d", h=NH), AX_X, ALU.add)\
                        .then_inc(sem("k_sums"), 1)
                dve.wait_ge(sem("k_sums"), r * NPG + NPG)
                e(ts(kss[:, :], kss[:, :], 1.0 / NOPE, EPS, ALU.mult, ALU.add))
                inverse_root(krn[:, :], kss[:, :], krt[:, :], e)
                dve.wait_ge(sem("kk_ps"), r * NPG + NPG)
                both = pb[4][:, 0:256].rearrange("p (g a h) -> p g a h", g=NPG, a=2)
                e(tt(sc_s[:, 0:NPG, :], both[:, :, 0, :], krn[:, :].rearrange("p (g h) -> p g h", g=NPG), ALU.mult))
                e(tt(sc_s[:, 0:NPG, :], sc_s[:, 0:NPG, :], both[:, :, 1, :], ALU.add))
                e(ts(sc_s[0:1, NPG, :], s_own[:, bass.ds(r * NH, NH)], 1.0, None, ALU.mult))
                e(dve.tensor_reduce(tiny[:, 0:NH], sc_s[:, :, :].rearrange("p g h -> p h g"), AX_X, ALU.max), "s_max")
                dve.wait_ge(sem("max_ps"), r + 1)
                e(dve.tensor_reduce(tiny[0:NH, 8:9], pb[5][0:NH, 0:P], AX_X, ALU.max))
                e(ts(tiny[0:NH, 16:24], ident[0:NH, 0:NH], tiny[0:NH, 8:9], None, ALU.mult), "max_diag")
                dve.wait_ge(sem("maxb_ps"), r + 1)
                e(tt(sc_s[:, :, :], sc_s[:, :, :], pb[5][:, P:P + NH].unsqueeze(1).to_broadcast([P, NPG + 1, NH]), ALU.subtract), "s_shift")
                dve.wait_ge(sem("ps_ready"), r + 1)
                e(dve.tensor_reduce(tiny[:, 24:24 + NH], ps_s[:, :, :].rearrange("p g h -> p h g"), AX_X, ALU.add), "p_sum")
                dve.wait_ge(sem("ctx_ps"), r + 1)
                e(dve.reciprocal(tiny[:, 32:40], pb[5][:, 144:144 + NH]))
                e(tt(ctx_s[:, :, :, bass.ds(r, 1)].rearrange("p c h s -> p c (h s)"), pb[5][:, 160:160 + 2 * NH].rearrange("p (c h) -> p c h", c=KLC),
                     tiny[:, 32:40].unsqueeze(1).to_broadcast([P, KLC, NH]), ALU.mult), "ctx_ready")
                assert at[0] == LINKS
            w.next("mods_in", 16)
            w.next("mix_ps")
            add_mixed(NT, mod_smp[:, 2, :])

            def topk(src, size, v8, i8, name=None):
                n = v8.shape[0]
                d(dve.max(v8[:, 0:8], src))
                d(dve.max_index(i8[:, 0:8], v8[:, 0:8], src))
                d(dve.match_replace(src, v8[:, 0:8], src, LOWEST))
                d(dve.max(v8[:, 8:16], src))
                d(dve.max_index(i8[:, 8:16], v8[:, 8:16], src), name)

            def route(u):
                l, t = units[u]
                n = tokens(t)
                norm(x_tok[:, t, :], hbuf[:, u % 2, :], mod_smp if t == NT else mod_ffn, n)
                w.next("sco_ready")
                for q in range(NQ):
                    topk(sco[0:n, q * NK:(q + 1) * NK], NK, vals[0:n, q * TOPK:(q + 1) * TOPK], idx[0:n, q * TOPK:(q + 1) * TOPK])
                d(dve.tensor_copy(idxf[0:n, :], idx[0:n, :]))
                v4 = vals[0:n, :].rearrange("p (h a k) -> p h a k", h=PH, a=2)
                d(tt(cand[0:n, :].rearrange("p (h i j) -> p h i j", h=PH, i=TOPK), v4[:, :, 0, :].unsqueeze(3).to_broadcast([n, PH, TOPK, TOPK]),
                     v4[:, :, 1, :].unsqueeze(2).to_broadcast([n, PH, TOPK, TOPK]), ALU.add))
                for h in range(PH):
                    topk(cand[0:n, h * 256:(h + 1) * 256], 256, best[0:n, h * TOPK:(h + 1) * TOPK], flat[0:n, h * TOPK:(h + 1) * TOPK])
                d(ts(e1[0:n, :].bitcast(U32), flat[0:n, :], 4, None, ALU.logical_shift_right))
                d(dve.tensor_copy(fhi[0:n, :], e1[0:n, :].bitcast(U32)))
                d(ts(e1[0:n, :].bitcast(U32), flat[0:n, :], TOPK - 1, None, ALU.bitwise_and))
                d(dve.tensor_copy(flo[0:n, :], e1[0:n, :].bitcast(U32)))
                i4 = idxf[0:n, :].rearrange("p (h a k) -> p h a k", h=PH, a=2)
                hot = hits[0:n, :].rearrange("p (m k) -> p m k", m=KK)
                hot4 = hits[0:n, :].rearrange("p (h m k) -> p h m k", h=PH, m=TOPK)
                for side, (place, out) in enumerate(((fhi, e1), (flo, e2))):
                    d(tt(hot, place[0:n, :].unsqueeze(2).to_broadcast([n, KK, TOPK]), iota[0:n, :].unsqueeze(1).to_broadcast([n, KK, TOPK]), ALU.is_equal))
                    d(tt(hot4, hot4, i4[:, :, side, :].unsqueeze(2).to_broadcast([n, PH, TOPK, TOPK]), ALU.mult))
                    d(dve.tensor_reduce(out[0:n, :], hot, AX_X, ALU.add))
                d(stt(e1[0:n, :], e1[0:n, :], float(NK), e2[0:n, :], ALU.mult, ALU.add))
                b3 = best[0:n, :].rearrange("p (h k) -> p h k", h=PH)
                g3 = gate[0:n, :].rearrange("p (h k) -> p h k", h=PH)
                d(tt(e2[0:n, :].rearrange("p (h k) -> p h k", h=PH), b3, b3[:, :, 0:1].to_broadcast([n, PH, TOPK]), ALU.subtract), "best_neg")
                w.next("gate_exp")
                d(dve.tensor_reduce(tiny[0:n, 8:16], g3, AX_X, ALU.add))
                d(dve.reciprocal(tiny[0:n, 8:16], tiny[0:n, 8:16]))
                d(tt(g3, g3, tiny[0:n, 8:16].unsqueeze(2).to_broadcast([n, PH, TOPK]), ALU.mult), "route_done" if t == NT else None)
                if t < NT:
                    d(ts(expert[0:n, :], e1[0:n, :], float(l * NK * NK), None, ALU.add), "expert_set")
                else:
                    w.next("lane_ps")
                    pick = hits[:, 0:2 * KK].rearrange("p (a h k) -> p a h k", a=2, h=PH)
                    d(tt(pick, pb[2][:, 0:2 * KK].rearrange("p (a h k) -> p a h k", a=2, h=PH), lane.unsqueeze(1).unsqueeze(1).to_broadcast([P, 2, PH, TOPK]), ALU.mult))
                    d(dve.tensor_reduce(g_lane[:, :], pick[:, 1], AX_X, ALU.add))
                    d(dve.tensor_reduce(e2[:, 0:PH], pick[:, 0], AX_X, ALU.add))
                    d(ts(e_lane[:, :], e2[:, 0:PH], float(l * NK * NK), None, ALU.add), "expert_set")
                    w.next("lane_hidden")

            def experts(u, a, b):
                t = units[u][1]
                hb = hbuf[:, u % 2, :] if t < NT else hbuf[:, 2, :]
                g_all = gate if t < NT else g_lane
                with dve.Fori(a, b) as r:
                    for j in range(GRP):
                        dve.wait_ge(sem(f"u_in{j}"), r * 16 + (before[u] + 1) * 16)
                        if j == 0:
                            dve.wait_ge(sem("acts_set"), r + before[u])
                        ins = dve.tensor_tensor_reduce(ring[:, j, :], ring[:, j, :], hb, 1.0, 0.0, ALU.mult, ALU.add, dots[:, j:j + 1])
                        ins.then_inc(sem("u_used"), 1)
                    dve.wait_ge(sem("u_used"), r * GRP + (before[u] * GRP + 2 * GRP))
                    dve.sem_inc(sem("dots_set"), 1)
                    dve.wait_ge(sem("acts_set"), r + (before[u] + 1))
                    dve.wait_ge(sem("diag_set"), r * GRP + before[u] * GRP)
                    tt(wts[:, :], acts[:, :], g_all[:, bass.ds(r * GRP, GRP)], ALU.mult).then_inc(sem("wts_set"), 1)

            dve.sem_inc(sem("u_used"), GRP)
            for u, (l, t) in enumerate(units):
                if t == 0:
                    if l:
                        w.next("pool_in", 16, 3)
                        set_mods(mod_mix, P)
                        d(tt(mod_mix[:, 2, :], mod_mix[:, 2, :], pool_gain, ALU.mult))
                        for k in range(NT):
                            norm(x_tok[:, k, :], hbuf[:, k % 2, :], mod_mix, P)
                            w.next("mix_ps")
                            add_mixed(k, mod_mix[:, 2, :])
                        set_mods(mod_mix, NS)
                        d(tt(mod_mix[0:NS, 2, :], mod_mix[0:NS, 2, :], pool_gain[0:NS], ALU.mult))
                        norm(x_tok[:, NT, :], hbuf[:, NT % 2, :], mod_mix, NS)
                        w.next("mix_ps")
                        add_mixed(NT, mod_mix[:, 2, :])
                    set_mods(mod_ffn, P)
                    if l:
                        w.next("hbuf_free")
                if t == NT:
                    set_mods(mod_smp, NS)
                route(u)
                dve.sem_inc(sem("y_free"), 1)
                experts(u, 0, before[u + 1] - before[u])
                w.next("y_ps")
                add_mixed(t, (mod_smp if t == NT else mod_ffn)[:, 2, :], "x_routed")



_INS = ["x_prompt", "x_sample", "cache_mla", "state_pool", "page_table", "norm_mix", "norm_ffn", "w_ada", "b_ada", "w_mla_in",
        "g_q_lat", "g_kv_lat", "w_uq", "w_uk", "w_uv", "g_qn_nope", "g_qn_rope", "g_kn_nope", "g_kn_rope", "w_mla_out",
        "w_pool", "pool_scale", "w_peer_q", "peer_u", "peer_v"]
_OUTS = [("y_p", (1, SEQ, D)), ("y_s", (NS, 1, D)), ("rows_p", (1, 1, SEQ, ROW)), ("rows_s", (1, NS, 1, ROW)),
         ("pst_p", (1, 1, STATE, D)), ("pst_s", (1, NS, STATE, D))]


def kernel(**inputs):
    import concourse.bacc as bacc
    from concourse.bass_utils import run_bass_kernel_spmd

    nc = bacc.Bacc("TRN2", target_bir_lowering=False, num_devices=1)
    host = {name: np.ascontiguousarray(inputs[name]) for name in _INS}
    host["cT"] = np.ascontiguousarray(np.concatenate([inputs["c_sample"], inputs["c_prompt"]], axis=0).T)
    host["w_ukT"] = np.ascontiguousarray(np.transpose(inputs["w_uk"][0], (2, 1, 0)))
    keys = np.transpose(inputs["peer_subkeys"], (0, 4, 1, 2, 3))
    host["subkeysT"] = np.ascontiguousarray(keys.reshape(DEPTH, PEER_HALF, NQ, NK))
    host.update(shape_constants())
    arrays, T, O = {}, {}, {}
    for name, a in host.items():
        arrays["in_" + name] = a
        T[name] = nc.dram_tensor("in_" + name, a.shape, mybir.dt.from_np(a.dtype), kind="ExternalInput").ap()
    for name, shape in _OUTS:
        O[name] = nc.dram_tensor("out_" + name, shape, F32, kind="ExternalOutput").ap()
    decoder_step(nc, T, O)
    r = run_bass_kernel_spmd(nc, [arrays], core_ids=[0])
    return tuple(r.results[0]["out_" + name] for name, _ in _OUTS)
```

```python
from contextlib import ExitStack

import numpy as np

import concourse.bass as bass
from concourse import mybir

F32 = mybir.dt.float32
U32 = mybir.dt.uint32
I32 = mybir.dt.int32
ALU = mybir.AluOpType
ACT = mybir.ActivationFunctionType
AX_X = mybir.AxisListType.X

P = 128
D = 1024
DC = D // P
SEQ = 512
NT = SEQ // P
NS = 8
NC = NS + 1
PAST = 2048
PAGE = 128
NPG = PAST // PAGE
DEPTH = 2
EPS = 1e-6
NH = 8
NOPE, ROPE, VD = 128, 64, 128
QH = NOPE + ROPE
QL, KL = 384, 256
QLC, KLC = QL // P, KL // P
ROW = KL + ROPE
ZW = QL + KL + ROPE
SCALE = float(QH) ** -0.5
WINDOWS = (2, 4, 8, 16)
GD = D // 4
STATE = 15
PH = 8
NK = 128
TOPK = 16
PEER_HALF = 128
NQ = PH * 2
KK = PH * TOPK
NEG = -1.0e30
LOWEST = -3.0e38
GRP = 4
ADA = 6 * D


def shape_constants():
    inv = (10000.0 ** (-np.arange(0, ROPE, 2) / ROPE)).astype(np.float32)
    pos = np.concatenate([np.arange(SEQ), np.full(NS, PAST)]).astype(np.float32)
    ang = (pos[:, None] * inv[None, :]).astype(np.float32)
    cos, sin = np.cos(ang).astype(np.float32), np.sin(ang).astype(np.float32)
    rot = np.zeros((P, NT + 1, 2, ROPE), np.float32)
    for t in range(NT + 1):
        n = P if t < NT else NS
        rot[:n, t, 0] = np.tile(cos[t * P:t * P + n], 2)
        rot[:n, t, 1] = np.tile(sin[t * P:t * P + n], 2)
    i = np.arange(P)
    small = np.concatenate([
        np.eye(P), np.where(i[None, :] <= i[:, None], 0.0, NEG),
        (i[None, :] // TOPK == i[:, None]), (i[:, None] // TOPK == np.arange(NS)[None, :]),
        (i[:, None] % TOPK == np.arange(TOPK)[None, :]), np.tile(np.arange(TOPK), (P, 1)),
    ], axis=1).astype(np.float32)
    band = np.zeros((P, 4, 4, P), np.float32)
    for g, w in enumerate(WINDOWS):
        near = (i[:, None] <= i[None, :]) & (i[:, None] > i[None, :] - w)
        band[:, 0, g] = near / np.minimum(i + 1, w)[None, :] - np.eye(P)
        band[:, 1, g] = near / w - np.eye(P)
        band[:, 2, g] = (i[:, None] - P > i[None, :] - w) / w
        r = np.arange(NS * STATE)
        band[:NS * STATE, 3, g, :NS] = ((r[:, None] // STATE == np.arange(NS)) & (r[:, None] % STATE >= STATE - (w - 1))) / w
        band[:NS, 3, g, NS:2 * NS] = np.eye(NS) * (1.0 / w - 1.0)
    return {"rot": rot.reshape(P, -1), "small": small, "band": band.reshape(P, -1)}


def decoder_step(nc, T, O):
    ctx = ExitStack()
    with ctx:
        def sb(name, shape, dt=F32):
            return ctx.enter_context(nc.sbuf_tensor(name, shape, dt))

        sems = {}

        def sem(name):
            if name not in sems:
                sems[name] = ctx.enter_context(nc.semaphore(name))
            return sems[name]

        ada_rows = nc.dram_tensor("ada_rows", (DEPTH, NC, ADA), F32, kind="Internal").ap()

        W = 11904
        x_tok = sb("x_tok", [P, NT + 1, D])
        big = sb("big", [P, 16384])
        ring = sb("ring", [P, 8, D])
        mod_mix = sb("mod_mix", [P, 3, D])
        mod_smp = sb("mod_smp", [P, 3, D])
        hT = sb("hT", [P, DC * P])
        hbuf = sb("hbuf", [P, 3, D])
        work = sb("work", [P, W])
        small = sb("small", [P, 3 * P + NS + 2 * TOPK])
        tiny = sb("tiny", [P, 64])
        newton = sb("newton", [P, 48])
        ones = sb("ones", [P, P])
        ident = small[:, 0:P]
        causal = small[:, P:2 * P]
        sel = small[:, 2 * P:3 * P]
        selT = small[:, 3 * P:3 * P + NS]
        lane = small[:, 3 * P + NS:3 * P + NS + TOPK]
        iota = small[:, 3 * P + NS + TOPK:3 * P + NS + 2 * TOPK]

        pos = [0]

        def region(base, size, total):
            o = pos[0]
            pos[0] += size
            assert pos[0] <= total, (pos[0], total)
            return base[:, o:o + size]

        w_in = region(big, DC * ZW, 16384).rearrange("p (c n) -> p c n", c=DC)
        w_uq = region(big, QLC * NH * QH, 16384).rearrange("p (c n) -> p c n", c=QLC)
        w_uk = region(big, KLC * NH * NOPE, 16384).rearrange("p (c n) -> p c n", c=KLC)
        w_uv = region(big, KLC * NH * VD, 16384).rearrange("p (c n) -> p c n", c=KLC)
        w_ukT = region(big, NH * KL, 16384).rearrange("p (h n) -> p h n", h=NH)
        w_q = big[:, :].rearrange("p (c n) -> p c n", c=DC)
        w_ada = big[:, :].rearrange("p (s c n) -> p s c n", s=4, c=DC)
        w_out = ring[:, :, :]
        pos[0] = 0
        knT = region(work, NH * SEQ, W).rearrange("p (h n) -> p h n", h=NH)
        krT = region(work, SEQ, W)
        rows = region(work, (NT + 1) * ROW, W).rearrange("p (t n) -> p t n", t=NT + 1)
        latT = region(work, KLC * P, W).rearrange("p (c n) -> p c n", c=KLC)
        cqT = region(work, QLC * P, W).rearrange("p (c n) -> p c n", c=QLC)
        z = region(work, ZW, W)
        qs = region(work, NH * QH, W)
        qnT = region(work, NH * P, W)
        qrT = region(work, NH * P, W)
        pT = region(work, SEQ, W)
        ctxT = region(work, KLC * P, W)
        rot = sb("rot", [P, 2, ROPE])
        spare = mod_smp[:, :, :].rearrange("p m n -> p (m n)")
        gain_all = spare[:, 0:ZW + QH + NOPE]
        sq = spare[:, ZW + QH + NOPE:ZW + QH + NOPE + NH * QH]
        ks = hbuf[:, 1, :]
        oT = hbuf[:, 2, :]
        probs = hT[:, :].rearrange("p (b n) -> p b n", b=2)

        pos[0] = 0
        cached = region(work, (NPG + 1) * ROW, W).rearrange("p (g n) -> p g n", g=NPG + 1)
        cachedT = region(work, 2 * 3 * P, W).rearrange("p (b n) -> p b n", b=2)
        ksq = region(work, 2 * D, W).rearrange("p (b n) -> p b n", b=2)
        kss = region(work, NPG * NH, W)
        krn = region(work, NPG * NH, W)
        krt = region(work, NPG * NH, W)
        sc_s = region(work, (NPG + 1) * NH, W).rearrange("p (g h) -> p g h", g=NPG + 1)
        ps_s = region(work, (NPG + 1) * NH, W).rearrange("p (g h) -> p g h", g=NPG + 1)
        ctx_s = region(work, KLC * NH * NS, W).rearrange("p (c h s) -> p c h s", c=KLC, h=NH)
        oT_s = region(work, NH * NS, W)
        keep = sb("keep", [P, 256])
        own_dram = nc.dram_tensor("own_scores", (NS, NH), F32, kind="Internal").ap()
        zero = causal
        cact = hbuf[:, 2, 0:DC * NC].rearrange("p (c n) -> p c n", c=DC)

        def ada_bias(l):
            return work[0:NC, 0:ADA] if l == 0 else ring[0:NC, 0:6, :].rearrange("p a n -> p (a n)")
        q_abs = keep[:, 0:128].rearrange("p (c m) -> p c m", c=KLC)
        q_rot = keep[0:ROPE, 128:192]
        s_own = keep[0:1, 192:256]
        pages = sb("pages", [1, NS * NPG], mybir.dt.int32)

        pos[0] = 0
        mod_ffn = region(work, 3 * D, W).rearrange("p (m n) -> p m n", m=3)
        keysT = region(work, NQ * NK, W)
        shared = region(work, 5 * 2 * NK + 2 * D, W)
        q_tok, qT, sco, cand, hits = (shared[:, i * 2 * NK:(i + 1) * 2 * NK] for i in range(5))
        gain, mixed = shared[:, 10 * NK:10 * NK + D], shared[:, 10 * NK + D:10 * NK + 2 * D]
        vals = region(work, 2 * TOPK, W)
        idx = region(work, 2 * TOPK, W).bitcast(U32)
        idxf = region(work, 2 * TOPK, W)
        best = region(work, TOPK, W)
        flat = region(work, TOPK, W).bitcast(U32)
        place = region(work, 4 * TOPK, W)
        e_side = region(work, 2 * TOPK, W)
        soft = region(work, TOPK, W)
        soft_n = region(work, 4, W)
        expert = [region(work, KK, W) for _ in range(2)]
        gate = [region(work, KK, W) for _ in range(2)]
        turn = region(work, 2 * GRP, W).bitcast(U32).rearrange("p (b j) -> p b j", b=2)
        dots = region(work, GRP, W)
        acts = region(work, GRP, W)
        wts = region(work, GRP, W)
        diag = region(work, GRP * P, W).rearrange("p (j n) -> p j n", j=GRP)
        e_lane = region(work, PH, W).bitcast(U32)
        g_lane = region(work, PH, W)
        e_pick = region(work, PH, W)
        lane_pick = region(work, 2 * KK, W)
        band, dT = shared[:, 0:16 * P], shared[:, 16 * P:16 * P + D]
        state = mod_smp[:, 0, :]
        pool_gain = mod_smp[:, 1, :]
        w_pool = big[:, 0:DC * GD].rearrange("p (c n) -> p c n", c=DC)

        pb = [ctx.enter_context(nc.psum_tensor(f"bank{i}", [P, 512], F32)) for i in range(8)]

        units = [(l, t) for l in range(DEPTH) for t in range(NT + 1)]
        tokens = lambda t: P if t < NT else NS
        STEPS = KK // GRP
        SSTEPS = PH // GRP
        before = [0]
        for _, t in units:
            before.append(before[-1] + (STEPS if t < NT else SSTEPS))
        FREE = 2 * GRP
        ybank = lambda u: pb[4 + u % 2 * 2:6 + u % 2 * 2]

        def first_head(v, h):
            return h + v * PH

        mla_order = [NT] + list(range(NT))

        class Turns:

            def __init__(self, eng, own):
                self.eng, self.own, self.n, self.given = eng, own, {}, {}

            def next(self, name, unit=1, times=1):
                self.n[name] = self.n.get(name, 0) + unit * times
                self.eng.wait_ge(sem(name), self.n[name])

            def done(self, ins, name=None):
                name = name or self.own
                self.given[name] = self.given.get(name, 0) + 1
                ins.then_inc(sem(name), 1)
                self.eng.wait_ge(sem(name), self.given[name])

        for name in ("x_in", "consts_in", "c_in", "b_in", "table_in", "mix_w_in", "out_w_in", "gains_in", "rot_in",
                     "mods_in", "keys_in", "query_w_in", "pool_in", "state_in", "rows_out", "own_out", "own_in",
                     "y_out", "state_out", "dve_step", "act_step", "idx_read", "slot_turn"):
            sem(name)
        block = ctx.enter_context(nc.Block())

        @block.sync
        def _(sp):
            w = Turns(sp, "sp")

            def ld(dst, src, name):
                sp.dma_start(dst, src).then_inc(sem(name), 16)

            ld(small[:, :], T["small"], "consts_in")
            ld(hbuf[:, 0, 0:DC * NC].rearrange("p (c n) -> p c n", c=DC), T["cT"].rearrange("(c p) n -> p c n", p=P), "c_in")
            ld(pages[:, :], T["page_table"].rearrange("(a s) g -> a (s g)", a=1), "table_in")
            for l in range(DEPTH):
                ld(ada_bias(l),
                   T["b_ada"][l].partition_broadcast(NC), "b_in")
            def store_ada(i):
                l, j = divmod(i, ADA // 512)
                ld(ada_rows[l, :, j * 512:(j + 1) * 512], mod_mix[0:NC, 0, i % 2 * 512:(i % 2 + 1) * 512], f"ada_out{i % 2}")

            for l in range(DEPTH):
                for j in range(ADA // 512):
                    i = l * (ADA // 512) + j
                    if i >= 4:
                        sp.wait_ge(sem("ada_ps"), i - 3)
                    ld(w_ada[:, i % 4], T["w_ada"][l].rearrange("(c p) n -> p c n", p=P)[:, :, j * 512:(j + 1) * 512],
                       f"ada_w_in{i % 4}")
                    if i == 3:
                        for t in range(NT):
                            ld(x_tok[:, t, :], T["x_prompt"][0, t * P:(t + 1) * P, :], "x_in")
                        ld(x_tok[0:NS, NT, :], T["x_sample"].rearrange("b s d -> (b s) d"), "x_in")
                    if i >= 2:
                        sp.wait_ge(sem("ada_row"), i - 1)
                        store_ada(i - 2)
            for i in (2 * ADA // 512 - 2, 2 * ADA // 512 - 1):
                sp.wait_ge(sem("ada_row"), i + 1)
                store_ada(i)
            for j in range(2):
                sp.wait_ge(sem(f"ada_out{j}"), 16 * (ADA // 512))

            def mods(dst, l, first, who, n, norm, gain_=hT):
                for m, k in ((0, 1), (1, 0), (2, 2)):
                    cols = slice((first + k) * D, (first + k + 1) * D)
                    src = ada_rows[l, NC - 1, cols].partition_broadcast(n) if who == "prompt" else ada_rows[l, 0:NS, cols]
                    ld(dst[0:n, m, :], src, "mods_in")
                ld(gain_[0:n, :], norm.partition_broadcast(n), "mods_in")

            sp.wait_ge(sem("ada_ps"), 2 * ADA // 512)
            for dst, src in ((w_in, T["w_mla_in"][0]), (w_uq, T["w_uq"][0]),
                             (w_uk, T["w_uk"][0].rearrange("c h d -> c (h d)")), (w_uv, T["w_uv"][0].rearrange("c h d -> c (h d)"))):
                ld(dst, src.rearrange("(c p) n -> p c n", p=P), "mix_w_in")
            ld(w_ukT, T["w_ukT"], "mix_w_in")
            mods(mod_smp, 0, 0, "sample", NS, T["norm_mix"][0])
            w.next("mods_set")
            mods(mod_mix, 0, 0, "prompt", P, T["norm_mix"][0])
            sp.wait_ge(sem("ada_row"), 2 * ADA // 512)
            ld(w_out, T["w_mla_out"][0].rearrange("(c p) n -> p c n", p=P), "out_w_in")
            w.next("h_ready")
            o = 0
            for a, size in (("g_q_lat", QL), ("g_kv_lat", KL), ("g_kn_rope", ROPE), ("g_qn_nope", NOPE), ("g_qn_rope", ROPE), ("g_kn_nope", NOPE)):
                ld(gain_all[:, o:o + size], T[a][0].partition_broadcast(P), "gains_in")
                o += size
            for n_, t in enumerate(mla_order):
                if n_:
                    w.next("qk_norm")
                ld(rot[:, :, :], T["rot"].rearrange("p (t a b) -> p t a b", t=NT + 1, a=2)[:, t], "rot_in")
                w.next("row_ready")
                n = tokens(t)
                if t < NT:
                    ld(O["rows_p"][0, 0, t * P:(t + 1) * P, :], rows[:, t, :], "rows_out")
                else:
                    ld(O["rows_s"].rearrange("l b s n -> (l b s) n"), rows[0:NS, NT, :], "rows_out")
                    w.next("own_ready")
                    ld(own_dram, tiny[0:NS, 40:48], "own_out")
            w.next("qk_norm")
            for t in range(NT):
                w.next("x_mixed")
            sp.wait_ge(sem("rows_out"), 16 * (NT + 1))
            sp.wait_ge(sem("own_out"), 16)
            ld(s_own, own_dram.rearrange("(a s) h -> a (s h)", a=1), "own_in")
            w.next("smp_clear")
            ld(mod_smp[0:NS, 2, :], ada_rows[0, 0:NS, 2 * D:3 * D], "mods_in")
            w.next("table_in", 16)
            sp.sem_inc(sem("cached_free"), 1)
            with sp.Fori(0, NS) as r:
                sp.wait_ge(sem("cached_free"), r + 1)
                for g in range(NPG):
                    page = sp.value_load(pages[0:1, bass.ds(r * NPG + g, 1)], min_val=0, max_val=T["cache_mla"].shape[1] - 1)
                    ld(cached[:, g, :], T["cache_mla"][0, bass.ds(page, 1)].rearrange("a p n -> (a p) n"), f"page_in{g}")
                ld(cached[0:1, NPG, 0:KL], O["rows_s"][0, bass.ds(r, 1), 0, 0:KL], f"page_in{NPG}")
            w.next("x_mixed")
            for l in range(DEPTH):
                if l:
                    w.next("x_routed")
                    ld(w_pool, T["w_pool"][0].rearrange("g (a p) n -> p (g a) n", p=P), "pool_in")
                    ld(band.rearrange("p (k n) -> p k n", k=16), T["band"].rearrange("p (k n) -> p k n", k=16), "pool_in")
                    mods(mod_mix, 1, 0, "prompt", P, T["norm_mix"][1])
                    ld(pool_gain, T["pool_scale"][0].partition_broadcast(P), "pool_in")
                    w.next("mods_set")
                    for t in range(NT):
                        w.next("x_mixed")
                    ld(O["pst_p"][0, 0], hbuf[P - STATE:P, (NT - 1) % 2, :], "state_out")
                    mods(mod_mix, 1, 0, "sample", NS, T["norm_mix"][1])
                    w.next("mods_set")
                    ld(state[0:NS * STATE], T["state_pool"].rearrange("l b r d -> (l b r) d"), "state_in")
                    ld(O["pst_s"][0, :, 0:STATE - 1, :], T["state_pool"][0, :, 1:STATE, :], "state_out")
                    w.next("x_mixed")
                    ld(O["pst_s"][0, :, STATE - 1, :], hbuf[0:NS, NT % 2, :], "state_out")
                ld(w_q, T["w_peer_q"][l].rearrange("(c p) n -> p c n", p=P), "query_w_in")
                ld(keysT, T["subkeysT"][l], "keys_in")
                mods(mod_ffn, l, 3, "prompt", P, T["norm_ffn"][l], gain)
                for m, k in ((0, 1), (1, 0), (2, 2)):
                    ld(mod_smp[0:NS, m, :], ada_rows[l, 0:NS, (3 + k) * D:(4 + k) * D], "smp_mods_in")
                w.next("mods_set")
                if l:
                    sp.wait_ge(sem("state_out"), 48)
                    sp.sem_inc(sem("hbuf_free"), 1)
                for t in range(1, NT + 1):
                    w.next("x_routed")
                    if l:
                        ld(O["y_p"][0, (t - 1) * P:t * P, :], x_tok[:, t - 1, :], "y_out")
            w.next("x_routed")
            ld(O["y_s"].rearrange("b s d -> (b s) d"), x_tok[0:NS, NT, :], "y_out")
            sp.wait_ge(sem("y_out"), 16 * (NT + 1))

        @block.tensor
        def _(pe):
            w = Turns(pe, "pe")
            mm = pe.matmul

            w.next("consts_in", 16)
            w.next("c_act")
            for i in range(2 * ADA // 512):
                w.next(f"ada_w_in{i % 4}", 16)
                if i >= 2:
                    pe.wait_ge(sem("ada_row"), i - 1)
                for c in range(DC):
                    last = mm(pb[i % 2][0:NC, :], cact[:, c, :], w_ada[:, i % 4, c, :], start=(c == 0), stop=(c == DC - 1))
                last.then_inc(sem("ada_ps"), 1)

            def transpose_h(t, hb):
                n = tokens(t)
                w.next("h_ready")
                for c in range(DC):
                    k = c if n == NS else c % 4
                    last = pe.transpose(pb[4 + (c // 4 if n == P else 0)][:, k * n:k * n + n], hb[0:n, c * P:(c + 1) * P],
                                        ident[0:n, 0:n])
                last.then_inc(sem("hT_ps"), 1)

            for i, t in enumerate(mla_order):
                n = tokens(t)
                ht = lambda c: hT[:, c * n:(c + 1) * n]
                transpose_h(t, hbuf[:, 0, :])
                w.next("hT_ready")
                if i == 0:
                    w.next("mix_w_in", 16, 5)
                for half in range(2):
                    for c in range(DC):
                        last = mm(pb[half][0:n, 0:ZW // 2], ht(c), w_in[:, c, half * ZW // 2:(half + 1) * ZW // 2],
                                  start=(c == 0), stop=(c == DC - 1))
                last.then_inc(sem("z_ps"), 1)
                w.next("row_ready")
                for c in range(QLC):
                    pe.transpose(pb[6][:, c * n:(c + 1) * n], z[0:n, c * P:(c + 1) * P], ident[0:n, 0:n])
                for c in range(KLC):
                    pe.transpose(pb[7][:, c * n:(c + 1) * n], rows[0:n, t, c * P:(c + 1) * P], ident[0:n, 0:n])
                pe.transpose(pb[7][0:ROPE, KLC * n:KLC * n + n], rows[0:n, t, KL:ROW], ident[0:n, 0:n])\
                    .then_inc(sem("zT_ps"), 1)
                w.next("zT_ready")
                for b in range(3):
                    for c in range(QLC):
                        mm(pb[2 + b][0:n, :], cqT[:, c, 0:n], w_uq[:, c, b * 512:(b + 1) * 512], start=(c == 0), stop=(c == QLC - 1))
                for b in range(2):
                    for c in range(KLC):
                        last = mm(pb[b][0:n, :], latT[:, c, 0:n], w_uk[:, c, b * 512:(b + 1) * 512], start=(c == 0), stop=(c == KLC - 1))
                last.then_inc(sem("qk_ps"), 1)
                w.next("qk_norm")
                q3 = qs[0:n, :].rearrange("p (h d) -> p h d", h=NH)
                if t < NT:
                    for h in range(NH):
                        pe.transpose(pb[6 + h // 4][:, h % 4 * P:(h % 4 + 1) * P], q3[:, h, 0:NOPE], ident)
                        pe.transpose(pb[h // 4][0:ROPE, h % 4 * P:(h % 4 + 1) * P], q3[:, h, NOPE:QH], ident)
                        last = pe.transpose(pb[2 + h // 4][:, h % 4 * P:(h % 4 + 1) * P], ks[:, h * NOPE:(h + 1) * NOPE], ident)
                    last.then_inc(sem("qkT_ps"), 1)
                    w.next("qkT_ready")
                    keys = (t + 1) * P

                    def scores(h):
                        mm(pb[h % 2][:, 0:keys], qnT[:, h * P:(h + 1) * P], knT[:, h, 0:keys], start=True, stop=False)
                        mm(pb[h % 2][:, 0:keys], qrT[0:ROPE, h * P:(h + 1) * P], krT[0:ROPE, 0:keys], start=False, stop=True)\
                            .then_inc(sem("s_ps"), 1)

                    scores(0)
                    for h in range(NH):
                        if h + 1 < NH:
                            scores(h + 1)
                        w.next("p_norm")
                        for k in range(t + 1):
                            last = pe.transpose(pb[2][:, k * P:(k + 1) * P], probs[:, h % 2, k * P:(k + 1) * P], ident)
                        last.then_inc(sem("pT_ps"), 1)
                        w.next("pT_ready")
                        for c in range(KLC):
                            for k in range(t + 1):
                                last = mm(pb[3][:, c * P:(c + 1) * P], rows[:, k, c * P:(c + 1) * P], pT[:, k * P:(k + 1) * P],
                                          start=(k == 0), stop=(k == t))
                        last.then_inc(sem("cT_ps"), 1)
                        w.next("cT_ready")
                        for c in range(KLC):
                            last = mm(pb[4 + h // 4][:, h % 4 * P:(h % 4 + 1) * P], w_uv[:, c, h * VD:(h + 1) * VD],
                                      ctxT[:, c * P:(c + 1) * P], start=(c == 0), stop=(c == KLC - 1))
                    last.then_inc(sem("o_ps"), 1)
                    w.next("o_ready")
                    if t == 0:
                        w.next("out_w_in", 16)
                    for b in range(2):
                        for h in range(NH):
                            last = mm(pb[6 + b][:, :], oT[:, h * P:(h + 1) * P], w_out[:, h, b * 512:(b + 1) * 512],
                                      start=(h == 0), stop=(h == NH - 1))
                    last.then_inc(sem("mix_ps"), 1)
                else:
                    for h in range(NH):
                        pe.transpose(pb[6][:, h * NS:(h + 1) * NS], q3[:, h, 0:NOPE], ident[0:n, 0:n])
                        last = pe.transpose(pb[7][0:ROPE, h * NS:(h + 1) * NS], q3[:, h, NOPE:QH], ident[0:n, 0:n])
                    last.then_inc(sem("qkT_ps"), 1)
                    w.next("qkT_ready")
                    for c in range(KLC):
                        for h in range(NH):
                            last = mm(pb[2][:, (c * NH + h) * NS:(c * NH + h + 1) * NS], w_ukT[:, h, c * P:(c + 1) * P],
                                      qnT[:, h * NS:(h + 1) * NS], start=True, stop=True)
                    last.then_inc(sem("qa_ps"), 1)

            w.next("smp_clear")
            w.next("ones_set")
            with pe.Fori(0, NS) as r:
                def turn_page(g):
                    pe.wait_ge(sem(f"page_in{g}"), r * 16 + 16)
                    for c in range(KLC):
                        pe.transpose(pb[6 + g % 2][:, c * P:(c + 1) * P], cached[:, g, c * P:(c + 1) * P], ident)
                    pe.transpose(pb[6 + g % 2][0:ROPE, 2 * P:3 * P], cached[:, g, KL:ROW], ident).then_inc(sem("page_ps"), 1)

                turn_page(0)
                for g in range(NPG):
                    if g + 1 < NPG:
                        turn_page(g + 1)
                    pe.wait_ge(sem("pageT"), r * NPG + g + 1)
                    b = g % 2
                    for c in range(KLC):
                        mm(pb[4][:, g * 16:g * 16 + 8], cachedT[:, b, c * P:(c + 1) * P], q_abs[:, c, bass.ds(r * NH, NH)],
                           start=(c == 0), stop=(c == KLC - 1), skip_group_check=True)
                    mm(pb[4][:, g * 16 + 8:g * 16 + 16], cachedT[0:ROPE, b, 2 * P:3 * P], q_rot[:, bass.ds(r * NH, NH)],
                       start=True, stop=True, skip_group_check=True)
                    if g >= 2:
                        pe.wait_ge(sem("k_squares"), r * NPG + g - 1)
                    for half in range(2):
                        for c in range(KLC):
                            last = mm(pb[2 * b + half][:, :], cachedT[:, b, c * P:(c + 1) * P], w_uk[:, c, half * 512:(half + 1) * 512],
                                      start=(c == 0), stop=(c == KLC - 1))
                    last.then_inc(sem("kk_ps"), 1)
                pe.wait_ge(sem("s_max"), r + 1)
                pe.transpose(pb[5][0:NH, 0:P], tiny[:, 0:NH], ident).then_inc(sem("max_ps"), 1)
                pe.wait_ge(sem("max_diag"), r + 1)
                mm(pb[5][:, P:P + NH], ones[0:NH, :], tiny[0:NH, 16:16 + NH], start=True, stop=True).then_inc(sem("maxb_ps"), 1)
                pe.wait_ge(sem("p_sum"), r + 1)
                mm(pb[5][:, 144:144 + NH], ones[:, :], tiny[:, 24:24 + NH], start=True, stop=True)
                pe.wait_ge(sem(f"page_in{NPG}"), r * 16 + 16)
                for c in range(KLC):
                    for g in range(NPG + 1):
                        last = mm(pb[5][:, 160 + c * NH:160 + (c + 1) * NH], cached[:, g, c * P:(c + 1) * P], ps_s[:, g, :],
                                  start=(g == 0), stop=(g == NPG))
                last.then_inc(sem("ctx_ps"), 1)
                pe.wait_ge(sem("ctx_ps"), r + 1)
                pe.sem_inc(sem("cached_free"), 1)
            pe.wait_ge(sem("ctx_ready"), NS)
            for h in range(NH):
                for c in range(KLC):
                    last = mm(pb[0][:, h * NS:(h + 1) * NS], w_uv[:, c, h * VD:(h + 1) * VD], ctx_s[:, c, h, :],
                              start=(c == 0), stop=(c == KLC - 1))
            last.then_inc(sem("o_ps"), 1)
            w.next("o_ready")
            for b in range(2):
                for h in range(NH):
                    last = mm(pb[6 + b][0:NS, :], oT_s[:, h * NS:(h + 1) * NS], w_out[:, h, b * 512:(b + 1) * 512],
                              start=(h == 0), stop=(h == NH - 1))
            last.then_inc(sem("mix_ps"), 1)

            def pool(t):
                n = tokens(t)
                w.next("h_ready")
                if t == 0:
                    w.next("pool_in", 16, 3)
                if t == NT:
                    w.next("state_in", 16)
                hb = hbuf[:, t % 2, :]
                bd = band.rearrange("p (k g n) -> p k g n", k=4, g=4)
                for c in range(DC):
                    out = pb[c // 4 if n == P else 0][:, (c % 4 if n == P else c) * n:(c % 4 if n == P else c) * n + n]
                    ch = slice(c * P, (c + 1) * P)
                    if t == NT:
                        mm(out, state[0:NS * STATE, ch], bd[0:NS * STATE, 3, c // 2, 0:NS], start=True, stop=False)
                        last = mm(out, hb[0:NS, ch], bd[0:NS, 3, c // 2, NS:2 * NS], start=False, stop=True)
                    else:
                        if t:
                            mm(out, hbuf[:, (t - 1) % 2, ch], bd[:, 2, c // 2, :], start=True, stop=False)
                        last = mm(out, hb[:, ch], bd[:, min(t, 1), c // 2, :], start=(t == 0), stop=True)
                last.then_inc(sem("dT_ps"), 1)
                w.next("dT_ready")
                for g in range(4):
                    for a in range(2):
                        c = 2 * g + a
                        last = mm(pb[6 + g // 2][0:n, g % 2 * GD:(g % 2 + 1) * GD], dT[:, c * n:(c + 1) * n], w_pool[:, c, :],
                                  start=(a == 0), stop=(a == 1))
                last.then_inc(sem("mix_ps"), 1)

            def hidden_T(v):
                t = units[v][1]
                n = tokens(t)
                w.next("h_ready")
                for c in range(DC):
                    k = c if n == NS else c % 4
                    last = pe.transpose(pb[3 if c // 4 or n == NS else 0][:, k * n:k * n + n], hbuf[0:n, v % 3, c * P:(c + 1) * P],
                                        ident[0:n, 0:n])
                last.then_inc(sem("peer_hT_ps"), 1)

            def queries(v, h, first=False):
                n = tokens(units[v][1])
                if first:
                    w.next("peer_hT_ready")
                    if units[v][1] == 0:
                        w.next("query_w_in", 16)
                        w.next("keys_in", 16)
                for c in range(DC):
                    last = mm(pb[0][0:n, 0:2 * NK], hT[:, c * n:(c + 1) * n], w_q[:, c, bass.ds(h * 2 * NK, 2 * NK)],
                              start=(c == 0), stop=(c == DC - 1))
                last.then_inc(sem("q_ps"), 1)

            def queries_T(v, h):
                n = tokens(units[v][1])
                pe.wait_ge(sem("q_ready"), first_head(v, h) + 1)
                if n == NS:
                    pe.sem_inc(sem("wait_done"), 1)
                for side in range(2):
                    last = pe.transpose(pb[1][:, side * n:(side + 1) * n], q_tok[0:n, side * NK:(side + 1) * NK], ident[0:n, 0:n])
                last.then_inc(sem("qT_ps"), 1)

            def key_scores(v, h):
                n = tokens(units[v][1])
                pe.wait_ge(sem("qT_ready"), first_head(v, h) + 1)
                for side in range(2):
                    last = mm(pb[2][0:n, side * NK:(side + 1) * NK], qT[:, side * n:(side + 1) * n],
                              keysT[:, bass.ds(h * 2 * NK + side * NK, NK)], start=True, stop=True, skip_group_check=True)
                last.then_inc(sem("sco_ps"), 1)

            def expert_turn(u, k):
                n = tokens(units[u][1])
                for j in range(GRP):
                    pe.wait_ge(sem("diag_set"), k * GRP + (before[u] * GRP + GRP + j + 1))
                    pe.wait_ge(sem(f"v_in{j}"), k * 16 + (before[u] + 1) * 16)
                    for half in range(2):
                        last = mm(ybank(u)[half][0:n, :], diag[:, j, 0:n], ring[:, GRP + j, half * 512:(half + 1) * 512],
                                  start=False, stop=False, skip_group_check=True)
                    last.then_inc(sem("v_used"), 1)

            def open_y(u):
                n = tokens(units[u][1])
                if u >= 2:
                    pe.wait_ge(sem("x_routed"), u - 1)
                for half in range(2):
                    mm(ybank(u)[half][0:n, :], zero[:, 0:n], w_q[:, 0, half * 512:(half + 1) * 512],
                       start=True, stop=False, skip_group_check=True)

            def close_y(u):
                n = tokens(units[u][1])
                mm(ybank(u)[1][0:n, 0:64], zero[:, 0:n], w_q[:, 0, 0:64], start=False, stop=True, skip_group_check=True)\
                    .then_inc(sem("y_ps"), 1)

            def route(v, u, nxt):
                def head(h, last):
                    for k in range(4):
                        if u is not None:
                            expert_turn(u, h * 4 + k)
                        if not last:
                            (lambda: queries(v, h + 1), lambda: queries_T(v, h + 1), lambda: key_scores(v, h + 1), lambda: None)[k]()
                        elif nxt is not None:
                            (lambda: hidden_T(nxt), lambda: queries(nxt, 0, True), lambda: queries_T(nxt, 0), lambda: None)[k]()

                if u is not None:
                    open_y(u)
                with pe.Fori(0, PH - 1) as h:
                    head(h, False)
                head(PH - 1, True)
                if u is not None:
                    close_y(u)
                if nxt is not None:
                    key_scores(nxt, 0)

            pe.sem_inc(sem("v_used"), FREE)
            for u, (l, t) in enumerate(units):
                if t == 0:
                    if l:
                        for k in range(NT + 1):
                            pool(k)
                    hidden_T(u)
                    queries(u, 0, True)
                    queries_T(u, 0)
                    key_scores(u, 0)
                    route(u, None, u + 1)
                if t < NT:
                    route(u + 1, u, u + 2 if t + 2 <= NT else None)
                else:
                    w.next("route_done")
                    for half in range(2):
                        mm(pb[half][:, :], sel[0:NS, :], hbuf[0:NS, u % 3, half * 512:(half + 1) * 512], start=True, stop=True)
                    mm(pb[2][:, 0:KK], sel[0:NS, :], expert[u % 2][0:NS, :], start=True, stop=True)
                    mm(pb[2][:, KK:2 * KK], sel[0:NS, :], gate[u % 2][0:NS, :], start=True, stop=True, skip_group_check=True)\
                        .then_inc(sem("lane_ps"), 1)
                    open_y(u)
                    with pe.Fori(0, SSTEPS) as r:
                        expert_turn(u, r)
                    close_y(u)

        @block.scalar
        def _(act):
            w = Turns(act, "act_step")

            def copy(out, in_, name=None):
                w.done(act.activation(out, in_, ACT.Copy), name)

            w.next("c_in", 16)
            w.done(act.activation(hbuf[:, 1, 0:DC * NC], hbuf[:, 0, 0:DC * NC], ACT.Exp, scale=-1.0), "c_exp")

            def copy_hT(t):
                w.next("hT_ps")
                if tokens(t) == P:
                    copy(hT[:, 0:512], pb[4][:, :])
                    copy(hT[:, 512:1024], pb[5][:, :], "hT_ready")
                else:
                    copy(hT[:, 0:DC * NS], pb[4][:, 0:DC * NS], "hT_ready")

            for t in mla_order:
                n = tokens(t)
                copy_hT(t)
                w.next("z_ps")
                copy(z[0:n, 0:ZW // 2], pb[0][0:n, 0:ZW // 2])
                copy(z[0:n, ZW // 2:ZW], pb[1][0:n, 0:ZW // 2], "z_ready")
                w.next("zT_ps")
                copy(cqT[:, :, 0:n], pb[6][:, 0:QLC * n].rearrange("p (c n) -> p c n", c=QLC))
                if t < NT:
                    copy(krT[0:ROPE, t * P:(t + 1) * P], pb[7][0:ROPE, KLC * n:KLC * n + n])
                copy(latT[:, :, 0:n], pb[7][:, 0:KLC * n].rearrange("p (c n) -> p c n", c=KLC), "zT_ready")
                w.next("qk_ps")
                for b in range(3):
                    copy(qs[0:n, b * 512:(b + 1) * 512], pb[2 + b][0:n, :])
                copy(ks[0:n, 0:512], pb[0][0:n, :])
                copy(ks[0:n, 512:1024], pb[1][0:n, :], "qk_ready")
                w.next("qkT_ps")
                if t == NT:
                    copy(q_rot.rearrange("p (s h) -> p s h", s=NS), pb[7][0:ROPE, 0:64].rearrange("p (h s) -> p s h", h=NH))
                    copy(qnT[:, 0:64], pb[6][:, 0:64], "qkT_ready")
                    w.next("qa_ps")
                    for c in range(KLC):
                        copy(q_abs[:, c, :].rearrange("p (s h) -> p s h", s=NS),
                             pb[2][:, c * 64:(c + 1) * 64].rearrange("p (h s) -> p s h", h=NH), "qa_ready" if c else None)
                    continue
                for b in range(2):
                    copy(qnT[:, b * 512:(b + 1) * 512], pb[6 + b][:, :])
                    copy(qrT[0:ROPE, b * 512:(b + 1) * 512], pb[b][0:ROPE, :])
                    copy(knT[:, 4 * b:4 * b + 4, t * P:(t + 1) * P], pb[2 + b][:, :].rearrange("p (h n) -> p h n", h=4),
                         "qkT_ready" if b else None)
                keys = (t + 1) * P
                def soften(h):
                    w.next("s_neg")
                    w.done(act.activation(probs[:, h % 2, 0:keys], pb[h % 2][:, 0:keys], ACT.Exp, bias=tiny[:, 56 + h % 2:57 + h % 2],
                                          accum_out=tiny[:, 58 + h % 2:59 + h % 2]), "p_ready")
                soften(0)
                for h in range(NH):
                    if h + 1 < NH:
                        soften(h + 1)
                    w.next("pT_ps")
                    copy(pT[:, 0:keys], pb[2][:, 0:keys], "pT_ready")
                    w.next("cT_ps")
                    copy(ctxT[:, :], pb[3][:, 0:256], "cT_ready")
                w.next("o_ps")
                copy(oT[:, 0:512], pb[4][:, :])
                copy(oT[:, 512:1024], pb[5][:, :], "o_ready")

            w.next("smp_clear")
            with act.Fori(0, NS) as r:
                for g in range(NPG):
                    def square(k):
                        act.wait_ge(sem("kk_ps"), r * NPG + k + 1)
                        if k >= 2:
                            act.wait_ge(sem("k_sums"), r * NPG + k - 1)
                        for half in range(2):
                            last = act.activation(ksq[:, k % 2, half * 512:(half + 1) * 512], pb[2 * (k % 2) + half][:, :], ACT.Square)
                        last.then_inc(sem("k_squares"), 1)
                    act.wait_ge(sem("page_ps"), r * NPG + g + 1)
                    act.activation(cachedT[:, g % 2, 0:256], pb[6 + g % 2][:, 0:256], ACT.Copy)
                    act.activation(cachedT[0:ROPE, g % 2, 256:384], pb[6 + g % 2][0:ROPE, 256:384], ACT.Copy).then_inc(sem("pageT"), 1)
                    if g:
                        square(g - 1)
                square(NPG - 1)
                act.wait_ge(sem("s_shift"), r + 1)
                act.activation(ps_s[:, :, :], sc_s[:, :, :], ACT.Exp).then_inc(sem("ps_ready"), 1)
            w.next("o_ps")
            copy(oT_s[:, :], pb[0][:, 0:64], "o_ready")

            def copy_hidden_T(v):
                n = tokens(units[v][1])
                w.next("peer_hT_ps")
                if n == P:
                    copy(hT[:, 0:512], pb[0][:, :])
                    copy(hT[:, 512:1024], pb[3][:, :], "peer_hT_ready")
                else:
                    copy(hT[:, 0:DC * NS], pb[3][:, 0:DC * NS], "peer_hT_ready")

            def copy_queries(v, h):
                n = tokens(units[v][1])
                act.wait_ge(sem("q_ps"), first_head(v, h) + 1)
                act.activation(q_tok[0:n, :], pb[0][0:n, 0:2 * NK], ACT.Copy).then_inc(sem("q_ready"), 1)

            def copy_queries_T(v, h):
                n = tokens(units[v][1])
                act.wait_ge(sem("qT_ps"), first_head(v, h) + 1)
                act.activation(qT[:, 0:2 * n], pb[1][:, 0:2 * n], ACT.Copy).then_inc(sem("qT_ready"), 1)

            def copy_scores(v, h):
                n = tokens(units[v][1])
                act.wait_ge(sem("sco_ps"), first_head(v, h) + 1)
                act.wait_ge(sem("sides_done"), first_head(v, h) + 1)
                act.activation(sco[0:n, :], pb[2][0:n, 0:2 * NK], ACT.Copy).then_inc(sem("sco_ready"), 1)

            def soften_best(v, h):
                n = tokens(units[v][1])
                act.wait_ge(sem("best_ready"), first_head(v, h) + 1)
                act.activation(soft[0:n, :], best[0:n, :], ACT.Exp, bias=soft_n[0:n, 0:1], accum_out=soft_n[0:n, 1:2])\
                    .then_inc(sem("soft_ready"), 1)

            def expert_turn(u, k):
                n = tokens(units[u][1])
                scale_rows = ident if n == P else selT
                act.wait_ge(sem("dots_set"), k + (before[u] + 1))
                act.activation(acts[:, :], dots[:, :], ACT.Gelu).then_inc(sem("acts_set"), 1)
                act.wait_ge(sem("wts_set"), k + (before[u] + 1))
                for j in range(GRP):
                    act.wait_ge(sem("v_used"), k * GRP + (before[u] * GRP + GRP + j + 1))
                    act.activation(diag[:, j, 0:n], scale_rows, ACT.Copy, scale=wts[:, j:j + 1]).then_inc(sem("diag_set"), 1)

            def route(v, u, nxt):
                def head(h, last):
                    for k in range(4):
                        if u is not None:
                            expert_turn(u, h * 4 + k)
                        if k == 3:
                            soften_best(v, h)
                        if not last:
                            (lambda: None, lambda: copy_queries(v, h + 1), lambda: copy_queries_T(v, h + 1), lambda: copy_scores(v, h + 1))[k]()
                        elif nxt is not None:
                            (lambda: None, lambda: copy_hidden_T(nxt), lambda: copy_queries(nxt, 0), lambda: copy_queries_T(nxt, 0))[k]()

                with act.Fori(0, PH - 1) as h:
                    head(h, False)
                head(PH - 1, True)
                if nxt is not None:
                    copy_scores(nxt, 0)

            for u, (l, t) in enumerate(units):
                if t == 0:
                    if l:
                        for k in range(NT + 1):
                            w.next("dT_ps")
                            if k < NT:
                                copy(dT[:, 0:512], pb[0][:, :])
                                copy(dT[:, 512:1024], pb[1][:, :], "dT_ready")
                            else:
                                copy(dT[:, 0:DC * NS], pb[0][:, 0:DC * NS], "dT_ready")
                    copy_hidden_T(u)
                    copy_queries(u, 0)
                    copy_queries_T(u, 0)
                    copy_scores(u, 0)
                    route(u, None, u + 1)
                if t < NT:
                    route(u + 1, u, u + 2 if t + 2 <= NT else None)
                else:
                    w.next("lane_ps")
                    for half in range(2):
                        copy(hbuf[:, (u + 1) % 3, half * 512:(half + 1) * 512], pb[half][:, :], "lane_hidden" if half else None)
                    with act.Fori(0, SSTEPS) as r:
                        expert_turn(u, r)

        @block.gpsimd
        def _(pool):
            nc.gpsimd.memset(ones[:, :], 1.0).then_inc(sem("ones_set"), 1)
            for u, (l, t) in enumerate(units):
                pool.wait_ge(sem("expert_set"), u + 1)
                if u == 0:
                    pool.wait_ge(sem("mix_ps"), NT + 1)
                with pool.Fori(0, (before[u + 1] - before[u]) // 2) as r:
                    for half in range(2):
                        base = before[u] + half
                        pool.wait_ge(sem("u_used"), r * 2 * GRP + (base * GRP + GRP))
                        pool.sem_inc(sem("slot_turn"), 1)
                        pool.wait_ge(sem("v_used"), r * 2 * GRP + (base * GRP + GRP))
                        pool.sem_inc(sem("slot_turn"), 1)
                        src = expert[u % 2].bitcast(U32) if t < NT else e_lane
                        pool.tensor_copy(turn[:, half, :], src[:, bass.ds(r * 2 * GRP + half * GRP, GRP)]).then_inc(sem("turn_set"), 1)
                        pool.wait_ge(sem("turn_set"), r * 2 + (base + 1))
                        pool.sem_inc(sem("slot_turn"), 1)
                        for kind, table, used in (("u", T["peer_u"].rearrange("l e d -> (l e) d"), "u_used"),
                                                  ("v", T["peer_v"].rearrange("l e d -> (l e) d"), "v_used")):
                            for j in range(GRP):
                                pool.wait_ge(sem(used), r * 2 * GRP + (base * GRP + GRP + j + 1))
                                pool.sem_inc(sem("slot_turn"), 1)
                                pool.indirect_dma_start(ring[:, (GRP if kind == "v" else 0) + j, :], None, table,
                                                        bass.IndirectOffsetOnAxis(turn[:, half, j:j + 1], 0))\
                                    .then_inc(sem(f"{kind}_in{j}"), 16)

        @block.vector
        def _(dve):
            w = Turns(dve, "dve_step")
            d = w.done
            tt, ts, stt = dve.tensor_tensor, dve.tensor_scalar, dve.scalar_tensor_tensor

            w.next("c_exp")
            d(ts(hbuf[:, 1, 0:DC * NC], hbuf[:, 1, 0:DC * NC], 1.0, None, ALU.add))
            d(dve.reciprocal(hbuf[:, 1, 0:DC * NC], hbuf[:, 1, 0:DC * NC]))
            d(tt(cact.rearrange("p c n -> p (c n)"), hbuf[:, 0, 0:DC * NC], hbuf[:, 1, 0:DC * NC], ALU.mult), "c_act")
            w.next("b_in", 16, 2)
            for i in range(2 * ADA // 512):
                l, j = divmod(i, ADA // 512)
                w.next("ada_ps")
                if i >= 2:
                    dve.wait_ge(sem(f"ada_out{i % 2}"), 16 * (i // 2))
                bias = ada_bias(l)
                d(tt(mod_mix[0:NC, 0, i % 2 * 512:(i % 2 + 1) * 512], pb[i % 2][0:NC, :], bias[:, j * 512:(j + 1) * 512], ALU.add), "ada_row")

            def inverse_root(y, v, t, link):
                link(ts(y.bitcast(I32), v.bitcast(I32), -0.5, float(0x5F3759DF), ALU.mult, ALU.add))
                for _ in range(3):
                    link(tt(t, y, y, ALU.mult))
                    link(stt(t, t, -0.5, v, ALU.mult, ALU.mult))
                    link(stt(y, t, 1.5, y, ALU.add, ALU.mult))

            def set_mods(m, n, gain_=hT, loads=("mods_in", 16, 4)):
                w.next(*loads)
                d(stt(m[0:n, 0, :], m[0:n, 0, :], 1.0, gain_[0:n, :], ALU.add, ALU.mult), "mods_set" if loads[0] == "mods_in" else None)

            def norm(xt, hb, m, n):
                d(stt(hb[0:n, :], xt[0:n, :], 1.0, xt[0:n, :], ALU.mult, ALU.mult, accum_out=tiny[0:n, 0:1]))
                d(ts(tiny[0:n, 1:2], tiny[0:n, 0:1], 1.0 / D, EPS, ALU.mult, ALU.add))
                inverse_root(tiny[0:n, 2:3], tiny[0:n, 1:2], newton[0:n, 0:1], d)
                d(stt(hb[0:n, :], xt[0:n, :], tiny[0:n, 2:3], m[0:n, 0, :], ALU.mult, ALU.mult))
                d(tt(hb[0:n, :], hb[0:n, :], m[0:n, 1, :], ALU.add), "h_ready")

            def add_mixed(t, gate_, name="x_mixed", banks=None, tmp=hT):
                n = tokens(t)
                for b, bank in enumerate(banks or pb[6:8]):
                    part = slice(b * 512, (b + 1) * 512)
                    d(tt(tmp[0:n, part], bank[0:n, :], gate_[0:n, part], ALU.mult))
                    d(tt(x_tok[0:n, t, part], x_tok[0:n, t, part], tmp[0:n, part], ALU.add), name if b else None)

            w.next("x_in", 16, NT + 1)
            w.next("consts_in", 16)
            set_mods(mod_smp, NS)
            set_mods(mod_mix, P)
            gq, gkv, gkr = gain_all[:, 0:QL], gain_all[:, QL:QL + KL], gain_all[:, QL + KL:ZW]
            gqn, gqr, gkn = (gain_all[:, ZW:ZW + NOPE], gain_all[:, ZW + NOPE:ZW + QH], gain_all[:, ZW + QH:ZW + QH + NOPE])

            def rotate(out1, out2, m1, m2):
                half = ROPE // 2
                d(tt(out1, m1[..., 0:half], m2[..., half:ROPE], ALU.subtract))
                return tt(out2, m2[..., 0:half], m1[..., half:ROPE], ALU.add)

            for i, t in enumerate(mla_order):
                n = tokens(t)
                norm(x_tok[:, t, :], hbuf[:, 0, :], mod_smp if t == NT else mod_mix, n)
                if i == 0:
                    w.next("gains_in", 16, 6)
                    d(stt(gqn, gqn, SCALE, gkn, ALU.mult, ALU.mult))
                    d(ts(gqr, gqr, SCALE, None, ALU.mult))
                w.next("z_ready")
                for k, (a, b) in enumerate(((0, QL), (QL, QL + KL), (QL + KL, ZW))):
                    d(stt(sq[0:n, a:b], z[0:n, a:b], 1.0, z[0:n, a:b], ALU.mult, ALU.mult, accum_out=tiny[0:n, 4 + k:5 + k]))
                    d(ts(newton[0:n, 24 + k:25 + k], tiny[0:n, 4 + k:5 + k], 1.0 / (b - a), EPS, ALU.mult, ALU.add))
                inverse_root(tiny[0:n, 4:7], newton[0:n, 24:27], newton[0:n, 0:3], d)
                d(stt(z[0:n, 0:QL], z[0:n, 0:QL], tiny[0:n, 4:5], gq[0:n], ALU.mult, ALU.mult))
                d(stt(rows[0:n, t, 0:KL], z[0:n, QL:QL + KL], tiny[0:n, 5:6], gkv[0:n], ALU.mult, ALU.mult))
                d(stt(z[0:n, QL + KL:ZW], z[0:n, QL + KL:ZW], tiny[0:n, 6:7], gkr[0:n], ALU.mult, ALU.mult))
                w.next("rot_in", 16)
                for k in range(2):
                    d(tt(sq[0:n, k * ROPE:(k + 1) * ROPE], z[0:n, QL + KL:ZW], rot[0:n, k, :], ALU.mult))
                d(rotate(rows[0:n, t, KL:KL + ROPE // 2], rows[0:n, t, KL + ROPE // 2:ROW], sq[0:n, 0:ROPE], sq[0:n, ROPE:2 * ROPE]), "row_ready")
                w.next("qk_ready")
                q3 = qs[0:n, :].rearrange("p (h d) -> p h d", h=NH)
                s3 = sq[0:n, :].rearrange("p (h d) -> p h d", h=NH)
                k3 = ks[0:n, :].rearrange("p (h d) -> p h d", h=NH)
                d(tt(sq[0:n, :], qs[0:n, :], qs[0:n, :], ALU.mult))
                d(dve.tensor_reduce(tiny[0:n, 8:16], s3[:, :, 0:NOPE], AX_X, ALU.add))
                d(dve.tensor_reduce(tiny[0:n, 16:24], s3[:, :, NOPE:QH], AX_X, ALU.add))
                d(tt(sq[0:n, 0:D], ks[0:n, :], ks[0:n, :], ALU.mult))
                d(dve.tensor_reduce(tiny[0:n, 24:32], sq[0:n, 0:D].rearrange("p (h d) -> p h d", h=NH), AX_X, ALU.add))
                for a, width in ((8, NOPE), (16, ROPE), (24, NOPE)):
                    d(ts(newton[0:n, a + 16:a + 24], tiny[0:n, a:a + 8], 1.0 / width, EPS, ALU.mult, ALU.add))
                inverse_root(tiny[0:n, 8:32], newton[0:n, 24:48], newton[0:n, 0:24], d)

                def heads(a, width):
                    return tiny[0:n, a:a + 8].unsqueeze(2).to_broadcast([n, NH, width])

                def over_heads(g, width):
                    return g[0:n, :].unsqueeze(1).to_broadcast([n, NH, width])

                d(tt(q3[:, :, 0:NOPE], q3[:, :, 0:NOPE], heads(8, NOPE), ALU.mult))
                d(tt(q3[:, :, 0:NOPE], q3[:, :, 0:NOPE], over_heads(gqn, NOPE), ALU.mult))
                d(tt(q3[:, :, NOPE:QH], q3[:, :, NOPE:QH], heads(16, ROPE), ALU.mult))
                d(tt(q3[:, :, NOPE:QH], q3[:, :, NOPE:QH], over_heads(gqr, ROPE), ALU.mult))
                m = [sq[0:n, k * 512:(k + 1) * 512].rearrange("p (h d) -> p h d", h=NH) for k in range(2)]
                for k in range(2):
                    d(tt(m[k], q3[:, :, NOPE:QH], rot[0:n, k, :].unsqueeze(1).to_broadcast([n, NH, ROPE]), ALU.mult))
                d(rotate(q3[:, :, NOPE:NOPE + 32], q3[:, :, NOPE + 32:QH], m[0], m[1]))
                d(tt(k3, k3, heads(24, NOPE), ALU.mult), "qk_norm")
                if t == NT:
                    d(tt(sq[0:n, 0:D].rearrange("p (h d) -> p h d", h=NH), q3[:, :, 0:NOPE], k3, ALU.mult))
                    d(dve.tensor_reduce(tiny[0:n, 32:40], sq[0:n, 0:D].rearrange("p (h d) -> p h d", h=NH), AX_X, ALU.add))
                    d(tt(sq[0:n, 0:512].rearrange("p (h d) -> p h d", h=NH), q3[:, :, NOPE:QH],
                         rows[0:n, NT, KL:ROW].unsqueeze(1).to_broadcast([n, NH, ROPE]), ALU.mult))
                    d(dve.tensor_reduce(tiny[0:n, 40:48], sq[0:n, 0:512].rearrange("p (h d) -> p h d", h=NH), AX_X, ALU.add))
                    d(tt(tiny[0:n, 40:48], tiny[0:n, 40:48], tiny[0:n, 32:40], ALU.add), "own_ready")
                    continue
                keys = (t + 1) * P
                def row_max(h):
                    w.next("s_ps")
                    b = pb[h % 2]
                    d(tt(b[:, t * P:keys], b[:, t * P:keys], causal, ALU.add))
                    d(dve.tensor_reduce(tiny[:, 60:61], b[:, 0:keys], AX_X, ALU.max))
                    d(ts(tiny[:, 56 + h % 2:57 + h % 2], tiny[:, 60:61], -1.0, None, ALU.mult), "s_neg")
                row_max(0)
                for h in range(NH):
                    if h + 1 < NH:
                        row_max(h + 1)
                    w.next("p_ready")
                    d(dve.reciprocal(tiny[:, 61:62], tiny[:, 58 + h % 2:59 + h % 2]))
                    d(ts(probs[:, h % 2, 0:keys], probs[:, h % 2, 0:keys], tiny[:, 61:62], None, ALU.mult), "p_norm")
                w.next("mix_ps")
                add_mixed(t, mod_mix[:, 2, :])

            d(dve.memset(sc_s[:, :, :], LOWEST))
            d(dve.memset(cached[:, NPG, :], 0.0), "smp_clear")
            w.next("own_in", 16)
            d(dve.memset(zero, 0.0), "zero_set")
            LINKS = 16
            with dve.Fori(0, NS) as r:
                at = [0]

                def e(ins, name=None):
                    if name is None:
                        at[0] += 1
                        ins.then_inc(sem("smp_step"), 1)
                        dve.wait_ge(sem("smp_step"), r * LINKS + at[0])
                    else:
                        ins.then_inc(sem(name), 1)
                        dve.wait_ge(sem(name), r + 1)

                for g in range(NPG):
                    dve.wait_ge(sem("k_squares"), r * NPG + g + 1)
                    dve.tensor_reduce(kss[:, g * NH:(g + 1) * NH], ksq[:, g % 2, :].rearrange("p (h d) -> p h d", h=NH), AX_X, ALU.add)\
                        .then_inc(sem("k_sums"), 1)
                dve.wait_ge(sem("k_sums"), r * NPG + NPG)
                e(ts(kss[:, :], kss[:, :], 1.0 / NOPE, EPS, ALU.mult, ALU.add))
                inverse_root(krn[:, :], kss[:, :], krt[:, :], e)
                dve.wait_ge(sem("kk_ps"), r * NPG + NPG)
                both = pb[4][:, 0:256].rearrange("p (g a h) -> p g a h", g=NPG, a=2)
                e(tt(sc_s[:, 0:NPG, :], both[:, :, 0, :], krn[:, :].rearrange("p (g h) -> p g h", g=NPG), ALU.mult))
                e(tt(sc_s[:, 0:NPG, :], sc_s[:, 0:NPG, :], both[:, :, 1, :], ALU.add))
                e(ts(sc_s[0:1, NPG, :], s_own[:, bass.ds(r * NH, NH)], 1.0, None, ALU.mult))
                e(dve.tensor_reduce(tiny[:, 0:NH], sc_s[:, :, :].rearrange("p g h -> p h g"), AX_X, ALU.max), "s_max")
                dve.wait_ge(sem("max_ps"), r + 1)
                e(dve.tensor_reduce(tiny[0:NH, 8:9], pb[5][0:NH, 0:P], AX_X, ALU.max))
                e(ts(tiny[0:NH, 16:24], ident[0:NH, 0:NH], tiny[0:NH, 8:9], None, ALU.mult), "max_diag")
                dve.wait_ge(sem("maxb_ps"), r + 1)
                e(tt(sc_s[:, :, :], sc_s[:, :, :], pb[5][:, P:P + NH].unsqueeze(1).to_broadcast([P, NPG + 1, NH]), ALU.subtract), "s_shift")
                dve.wait_ge(sem("ps_ready"), r + 1)
                e(dve.tensor_reduce(tiny[:, 24:24 + NH], ps_s[:, :, :].rearrange("p g h -> p h g"), AX_X, ALU.add), "p_sum")
                dve.wait_ge(sem("ctx_ps"), r + 1)
                e(dve.reciprocal(tiny[:, 32:40], pb[5][:, 144:144 + NH]))
                e(tt(ctx_s[:, :, :, bass.ds(r, 1)].rearrange("p c h s -> p c (h s)"), pb[5][:, 160:160 + 2 * NH].rearrange("p (c h) -> p c h", c=KLC),
                     tiny[:, 32:40].unsqueeze(1).to_broadcast([P, KLC, NH]), ALU.mult), "ctx_ready")
                assert at[0] == LINKS
            w.next("mods_in", 16)
            w.next("mix_ps")
            add_mixed(NT, mod_smp[:, 2, :])

            LINKS_HEAD = 26

            def rank(v, h, last, nxt):
                l, t = units[v]
                n = tokens(t)
                G = first_head(v, h)
                at = [0]

                def e(ins, name=None):
                    if name is None:
                        at[0] += 1
                        ins.then_inc(sem("head_step"), 1)
                        dve.wait_ge(sem("head_step"), G * LINKS_HEAD + at[0])
                    else:
                        ins.then_inc(sem(name), 1)
                        dve.wait_ge(sem(name), G + (2 if name == "sides_done" else 1))

                def link(ins):
                    e(ins)
                    dve.sem_inc(sem("link_done"), 1)

                def topk(src, rest, v8, i8):
                    dve.sem_inc(sem("link_done"), 1)
                    link(dve.max(v8[:, 0:8], src))
                    dve.max_index(i8[:, 0:8], v8[:, 0:8], src)
                    link(dve.match_replace(rest, v8[:, 0:8], src, LOWEST))
                    link(dve.max(v8[:, 8:16], rest))
                    e(dve.max_index(i8[:, 8:16], v8[:, 8:16], rest))

                def side(k):
                    topk(sco[0:n, k * NK:(k + 1) * NK], cand[0:n, 0:NK], vals[0:n, k * TOPK:(k + 1) * TOPK], idx[0:n, k * TOPK:(k + 1) * TOPK])

                def part0():
                    if last and nxt is not None:
                        norm(x_tok[:, units[nxt][1], :], hbuf[:, nxt % 3, :], mod_smp if units[nxt][1] == NT else mod_ffn, tokens(units[nxt][1]))
                    dve.wait_ge(sem("sco_ready"), G + 1)
                    side(0)

                def part1():
                    side(1)
                    e(dve.tensor_copy(idxf[0:n, :], idx[0:n, :]), "sides_done")

                def part2():
                    e(tt(cand[0:n, :].rearrange("p (i j) -> p i j", i=TOPK), vals[0:n, 0:TOPK].unsqueeze(2).to_broadcast([n, TOPK, TOPK]),
                         vals[0:n, TOPK:2 * TOPK].unsqueeze(1).to_broadcast([n, TOPK, TOPK]), ALU.add))
                    topk(cand[0:n, :], hits[0:n, :], best[0:n, :], flat[0:n, :])
                    e(ts(soft_n[0:n, 0:1], best[0:n, 0:1], -1.0, None, ALU.mult), "best_ready")

                def part3():
                    for k, (amount, op) in enumerate(((4, ALU.logical_shift_right), (TOPK - 1, ALU.bitwise_and))):
                        e(ts(place[0:n, k * TOPK:(k + 1) * TOPK].bitcast(U32), flat[0:n, :], amount, None, op))
                    e(dve.tensor_copy(place[0:n, 2 * TOPK:4 * TOPK], place[0:n, 0:2 * TOPK].bitcast(U32)))
                    hot = hits[0:n, :].rearrange("p (m k) -> p m k", m=TOPK)
                    for k in range(2):
                        e(tt(hot, place[0:n, (2 + k) * TOPK:(3 + k) * TOPK].unsqueeze(2).to_broadcast([n, TOPK, TOPK]),
                             iota[0:n, :].unsqueeze(1).to_broadcast([n, TOPK, TOPK]), ALU.is_equal))
                        e(tt(hot, hot, idxf[0:n, k * TOPK:(k + 1) * TOPK].unsqueeze(1).to_broadcast([n, TOPK, TOPK]), ALU.mult))
                        e(dve.tensor_reduce(e_side[0:n, k * TOPK:(k + 1) * TOPK], hot, AX_X, ALU.add))
                    e(ts(e_side[0:n, 0:TOPK], e_side[0:n, 0:TOPK], float(NK), float(l * NK * NK), ALU.mult, ALU.add))
                    dst = expert[v % 2] if t == NT else expert[v % 2].bitcast(U32)
                    e(tt(dst[0:n, bass.ds(h * TOPK, TOPK)], e_side[0:n, 0:TOPK], e_side[0:n, TOPK:2 * TOPK], ALU.add))
                    dve.wait_ge(sem("soft_ready"), G + 1)
                    e(dve.reciprocal(soft_n[0:n, 2:3], soft_n[0:n, 1:2]))
                    e(ts(gate[v % 2][0:n, bass.ds(h * TOPK, TOPK)], soft[0:n, :], soft_n[0:n, 2:3], None, ALU.mult))
                    assert at[0] == LINKS_HEAD, at[0]

                return part0, part1, part2, part3

            def expert_turn(u, k):
                t = units[u][1]
                hb = hbuf[:, u % 3, :] if t < NT else hbuf[:, (u + 1) % 3, :]
                g_all = gate[u % 2] if t < NT else g_lane
                for j in range(GRP):
                    dve.wait_ge(sem(f"u_in{j}"), k * 16 + (before[u] + 1) * 16)
                    if j == 0:
                        dve.wait_ge(sem("acts_set"), k + (before[u] + 1))
                    dve.tensor_tensor_reduce(ring[:, j, :], ring[:, j, :], hb, 1.0, 0.0, ALU.mult, ALU.add, dots[:, j:j + 1])\
                        .then_inc(sem("u_used"), 1)
                dve.wait_ge(sem("u_used"), k * GRP + (before[u] * GRP + FREE + GRP))
                dve.sem_inc(sem("dots_set"), 1)
                dve.wait_ge(sem("acts_set"), k + (before[u] + 2))
                dve.wait_ge(sem("diag_set"), k * GRP + (before[u] * GRP + GRP))
                tt(wts[:, :], acts[:, :], g_all[:, bass.ds(k * GRP, GRP)], ALU.mult).then_inc(sem("wts_set"), 1)

            def route(v, u, nxt):
                def head(h, last):
                    for k, part in enumerate(rank(v, h, last, nxt)):
                        if u is not None:
                            expert_turn(u, h * 4 + k)
                        part()

                with dve.Fori(0, PH - 1) as h:
                    head(h, False)
                head(PH - 1, True)
                if units[v][1] < NT:
                    dve.sem_inc(sem("expert_set"), 1)
                else:
                    dve.sem_inc(sem("route_done"), 1)

            dve.sem_inc(sem("u_used"), FREE)
            dve.sem_inc(sem("acts_set"), 1)
            dve.sem_inc(sem("diag_set"), GRP)
            dve.sem_inc(sem("sides_done"), 1)
            for u, (l, t) in enumerate(units):
                if t == 0:
                    if l:
                        w.next("pool_in", 16, 3)
                        set_mods(mod_mix, P)
                        d(tt(mod_mix[:, 2, :], mod_mix[:, 2, :], pool_gain, ALU.mult))
                        for k in range(NT):
                            norm(x_tok[:, k, :], hbuf[:, k % 2, :], mod_mix, P)
                            w.next("mix_ps")
                            add_mixed(k, mod_mix[:, 2, :])
                        set_mods(mod_mix, NS)
                        d(tt(mod_mix[0:NS, 2, :], mod_mix[0:NS, 2, :], pool_gain[0:NS], ALU.mult))
                        norm(x_tok[:, NT, :], hbuf[:, NT % 2, :], mod_mix, NS)
                        w.next("mix_ps")
                        add_mixed(NT, mod_mix[:, 2, :])
                    set_mods(mod_ffn, P, gain)
                    if l:
                        w.next("hbuf_free")
                    norm(x_tok[:, t, :], hbuf[:, u % 3, :], mod_ffn, P)
                    set_mods(mod_smp, NS, gain, ("smp_mods_in", 16, 3))
                    route(u, None, u + 1)
                if t < NT:
                    route(u + 1, u, u + 2 if t + 2 <= NT else None)
                else:
                    w.next("lane_ps")
                    pick = lane_pick[:, :].rearrange("p (a h k) -> p a h k", a=2, h=PH)
                    d(tt(pick, pb[2][:, 0:2 * KK].rearrange("p (a h k) -> p a h k", a=2, h=PH), lane.unsqueeze(1).unsqueeze(1).to_broadcast([P, 2, PH, TOPK]), ALU.mult))
                    d(dve.tensor_reduce(g_lane[:, :], pick[:, 1], AX_X, ALU.add))
                    d(dve.tensor_reduce(e_pick[:, :], pick[:, 0], AX_X, ALU.add))
                    d(ts(e_lane[:, :], e_pick[:, :], 1.0, None, ALU.mult), "expert_set")
                    w.next("lane_hidden")
                    with dve.Fori(0, SSTEPS) as r:
                        expert_turn(u, r)
                w.next("y_ps")
                add_mixed(t, (mod_smp if t == NT else mod_ffn)[:, 2, :], "x_routed", ybank(u), mixed)


_INS = ["x_prompt", "x_sample", "cache_mla", "state_pool", "page_table", "norm_mix", "norm_ffn", "w_ada", "b_ada", "w_mla_in",
        "g_q_lat", "g_kv_lat", "w_uq", "w_uk", "w_uv", "g_qn_nope", "g_qn_rope", "g_kn_nope", "g_kn_rope", "w_mla_out",
        "w_pool", "pool_scale", "w_peer_q", "peer_u", "peer_v"]
_OUTS = [("y_p", (1, SEQ, D)), ("y_s", (NS, 1, D)), ("rows_p", (1, 1, SEQ, ROW)), ("rows_s", (1, NS, 1, ROW)),
         ("pst_p", (1, 1, STATE, D)), ("pst_s", (1, NS, STATE, D))]


def kernel(**inputs):
    import concourse.bacc as bacc
    from concourse.bass_utils import run_bass_kernel_spmd

    nc = bacc.Bacc("TRN2", target_bir_lowering=False, num_devices=1)
    host = {name: np.ascontiguousarray(inputs[name]) for name in _INS}
    host["cT"] = np.ascontiguousarray(np.concatenate([inputs["c_sample"], inputs["c_prompt"]], axis=0).T)
    host["w_ukT"] = np.ascontiguousarray(np.transpose(inputs["w_uk"][0], (2, 1, 0)))
    keys = np.transpose(inputs["peer_subkeys"], (0, 4, 1, 2, 3))
    host["subkeysT"] = np.ascontiguousarray(keys.reshape(DEPTH, PEER_HALF, NQ, NK))
    host.update(shape_constants())
    arrays, T, O = {}, {}, {}
    for name, a in host.items():
        arrays["in_" + name] = a
        T[name] = nc.dram_tensor("in_" + name, a.shape, mybir.dt.from_np(a.dtype), kind="ExternalInput").ap()
    for name, shape in _OUTS:
        O[name] = nc.dram_tensor("out_" + name, shape, F32, kind="ExternalOutput").ap()
    decoder_step(nc, T, O)
    r = run_bass_kernel_spmd(nc, [arrays], core_ids=[0])
    return tuple(r.results[0]["out_" + name] for name, _ in _OUTS)
```

```python
from contextlib import ExitStack

import numpy as np

import concourse.bass as bass
from concourse import mybir

F32 = mybir.dt.float32
U32 = mybir.dt.uint32
I32 = mybir.dt.int32
ALU = mybir.AluOpType
ACT = mybir.ActivationFunctionType
AX_X = mybir.AxisListType.X

P = 128
D = 1024
DC = D // P
SEQ = 512
NT = SEQ // P
NS = 8
NC = NS + 1
PAST = 2048
PAGE = 128
NPG = PAST // PAGE
DEPTH = 2
EPS = 1e-6
NH = 8
NOPE, ROPE, VD = 128, 64, 128
QH = NOPE + ROPE
QL, KL = 384, 256
QLC, KLC = QL // P, KL // P
ROW = KL + ROPE
ZW = QL + KL + ROPE
SCALE = float(QH) ** -0.5
WINDOWS = (2, 4, 8, 16)
GD = D // 4
STATE = 15
PH = 8
NK = 128
TOPK = 16
PEER_HALF = 128
NQ = PH * 2
KK = PH * TOPK
NEG = -1.0e30
LOWEST = -3.0e38
GRP = 4
ADA = 6 * D


def shape_constants():
    inv = (10000.0 ** (-np.arange(0, ROPE, 2) / ROPE)).astype(np.float32)
    pos = np.concatenate([np.arange(SEQ), np.full(NS, PAST)]).astype(np.float32)
    ang = (pos[:, None] * inv[None, :]).astype(np.float32)
    cos, sin = np.cos(ang).astype(np.float32), np.sin(ang).astype(np.float32)
    rot = np.zeros((P, NT + 1, 2, ROPE), np.float32)
    for t in range(NT + 1):
        n = P if t < NT else NS
        rot[:n, t, 0] = np.tile(cos[t * P:t * P + n], 2)
        rot[:n, t, 1] = np.tile(sin[t * P:t * P + n], 2)
    i = np.arange(P)
    small = np.concatenate([
        np.eye(P), np.where(i[None, :] <= i[:, None], 0.0, NEG),
        (i[None, :] // TOPK == i[:, None]), (i[:, None] // TOPK == np.arange(NS)[None, :]),
        (i[:, None] % TOPK == np.arange(TOPK)[None, :]), np.tile(np.arange(TOPK), (P, 1)),
    ], axis=1).astype(np.float32)
    band = np.zeros((P, 4, 4, P), np.float32)
    for g, w in enumerate(WINDOWS):
        near = (i[:, None] <= i[None, :]) & (i[:, None] > i[None, :] - w)
        band[:, 0, g] = near / np.minimum(i + 1, w)[None, :] - np.eye(P)
        band[:, 1, g] = near / w - np.eye(P)
        band[:, 2, g] = (i[:, None] - P > i[None, :] - w) / w
        r = np.arange(NS * STATE)
        band[:NS * STATE, 3, g, :NS] = ((r[:, None] // STATE == np.arange(NS)) & (r[:, None] % STATE >= STATE - (w - 1))) / w
        band[:NS, 3, g, NS:2 * NS] = np.eye(NS) * (1.0 / w - 1.0)
    return {"rot": rot.reshape(P, -1), "small": small, "band": band.reshape(P, -1)}


def decoder_step(nc, T, O):
    ctx = ExitStack()
    with ctx:
        def sb(name, shape, dt=F32):
            return ctx.enter_context(nc.sbuf_tensor(name, shape, dt))

        sems = {}

        def sem(name):
            if name not in sems:
                sems[name] = ctx.enter_context(nc.semaphore(name))
            return sems[name]

        ada_rows = nc.dram_tensor("ada_rows", (DEPTH, NC, ADA), F32, kind="Internal").ap()

        W = 11904
        x_tok = sb("x_tok", [P, NT + 1, D])
        big = sb("big", [P, 16384])
        ring = sb("ring", [P, 8, D])
        mod_mix = sb("mod_mix", [P, 3, D])
        mod_smp = sb("mod_smp", [P, 3, D])
        hT = sb("hT", [P, DC * P])
        hbuf = sb("hbuf", [P, 3, D])
        work = sb("work", [P, W])
        small = sb("small", [P, 3 * P + NS + 2 * TOPK])
        tiny = sb("tiny", [P, 64])
        newton = sb("newton", [P, 48])
        ones = sb("ones", [P, P])
        ident = small[:, 0:P]
        causal = small[:, P:2 * P]
        sel = small[:, 2 * P:3 * P]
        selT = small[:, 3 * P:3 * P + NS]
        lane = small[:, 3 * P + NS:3 * P + NS + TOPK]
        iota = small[:, 3 * P + NS + TOPK:3 * P + NS + 2 * TOPK]

        pos = [0]

        def region(base, size, total):
            o = pos[0]
            pos[0] += size
            assert pos[0] <= total, (pos[0], total)
            return base[:, o:o + size]

        w_in = region(big, DC * ZW, 16384).rearrange("p (c n) -> p c n", c=DC)
        w_uq = region(big, QLC * NH * QH, 16384).rearrange("p (c n) -> p c n", c=QLC)
        w_uk_at = pos[0]
        w_uk = region(big, KLC * NH * NOPE, 16384).rearrange("p (c n) -> p c n", c=KLC)
        w_uv = region(big, KLC * NH * VD, 16384).rearrange("p (c n) -> p c n", c=KLC)
        w_ukT_at = pos[0]
        w_ukT = region(big, NH * KL, 16384).rearrange("p (h n) -> p h n", h=NH)
        w_q = big[:, :].rearrange("p (c n) -> p c n", c=DC)
        w_ada = big[:, :].rearrange("p (s c n) -> p s c n", s=4, c=DC)
        w_out = ring[:, :, :]
        pos[0] = 0
        knT = region(work, NH * SEQ, W).rearrange("p (h n) -> p h n", h=NH)
        krT = region(work, SEQ, W)
        rows = region(work, (NT + 1) * ROW, W).rearrange("p (t n) -> p t n", t=NT + 1)
        latT = region(work, KLC * P, W).rearrange("p (c n) -> p c n", c=KLC)
        cqT = region(work, QLC * P, W).rearrange("p (c n) -> p c n", c=QLC)
        pT_odd = region(work, ZW, W)
        qs = region(work, NH * QH, W)
        qnT = region(work, NH * P, W)
        qrT = region(work, NH * P, W)
        pT = [region(work, SEQ, W), pT_odd[:, 0:SEQ]]
        ctxT = [region(work, KLC * P, W), cqT[:, 0:KLC, :].rearrange("p c n -> p (c n)")]
        rot = sb("rot", [P, 2, ROPE])
        spare = mod_smp[:, :, :].rearrange("p m n -> p (m n)")
        gain_all = spare[:, 0:ZW + QH + NOPE]
        sq = spare[:, ZW + QH + NOPE:ZW + QH + NOPE + NH * QH]
        ks = hbuf[:, 1, :]
        z = hbuf[:, 0, 0:ZW]
        oT = hbuf[:, 2, :]
        probs = hT[:, :].rearrange("p (b n) -> p b n", b=2)

        pos[0] = 0
        cached = region(work, 2 * (NPG + 1) * ROW, W).rearrange("p (b g n) -> p b g n", b=2, g=NPG + 1)
        after_mix = mod_mix[:, :, :].rearrange("p m n -> p (m n)")
        pos[0] = 0
        cachedT = region(after_mix, 2 * 3 * P, 3 * D).rearrange("p (b n) -> p b n", b=2)
        kss = region(after_mix, NPG * NH, 3 * D)
        krn = region(after_mix, NPG * NH, 3 * D)
        krt = region(after_mix, NPG * NH, 3 * D)
        sc_s = region(after_mix, (NPG + 1) * NH, 3 * D).rearrange("p (g h) -> p g h", g=NPG + 1)
        ps_s = region(after_mix, (NPG + 1) * NH, 3 * D).rearrange("p (g h) -> p g h", g=NPG + 1)
        ctx_s = region(after_mix, KLC * NH * NS, 3 * D).rearrange("p (c h s) -> p c h s", c=KLC, h=NH)
        oT_s = region(after_mix, NH * NS, 3 * D)
        ctx_n = region(after_mix, KL, 3 * D)
        ksq = hbuf[:, 0:2, :]
        PGRP = 4
        keep = sb("keep", [P, 256])
        own_dram = nc.dram_tensor("own_scores", (NS, NH), F32, kind="Internal").ap()
        zero = causal
        cact = hbuf[:, 2, 0:DC * NC].rearrange("p (c n) -> p c n", c=DC)

        ada_stage = work[0:NC, W - D:W].rearrange("p (b n) -> p b n", b=2)

        def ada_bias(l):
            return work[0:NC, 0:ADA] if l == 0 else ring[0:NC, 0:6, :].rearrange("p a n -> p (a n)")
        q_abs = keep[:, 0:128].rearrange("p (c m) -> p c m", c=KLC)
        q_rot = keep[0:ROPE, 128:192]
        s_own = keep[0:1, 192:256]
        pages = sb("pages", [1, NS * NPG], mybir.dt.int32)

        pos[0] = 0
        mod_ffn = region(work, 3 * D, W).rearrange("p (m n) -> p m n", m=3)
        keysT = region(work, NQ * NK, W)
        shared = region(work, 5 * 2 * NK + 2 * D, W)
        q_tok, qT, sco, cand, hits = (shared[:, i * 2 * NK:(i + 1) * 2 * NK] for i in range(5))
        gain, mixed = shared[:, 10 * NK:10 * NK + D], shared[:, 10 * NK + D:10 * NK + 2 * D]
        vals = region(work, 2 * TOPK, W)
        idx = region(work, 2 * TOPK, W).bitcast(U32)
        idxf = region(work, 2 * TOPK, W)
        best = region(work, TOPK, W)
        flat = region(work, TOPK, W).bitcast(U32)
        place = region(work, 4 * TOPK, W)
        e_side = region(work, 2 * TOPK, W)
        soft = region(work, TOPK, W)
        soft_n = region(work, 4, W)
        expert = [region(work, KK, W) for _ in range(2)]
        gate = [region(work, KK, W) for _ in range(2)]
        turn = region(work, 2 * GRP, W).bitcast(U32).rearrange("p (b j) -> p b j", b=2)
        dots = region(work, GRP, W)
        acts = region(work, GRP, W)
        wts = region(work, GRP, W)
        diag = region(work, GRP * P, W).rearrange("p (j n) -> p j n", j=GRP)
        e_lane = region(work, PH, W).bitcast(U32)
        g_lane = region(work, PH, W)
        e_pick = region(work, PH, W)
        lane_pick = cand
        w_pool = region(work, DC * GD, W).rearrange("p (c n) -> p c n", c=DC)
        dT = [shared[:, 0:D], mixed]
        late_chunks = (DC - 2, DC - 1)
        band = w_q[:, DC - 1, :]
        pool_gain, pool_gain_s, state = mixed, w_q[:, DC - 2, D:2 * D], w_q[:, DC - 2, 0:D]

        pb = [ctx.enter_context(nc.psum_tensor(f"bank{i}", [P, 512], F32)) for i in range(8)]

        units = [(l, t) for l in range(DEPTH) for t in range(NT + 1)]
        tokens = lambda t: P if t < NT else NS
        STEPS = KK // GRP
        SSTEPS = PH // GRP
        before = [0]
        for _, t in units:
            before.append(before[-1] + (STEPS if t < NT else SSTEPS))
        LINKS_HEAD = 26
        FREE = 2 * GRP
        ybank = lambda u: pb[4 + u % 2 * 2:6 + u % 2 * 2]

        def first_head(v, h):
            return h + v * PH

        def turns_of(v, u, h):
            if units[u][1]:
                return [h * 4 + k for k in range(4)]
            start = h * 2 - 2 if v == u else h * 2 + STEPS // 2
            return [start, None, start + 1, None]

        mla_order = [NT] + list(range(NT))

        class Turns:

            def __init__(self, eng, own):
                self.eng, self.own, self.n, self.given = eng, own, {}, {}

            def next(self, name, unit=1, times=1):
                self.n[name] = self.n.get(name, 0) + unit * times
                self.eng.wait_ge(sem(name), self.n[name])

            def done(self, ins, name=None):
                name = name or self.own
                self.given[name] = self.given.get(name, 0) + 1
                ins.then_inc(sem(name), 1)
                self.eng.wait_ge(sem(name), self.given[name])

        for name in ("x_in", "consts_in", "c_in", "b_in", "table_in", "mix_w_in0", "mix_w_in1", "mix_w_in2", "mix_w_in3", "mix_w_in4", "out_w_in", "gains_in", "rot_in",
                     "mods_in", "keys_in", "query_w_in", "pool_in", "state_in", "rows_out", "own_out", "own_in",
                     "y_out", "state_out", "dve_step", "act_step", "idx_read", "slot_turn", "pool_w_in", "gain_s_in", "pool_gain_in", "smp_mods_in", "link_done", "wait_done", "head_step", "smp_step"):
            sem(name)
        block = ctx.enter_context(nc.Block())

        @block.sync
        def _(sp):
            w = Turns(sp, "sp")

            def ld(dst, src, name):
                sp.dma_start(dst, src).then_inc(sem(name), 16)

            ld(small[:, :], T["small"], "consts_in")
            ld(hbuf[:, 0, 0:DC * NC].rearrange("p (c n) -> p c n", c=DC), T["cT"].rearrange("(c p) n -> p c n", p=P), "c_in")
            ld(pages[:, :], T["page_table"].rearrange("(a s) g -> a (s g)", a=1), "table_in")
            for l in range(DEPTH):
                ld(ada_bias(l),
                   T["b_ada"][l].partition_broadcast(NC), "b_in")
            def mods(dst, l, first, who, n, norm, gain_=hT):
                for m, k in ((0, 1), (1, 0), (2, 2)):
                    cols = slice((first + k) * D, (first + k + 1) * D)
                    src = ada_rows[l, NC - 1, cols].partition_broadcast(n) if who == "prompt" else ada_rows[l, 0:NS, cols]
                    ld(dst[0:n, m, :], src, "mods_in")
                ld(gain_[0:n, :], norm.partition_broadcast(n), "mods_in")

            def sample_mods(l, first):
                for m, k in ((0, 1), (1, 0), (2, 2)):
                    ld(mod_smp[0:NS, m, :], ada_rows[l, 0:NS, (first + k) * D:(first + k + 1) * D], "smp_mods_in")

            def store_ada(i):
                l, j = divmod(i, ADA // 512)
                ld(ada_rows[l, :, j * 512:(j + 1) * 512], ada_stage[:, i % 2, :], f"ada_out{i % 2}")

            for l in range(DEPTH):
                for j in range(ADA // 512):
                    i = l * (ADA // 512) + j
                    if i >= 4:
                        sp.wait_ge(sem("ada_ps"), i - 3)
                    ld(w_ada[:, i % 4], T["w_ada"][l].rearrange("(c p) n -> p c n", p=P)[:, :, j * 512:(j + 1) * 512],
                       f"ada_w_in{i % 4}")
                    if i == 3:
                        for t in range(NT):
                            ld(x_tok[:, t, :], T["x_prompt"][0, t * P:(t + 1) * P, :], "x_in")
                        ld(x_tok[0:NS, NT, :], T["x_sample"].rearrange("b s d -> (b s) d"), "x_in")
                    if i >= 2:
                        sp.wait_ge(sem("ada_row"), i - 1)
                        store_ada(i - 2)
                    if i == ADA // 512 + 6:
                        for k in range(2):
                            sp.wait_ge(sem(f"ada_out{k}"), 16 * (ADA // 512 // 2))
                        mods(mod_mix, 0, 0, "prompt", P, T["norm_mix"][0])
                        sample_mods(0, 0)
            blocks = 2 * ADA // 512
            for n_, (dst, src, size) in enumerate(((w_in, T["w_mla_in"][0], DC * ZW), (w_uq, T["w_uq"][0], QLC * NH * QH),
                                                   (w_uk, T["w_uk"][0].rearrange("c h d -> c (h d)"), KLC * NH * NOPE),
                                                   (w_uv, T["w_uv"][0].rearrange("c h d -> c (h d)"), KLC * NH * VD))):
                end = (DC * ZW, w_uk_at, w_uk_at + KLC * NH * NOPE, w_ukT_at)[n_]
                sp.wait_ge(sem("ada_ps"), blocks - 4 + -(-end // (DC * 512)))
                ld(dst, src.rearrange("(c p) n -> p c n", p=P), f"mix_w_in{n_}")
                if n_ == 0:
                    sp.wait_ge(sem("ada_row"), blocks - 1)
                    store_ada(blocks - 2)
            ld(w_ukT, T["w_ukT"], "mix_w_in4")
            sp.wait_ge(sem("ada_row"), blocks)
            store_ada(blocks - 1)
            ld(w_out, T["w_mla_out"][0].rearrange("(c p) n -> p c n", p=P), "out_w_in")
            w.next("smp_mods_set")
            w.next("mods_set")
            w.next("h_ready")
            o = 0
            for a, size in (("g_q_lat", QL), ("g_kv_lat", KL), ("g_kn_rope", ROPE), ("g_qn_nope", NOPE), ("g_qn_rope", ROPE), ("g_kn_nope", NOPE)):
                ld(gain_all[:, o:o + size], T[a][0].partition_broadcast(P), "gains_in")
                o += size
            for j in range(2):
                sp.wait_ge(sem(f"ada_out{j}"), 16 * (ADA // 512))
            for n_, t in enumerate(mla_order):
                if n_:
                    w.next("qk_norm")
                ld(rot[:, :, :], T["rot"].rearrange("p (t a b) -> p t a b", t=NT + 1, a=2)[:, t], "rot_in")
                w.next("row_ready")
                n = tokens(t)
                if t < NT:
                    ld(O["rows_p"][0, 0, t * P:(t + 1) * P, :], rows[:, t, :], "rows_out")
                else:
                    ld(O["rows_s"].rearrange("l b s n -> (l b s) n"), rows[0:NS, NT, :], "rows_out")
                    w.next("own_ready")
                    ld(own_dram, tiny[0:NS, 40:48], "own_out")
            w.next("qk_norm")
            for t in range(NT):
                w.next("x_mixed")
            sp.wait_ge(sem("rows_out"), 16 * (NT + 1))
            sp.wait_ge(sem("own_out"), 16)
            ld(s_own, own_dram.rearrange("(a s) h -> a (s h)", a=1), "own_in")
            w.next("smp_clear")
            ld(mod_smp[0:NS, 2, :], ada_rows[0, 0:NS, 2 * D:3 * D], "mods_in")
            w.next("table_in", 16)

            def load_pages(r, b):
                for g in range(NPG):
                    page = sp.value_load(pages[0:1, bass.ds(r * NPG + g, 1)], min_val=0, max_val=T["cache_mla"].shape[1] - 1)
                    ld(cached[:, b, g, :], T["cache_mla"][0, bass.ds(page, 1)].rearrange("a p n -> (a p) n"), f"page_in{g // PGRP}_{b}")
                ld(cached[0:1, b, NPG, 0:KL], O["rows_s"][0, bass.ds(r, 1), 0, 0:KL], f"page_in{NPG // PGRP}_{b}")

            def query_weights(l, chunks):
                for c in chunks:
                    ld(w_q[:, c, :], T["w_peer_q"][l, c * P:(c + 1) * P, :], "query_w_in")

            load_pages(0, 0)
            load_pages(1, 1)
            free_chunks = [c for c in range(DC) if (c + 1) * PH * 2 * NK <= w_uk_at or c * PH * 2 * NK >= w_ukT_at]
            query_weights(0, free_chunks)
            with sp.Fori(0, NS // 2 - 1) as r:
                for b in range(2):
                    sp.wait_ge(sem("ctx_ps"), r * 2 + (b + 1))
                    load_pages(r * 2 + (2 + b), b)
            sp.wait_ge(sem("ctx_ps"), NS)
            for l in range(DEPTH):
                if l:
                    w.next("mods_set")
                    w.next("route_done")
                    ld(keysT, T["subkeysT"][l], "keys_in")
                    ld(band.rearrange("p (k n) -> p k n", k=16), T["band"].rearrange("p (k n) -> p k n", k=16), "pool_in")
                    ld(pool_gain_s[0:NS], T["pool_scale"][0].partition_broadcast(NS), "gain_s_in")
                    ld(state[0:NS * STATE], T["state_pool"].rearrange("l b r d -> (l b r) d"), "state_in")
                    query_weights(l, [c for c in range(DC) if c not in late_chunks])
                    ld(O["pst_s"][0, :, 0:STATE - 1, :], T["state_pool"][0, :, 1:STATE, :], "state_out")
                    for t in range(NT):
                        w.next("x_mixed")
                    ld(O["pst_p"][0, 0], hbuf[P - STATE:P, (NT - 1) % 3, :], "state_out")
                    w.next("x_routed")
                    sample_mods(l, 0)
                    w.next("smp_mods_set")
                    mods(mod_ffn, l, 3, "prompt", P, T["norm_ffn"][l], gain)
                    w.next("x_mixed")
                    query_weights(l, late_chunks)
                    ld(O["pst_s"][0, :, STATE - 1, :], hbuf[0:NS, NT % 3, :], "state_out")
                else:
                    mods(mod_ffn, l, 3, "prompt", P, T["norm_ffn"][l], gain)
                    ld(keysT, T["subkeysT"][l], "keys_in")
                    w.next("x_mixed")
                    query_weights(l, [c for c in range(DC) if c not in free_chunks])
                sample_mods(l, 3)
                w.next("mods_set")
                if l:
                    sp.wait_ge(sem("state_out"), 48)
                    sp.sem_inc(sem("hbuf_free"), 1)
                else:
                    w.next("smp_mods_set")
                    ld(w_pool, T["w_pool"][0].rearrange("g (a p) n -> p (g a) n", p=P), "pool_w_in")
                    mods(mod_mix, 1, 0, "prompt", P, T["norm_mix"][1], gain)
                    ld(pool_gain, T["pool_scale"][0].partition_broadcast(P), "pool_gain_in")
                for t in range(1, NT + 1):
                    w.next("x_routed")
                    if l:
                        ld(O["y_p"][0, (t - 1) * P:t * P, :], x_tok[:, t - 1, :], "y_out")
            w.next("x_routed")
            ld(O["y_s"].rearrange("b s d -> (b s) d"), x_tok[0:NS, NT, :], "y_out")
            sp.wait_ge(sem("y_out"), 16 * (NT + 1))

        @block.tensor
        def _(pe):
            w = Turns(pe, "pe")
            mm = pe.matmul

            w.next("consts_in", 16)
            w.next("c_act")
            for i in range(2 * ADA // 512):
                w.next(f"ada_w_in{i % 4}", 16)
                if i >= 2:
                    pe.wait_ge(sem("ada_row"), i - 1)
                for c in range(DC):
                    last = mm(pb[i % 2][0:NC, :], cact[:, c, :], w_ada[:, i % 4, c, :], start=(c == 0), stop=(c == DC - 1))
                last.then_inc(sem("ada_ps"), 1)

            def transpose_h(t, hb):
                n = tokens(t)
                w.next("h_ready")
                for c in range(DC):
                    k = c if n == NS else c % 4
                    last = pe.transpose(pb[4 + (c // 4 if n == P else 0)][:, k * n:k * n + n], hb[0:n, c * P:(c + 1) * P],
                                        ident[0:n, 0:n])
                last.then_inc(sem("hT_ps"), 1)

            def latents(i):
                t = mla_order[i]
                n = tokens(t)
                transpose_h(t, hbuf[:, 0, :])
                w.next("hT_ready")
                if i == 0:
                    w.next("mix_w_in0", 16)
                for half in range(2):
                    for c in range(DC):
                        last = mm(pb[half][0:n, 0:ZW // 2], hT[:, c * n:(c + 1) * n], w_in[:, c, half * ZW // 2:(half + 1) * ZW // 2],
                                  start=(c == 0), stop=(c == DC - 1))
                last.then_inc(sem("z_ps"), 1)
                w.next("z_ready")

            latents(0)
            for i, t in enumerate(mla_order):
                n = tokens(t)
                w.next("row_ready")
                for c in range(QLC):
                    pe.transpose(pb[6][:, c * n:(c + 1) * n], z[0:n, c * P:(c + 1) * P], ident[0:n, 0:n])
                for c in range(KLC):
                    pe.transpose(pb[7][:, c * n:(c + 1) * n], rows[0:n, t, c * P:(c + 1) * P], ident[0:n, 0:n])
                pe.transpose(pb[7][0:ROPE, KLC * n:KLC * n + n], rows[0:n, t, KL:ROW], ident[0:n, 0:n])\
                    .then_inc(sem("zT_ps"), 1)
                w.next("zT_ready")
                if i == 0:
                    for k in range(1, 5):
                        w.next(f"mix_w_in{k}", 16)
                for b in range(3):
                    for c in range(QLC):
                        mm(pb[2 + b][0:n, :], cqT[:, c, 0:n], w_uq[:, c, b * 512:(b + 1) * 512], start=(c == 0), stop=(c == QLC - 1))
                for b in range(2):
                    for c in range(KLC):
                        last = mm(pb[b][0:n, :], latT[:, c, 0:n], w_uk[:, c, b * 512:(b + 1) * 512], start=(c == 0), stop=(c == KLC - 1))
                last.then_inc(sem("qk_ps"), 1)
                if i < NT:
                    latents(i + 1)
                w.next("qk_norm")
                q3 = qs[0:n, :].rearrange("p (h d) -> p h d", h=NH)
                if t < NT:
                    for h in range(NH):
                        pe.transpose(pb[6 + h // 4][:, h % 4 * P:(h % 4 + 1) * P], q3[:, h, 0:NOPE], ident)
                        pe.transpose(pb[h // 4][0:ROPE, h % 4 * P:(h % 4 + 1) * P], q3[:, h, NOPE:QH], ident)
                        last = pe.transpose(pb[2 + h // 4][:, h % 4 * P:(h % 4 + 1) * P], ks[:, h * NOPE:(h + 1) * NOPE], ident)
                    last.then_inc(sem("qkT_ps"), 1)
                    w.next("qkT_ready")
                    keys = (t + 1) * P

                    def scores(h):
                        mm(pb[h % 2][:, 0:keys], qnT[:, h * P:(h + 1) * P], knT[:, h, 0:keys], start=True, stop=False)
                        mm(pb[h % 2][:, 0:keys], qrT[0:ROPE, h * P:(h + 1) * P], krT[0:ROPE, 0:keys], start=False, stop=True)\
                            .then_inc(sem("s_ps"), 1)

                    def probs_T(h):
                        w.next("p_norm")
                        for k in range(t + 1):
                            last = pe.transpose(pb[2 + h % 2 * 4][:, k * P:(k + 1) * P], probs[:, h % 2, k * P:(k + 1) * P], ident)
                        last.then_inc(sem("pT_ps"), 1)

                    def context_T(h):
                        w.next("pT_ready")
                        for c in range(KLC):
                            for k in range(t + 1):
                                last = mm(pb[3 + h % 2 * 4][:, c * P:(c + 1) * P], rows[:, k, c * P:(c + 1) * P], pT[h % 2][:, k * P:(k + 1) * P],
                                          start=(k == 0), stop=(k == t))
                        last.then_inc(sem("cT_ps"), 1)

                    def head_out(h):
                        w.next("cT_ready")
                        for c in range(KLC):
                            last = mm(pb[4 + h // 4][:, h % 4 * P:(h % 4 + 1) * P], w_uv[:, c, h * VD:(h + 1) * VD],
                                      ctxT[h % 2][:, c * P:(c + 1) * P], start=(c == 0), stop=(c == KLC - 1))
                        return last

                    scores(0)
                    for j in range(NH + 2):
                        for step, h in ((scores, j + 1), (probs_T, j), (context_T, j - 1), (head_out, j - 2)):
                            if 0 <= h < NH:
                                last = step(h)
                    last.then_inc(sem("o_ps"), 1)
                    w.next("o_ready")
                    if t == 0:
                        w.next("out_w_in", 16)
                    for b in range(2):
                        for h in range(NH):
                            last = mm(pb[6 + b][:, :], oT[:, h * P:(h + 1) * P], w_out[:, h, b * 512:(b + 1) * 512],
                                      start=(h == 0), stop=(h == NH - 1))
                    last.then_inc(sem("mix_ps"), 1)
                else:
                    for h in range(NH):
                        pe.transpose(pb[6][:, h * NS:(h + 1) * NS], q3[:, h, 0:NOPE], ident[0:n, 0:n])
                        last = pe.transpose(pb[7][0:ROPE, h * NS:(h + 1) * NS], q3[:, h, NOPE:QH], ident[0:n, 0:n])
                    last.then_inc(sem("qkT_ps"), 1)
                    w.next("qkT_ready")
                    for c in range(KLC):
                        for h in range(NH):
                            last = mm(pb[2][:, (c * NH + h) * NS:(c * NH + h + 1) * NS], w_ukT[:, h, c * P:(c + 1) * P],
                                      qnT[:, h * NS:(h + 1) * NS], start=True, stop=True)
                    last.then_inc(sem("qa_ps"), 1)

            w.next("smp_clear")
            w.next("ones_set")

            def turn_page(r, b, g):
                if g % PGRP == 0:
                    pe.wait_ge(sem(f"page_in{g // PGRP}_{b}"), (r - b) * (16 * PGRP // 2) + 16 * PGRP)
                for c in range(KLC):
                    pe.transpose(pb[6 + g % 2][:, c * P:(c + 1) * P], cached[:, b, g, c * P:(c + 1) * P], ident)
                pe.transpose(pb[6 + g % 2][0:ROPE, 2 * P:3 * P], cached[:, b, g, KL:ROW], ident).then_inc(sem("page_ps"), 1)

            def spread_max(r, b):
                pe.wait_ge(sem("s_max"), r + 1)
                pe.transpose(pb[4 + b][0:NH, 0:P], tiny[:, 0:NH], ident).then_inc(sem("max_ps"), 1)

            def spread_max2(r, b):
                pe.wait_ge(sem("max_diag"), r + 1)
                mm(pb[4 + b][:, P:P + NH], ones[0:NH, :], tiny[0:NH, 16:16 + NH], start=True, stop=True).then_inc(sem("maxb_ps"), 1)

            def context(r, b):
                pe.wait_ge(sem("p_sum"), r + 1)
                mm(pb[4 + b][0:NH, 144:145], tiny[:, 24:24 + NH], ones[:, 0:1], start=True, stop=True)
                pe.wait_ge(sem(f"page_in{NPG // PGRP}_{b}"), (r - b) * 8 + 16)
                for g in range(NPG + 1):
                    last = mm(pb[4 + b][0:NH, 160:160 + KL], ps_s[:, g, :], cached[:, b, g, 0:KL], start=(g == 0), stop=(g == NPG))
                last.then_inc(sem("ctx_ps"), 1)

            def context_cols(r, b):
                pe.wait_ge(sem("ctx_norm"), r + 1)
                pe.sem_inc(sem("wait_done"), 1)
                for c in range(KLC):
                    last = pe.transpose(pb[4 + b][:, 432 + c * NH:432 + (c + 1) * NH], ctx_n[0:NH, c * P:(c + 1) * P], ident[0:NH, 0:NH])
                last.then_inc(sem("ctx_cols"), 1)

            def sequence(r, b, last_one):
                for g in range(NPG):
                    if g + 1 < NPG:
                        turn_page(r, b, g + 1)
                    elif not last_one:
                        turn_page(r + 1, 1 - b, 0)
                    pe.wait_ge(sem("pageT"), r * NPG + (g + 1))
                    if g == 0 and not (isinstance(r, int) and r == 0):
                        pe.wait_ge(sem("ctx_ready"), r)
                    h = g % 2
                    at = g * 16
                    for c in range(KLC):
                        mm(pb[4 + b][:, at:at + 8], cachedT[:, h, c * P:(c + 1) * P], q_abs[:, c, bass.ds(r * NH, NH)],
                           start=(c == 0), stop=(c == KLC - 1), skip_group_check=True)
                    mm(pb[4 + b][:, at + 8:at + 16], cachedT[0:ROPE, h, 2 * P:3 * P], q_rot[:, bass.ds(r * NH, NH)],
                       start=True, stop=True, skip_group_check=True)
                    if not (isinstance(r, int) and r == 0 and g < 2):
                        pe.wait_ge(sem("k_squares"), r * NPG + (g - 1))
                    for half in range(2):
                        for c in range(KLC):
                            last = mm(pb[2 * h + half][:, :], cachedT[:, h, c * P:(c + 1) * P], w_uk[:, c, half * 512:(half + 1) * 512],
                                      start=(c == 0), stop=(c == KLC - 1))
                    last.then_inc(sem("kk_ps"), 1)
                    if g in tail_steps and not (isinstance(r, int) and r == 0):
                        tail_steps[g](r - 1, 1 - b)

            tail_steps = {3: spread_max, 5: spread_max2, 9: context, 12: context_cols}
            turn_page(0, 0, 0)
            sequence(0, 0, False)
            with pe.Fori(0, NS // 2 - 1) as i:
                sequence(i * 2 + 1, 1, False)
                sequence(i * 2 + 2, 0, False)
            sequence(NS - 1, 1, True)
            for step in tail_steps.values():
                step(NS - 1, 1)
            pe.wait_ge(sem("ctx_ready"), NS + 1)
            for h in range(NH):
                for c in range(KLC):
                    last = mm(pb[0][:, h * NS:(h + 1) * NS], w_uv[:, c, h * VD:(h + 1) * VD], ctx_s[:, c, h, :],
                              start=(c == 0), stop=(c == KLC - 1))
            last.then_inc(sem("o_ps"), 1)
            w.next("o_ready")
            for b in range(2):
                for h in range(NH):
                    last = mm(pb[6 + b][0:NS, :], oT_s[:, h * NS:(h + 1) * NS], w_out[:, h, b * 512:(b + 1) * 512],
                              start=(h == 0), stop=(h == NH - 1))
            last.then_inc(sem("mix_ps"), 1)

            def pool(t):
                n = tokens(t)
                w.next("h_ready")
                if t == 0:
                    w.next("pool_w_in", 16)
                    w.next("pool_in", 16)
                if t == NT:
                    w.next("state_in", 16)
                hb = hbuf[:, t % 3, :]
                bd = band.rearrange("p (k g n) -> p k g n", k=4, g=4)
                for c in range(DC):
                    out = pb[t % 2 * 2 + (c // 4 if n == P else 0)][:, (c % 4 if n == P else c) * n:(c % 4 if n == P else c) * n + n]
                    ch = slice(c * P, (c + 1) * P)
                    if t == NT:
                        mm(out, state[0:NS * STATE, ch], bd[0:NS * STATE, 3, c // 2, 0:NS], start=True, stop=False)
                        last = mm(out, hb[0:NS, ch], bd[0:NS, 3, c // 2, NS:2 * NS], start=False, stop=True)
                    else:
                        if t:
                            mm(out, hbuf[:, (t - 1) % 3, ch], bd[:, 2, c // 2, :], start=True, stop=False)
                        last = mm(out, hb[:, ch], bd[:, min(t, 1), c // 2, :], start=(t == 0), stop=True)
                last.then_inc(sem("dT_ps"), 1)

            def pool_map(t):
                n = tokens(t)
                w.next("dT_ready")
                for g in range(4):
                    for a in range(2):
                        c = 2 * g + a
                        last = mm(pb[4 + t % 2 * 2 + g // 2][0:n, g % 2 * GD:(g % 2 + 1) * GD], dT[t % 2][:, c * n:(c + 1) * n], w_pool[:, c, :],
                                  start=(a == 0), stop=(a == 1))
                last.then_inc(sem("mix_ps"), 1)

            def hidden_T(v):
                t = units[v][1]
                n = tokens(t)
                w.next("h_ready")
                for c in range(DC):
                    k = c if n == NS else c % 4
                    last = pe.transpose(pb[3 if c // 4 or n == NS else 0][:, k * n:k * n + n], hbuf[0:n, v % 3, c * P:(c + 1) * P],
                                        ident[0:n, 0:n])
                last.then_inc(sem("peer_hT_ps"), 1)

            def queries(v, h, first=False):
                n = tokens(units[v][1])
                if first:
                    w.next("peer_hT_ready")
                    if units[v][1] == 0:
                        w.next("query_w_in", 16, DC)
                        w.next("keys_in", 16)
                for c in range(DC):
                    last = mm(pb[0][0:n, 0:2 * NK], hT[:, c * n:(c + 1) * n], w_q[:, c, bass.ds(h * 2 * NK, 2 * NK)],
                              start=(c == 0), stop=(c == DC - 1))
                last.then_inc(sem("q_ps"), 1)

            def queries_T(v, h):
                n = tokens(units[v][1])
                pe.wait_ge(sem("q_ready"), first_head(v, h) + 1)
                if n == NS:
                    pe.sem_inc(sem("wait_done"), 1)
                for side in range(2):
                    last = pe.transpose(pb[1][:, side * n:(side + 1) * n], q_tok[0:n, side * NK:(side + 1) * NK], ident[0:n, 0:n])
                last.then_inc(sem("qT_ps"), 1)

            def key_scores(v, h):
                n = tokens(units[v][1])
                pe.wait_ge(sem("qT_ready"), first_head(v, h) + 1)
                for side in range(2):
                    last = mm(pb[2][0:n, side * NK:(side + 1) * NK], qT[:, side * n:(side + 1) * n],
                              keysT[:, bass.ds(h * 2 * NK + side * NK, NK)], start=True, stop=True, skip_group_check=True)
                last.then_inc(sem("sco_ps"), 1)

            def expert_turn(u, k):
                n = tokens(units[u][1])
                for j in range(GRP):
                    pe.wait_ge(sem("diag_set"), k * GRP + (before[u] * GRP + GRP + j + 1))
                    pe.wait_ge(sem(f"v_in{j}"), k * 16 + (before[u] + 1) * 16)
                    for half in range(2):
                        last = mm(ybank(u)[half][0:n, :], diag[:, j, 0:n], ring[:, GRP + j, half * 512:(half + 1) * 512],
                                  start=False, stop=False, skip_group_check=True)
                    last.then_inc(sem("v_used"), 1)

            def open_y(u):
                n = tokens(units[u][1])
                if u >= 2:
                    pe.wait_ge(sem("x_routed"), u - 1)
                for half in range(2):
                    for k in range(4):
                        mm(ybank(u)[half][0:n, k * P:(k + 1) * P], zero[:, 0:n], ident, start=True, stop=False, skip_group_check=True)

            def close_y(u):
                n = tokens(units[u][1])
                mm(ybank(u)[1][0:n, 0:64], zero[:, 0:n], ident[:, 0:64], start=False, stop=True, skip_group_check=True)\
                    .then_inc(sem("y_ps"), 1)

            def route(v, u, nxt):
                def head(h, last, turns):
                    for k in range(4):
                        if turns[k] is not None:
                            expert_turn(u, turns[k])
                        if not last:
                            (lambda: queries(v, h + 1), lambda: queries_T(v, h + 1), lambda: key_scores(v, h + 1), lambda: None)[k]()
                        elif nxt is not None:
                            (lambda: hidden_T(nxt), lambda: queries(nxt, 0, True), lambda: queries_T(nxt, 0), lambda: None)[k]()

                own = v == u
                if own or units[u][1]:
                    open_y(u)
                if own:
                    head(0, False, [None] * 4)
                with pe.Fori(1 if own else 0, PH - 1) as h:
                    head(h, False, turns_of(v, u, h))
                head(PH - 1, True, turns_of(v, u, PH - 1))
                if own:
                    for k in range(STEPS // 2 - 2, STEPS // 2):
                        expert_turn(u, k)
                else:
                    close_y(u)
                if nxt is not None:
                    key_scores(nxt, 0)

            pe.sem_inc(sem("v_used"), FREE)
            for u, (l, t) in enumerate(units):
                if t == 0:
                    if l:
                        pool(NT)
                        pool_map(NT)
                    hidden_T(u)
                    queries(u, 0, True)
                    queries_T(u, 0)
                    key_scores(u, 0)
                    route(u, u, u + 1)
                if t < NT:
                    route(u + 1, u, u + 2 if t + 2 <= NT else None)
                else:
                    w.next("route_done")
                    for half in range(2):
                        mm(pb[half][:, :], sel[0:NS, :], hbuf[0:NS, u % 3, half * 512:(half + 1) * 512], start=True, stop=True)
                    mm(pb[2][:, 0:KK], sel[0:NS, :], expert[u % 2][0:NS, :], start=True, stop=True)
                    mm(pb[2][:, KK:2 * KK], sel[0:NS, :], gate[u % 2][0:NS, :], start=True, stop=True, skip_group_check=True)\
                        .then_inc(sem("lane_ps"), 1)
                    if l == 0:
                        for k in range(NT):
                            pool(k)
                            pool_map(k)
                        pe.wait_ge(sem("x_mixed"), 2 * NT + 1)
                    open_y(u)
                    with pe.Fori(0, SSTEPS) as r:
                        expert_turn(u, r)
                    close_y(u)

        @block.scalar
        def _(act):
            w = Turns(act, "act_step")

            def copy(out, in_, name=None):
                w.done(act.activation(out, in_, ACT.Copy), name)

            w.next("c_in", 16)
            w.done(act.activation(hbuf[:, 1, 0:DC * NC], hbuf[:, 0, 0:DC * NC], ACT.Exp, scale=-1.0), "c_exp")

            def copy_hT(t):
                w.next("hT_ps")
                if tokens(t) == P:
                    copy(hT[:, 0:512], pb[4][:, :])
                    copy(hT[:, 512:1024], pb[5][:, :], "hT_ready")
                else:
                    copy(hT[:, 0:DC * NS], pb[4][:, 0:DC * NS], "hT_ready")

            def latents(t):
                n = tokens(t)
                copy_hT(t)
                w.next("z_ps")
                copy(z[0:n, 0:ZW // 2], pb[0][0:n, 0:ZW // 2])
                copy(z[0:n, ZW // 2:ZW], pb[1][0:n, 0:ZW // 2], "z_ready")

            latents(mla_order[0])
            for i, t in enumerate(mla_order):
                n = tokens(t)
                w.next("zT_ps")
                copy(cqT[:, :, 0:n], pb[6][:, 0:QLC * n].rearrange("p (c n) -> p c n", c=QLC))
                if t < NT:
                    copy(krT[0:ROPE, t * P:(t + 1) * P], pb[7][0:ROPE, KLC * n:KLC * n + n])
                copy(latT[:, :, 0:n], pb[7][:, 0:KLC * n].rearrange("p (c n) -> p c n", c=KLC), "zT_ready")
                w.next("qk_ps")
                for b in range(3):
                    copy(qs[0:n, b * 512:(b + 1) * 512], pb[2 + b][0:n, :])
                copy(ks[0:n, 0:512], pb[0][0:n, :])
                copy(ks[0:n, 512:1024], pb[1][0:n, :], "qk_ready")
                if i < NT:
                    latents(mla_order[i + 1])
                w.next("qkT_ps")
                if t == NT:
                    copy(q_rot.rearrange("p (s h) -> p s h", s=NS), pb[7][0:ROPE, 0:64].rearrange("p (h s) -> p s h", h=NH))
                    copy(qnT[:, 0:64], pb[6][:, 0:64], "qkT_ready")
                    w.next("qa_ps")
                    for c in range(KLC):
                        copy(q_abs[:, c, :].rearrange("p (s h) -> p s h", s=NS),
                             pb[2][:, c * 64:(c + 1) * 64].rearrange("p (h s) -> p s h", h=NH), "qa_ready" if c else None)
                    continue
                for b in range(2):
                    copy(qnT[:, b * 512:(b + 1) * 512], pb[6 + b][:, :])
                    copy(qrT[0:ROPE, b * 512:(b + 1) * 512], pb[b][0:ROPE, :])
                    copy(knT[:, 4 * b:4 * b + 4, t * P:(t + 1) * P], pb[2 + b][:, :].rearrange("p (h n) -> p h n", h=4),
                         "qkT_ready" if b else None)
                keys = (t + 1) * P
                def soften(h):
                    w.next("s_neg")
                    w.done(act.activation(probs[:, h % 2, 0:keys], pb[h % 2][:, 0:keys], ACT.Exp, bias=tiny[:, 56 + h % 2:57 + h % 2],
                                          accum_out=tiny[:, 58 + h % 2:59 + h % 2]), "p_ready")
                soften(0)
                for h in range(NH + 1):
                    if h + 1 < NH:
                        soften(h + 1)
                    if h < NH:
                        w.next("pT_ps")
                        copy(pT[h % 2][:, 0:keys], pb[2 + h % 2 * 4][:, 0:keys], "pT_ready")
                    if h:
                        w.next("cT_ps")
                        copy(ctxT[(h - 1) % 2], pb[3 + (h - 1) % 2 * 4][:, 0:256], "cT_ready")
                w.next("o_ps")
                copy(oT[:, 0:512], pb[4][:, :])
                copy(oT[:, 512:1024], pb[5][:, :], "o_ready")

            w.next("smp_clear")

            def square(r, k):
                act.wait_ge(sem("kk_ps"), r * NPG + (k + 1))
                if not (isinstance(r, int) and r == 0 and k < 2):
                    act.wait_ge(sem("k_sums"), r * NPG + (k - 1))
                for half in range(2):
                    last = act.activation(ksq[:, k % 2, half * 512:(half + 1) * 512], pb[2 * (k % 2) + half][:, :], ACT.Square)
                last.then_inc(sem("k_squares"), 1)

            def exp_scores(r):
                act.wait_ge(sem("s_shift"), r + 1)
                act.activation(ps_s[:, :, :], sc_s[:, :, :], ACT.Exp).then_inc(sem("ps_ready"), 1)

            def sequence(r):
                for g in range(NPG):
                    act.wait_ge(sem("page_ps"), r * NPG + (g + 1))
                    act.activation(cachedT[:, g % 2, 0:256], pb[6 + g % 2][:, 0:256], ACT.Copy)
                    act.activation(cachedT[0:ROPE, g % 2, 256:384], pb[6 + g % 2][0:ROPE, 256:384], ACT.Copy).then_inc(sem("pageT"), 1)
                    if g:
                        square(r, g - 1)
                    if g == 7 and not (isinstance(r, int) and r == 0):
                        exp_scores(r - 1)
                square(r, NPG - 1)

            sequence(0)
            with act.Fori(1, NS) as r:
                sequence(r)
            exp_scores(NS - 1)
            w.next("o_ps")
            copy(oT_s[:, :], pb[0][:, 0:64], "o_ready")

            def copy_hidden_T(v):
                n = tokens(units[v][1])
                w.next("peer_hT_ps")
                if n == P:
                    copy(hT[:, 0:512], pb[0][:, :])
                    copy(hT[:, 512:1024], pb[3][:, :], "peer_hT_ready")
                else:
                    copy(hT[:, 0:DC * NS], pb[3][:, 0:DC * NS], "peer_hT_ready")

            def copy_queries(v, h):
                n = tokens(units[v][1])
                act.wait_ge(sem("q_ps"), first_head(v, h) + 1)
                act.activation(q_tok[0:n, :], pb[0][0:n, 0:2 * NK], ACT.Copy).then_inc(sem("q_ready"), 1)

            def copy_queries_T(v, h):
                n = tokens(units[v][1])
                act.wait_ge(sem("qT_ps"), first_head(v, h) + 1)
                act.activation(qT[:, 0:2 * n], pb[1][:, 0:2 * n], ACT.Copy).then_inc(sem("qT_ready"), 1)

            def copy_scores(v, h):
                n = tokens(units[v][1])
                act.wait_ge(sem("sco_ps"), first_head(v, h) + 1)
                act.wait_ge(sem("sides_done"), first_head(v, h) + 1)
                act.activation(sco[0:n, :], pb[2][0:n, 0:2 * NK], ACT.Copy).then_inc(sem("sco_ready"), 1)

            def soften_best(v, h):
                n = tokens(units[v][1])
                act.wait_ge(sem("best_ready"), first_head(v, h) + 1)
                act.activation(soft[0:n, :], best[0:n, :], ACT.Exp, bias=soft_n[0:n, 0:1], accum_out=soft_n[0:n, 1:2])\
                    .then_inc(sem("soft_ready"), 1)

            def expert_turn(u, k):
                n = tokens(units[u][1])
                scale_rows = ident if n == P else selT
                act.wait_ge(sem("dots_set"), k + (before[u] + 1))
                act.activation(acts[:, :], dots[:, :], ACT.Gelu).then_inc(sem("acts_set"), 1)
                act.wait_ge(sem("wts_set"), k + (before[u] + 1))
                for j in range(GRP):
                    act.wait_ge(sem("v_used"), k * GRP + (before[u] * GRP + GRP + j + 1))
                    act.activation(diag[:, j, 0:n], scale_rows, ACT.Copy, scale=wts[:, j:j + 1]).then_inc(sem("diag_set"), 1)

            def route(v, u, nxt):
                def head(h, last, turns):
                    for k in range(4):
                        if turns[k] is not None:
                            expert_turn(u, turns[k])
                        if k == 3:
                            soften_best(v, h)
                        if not last:
                            (lambda: None, lambda: copy_queries(v, h + 1), lambda: copy_queries_T(v, h + 1), lambda: copy_scores(v, h + 1))[k]()
                        elif nxt is not None:
                            (lambda: None, lambda: copy_hidden_T(nxt), lambda: copy_queries(nxt, 0), lambda: copy_queries_T(nxt, 0))[k]()

                own = v == u
                if own:
                    head(0, False, [None] * 4)
                with act.Fori(1 if own else 0, PH - 1) as h:
                    head(h, False, turns_of(v, u, h))
                head(PH - 1, True, turns_of(v, u, PH - 1))
                if own:
                    for k in range(STEPS // 2 - 2, STEPS // 2):
                        expert_turn(u, k)
                if nxt is not None:
                    copy_scores(nxt, 0)

            def copy_pooled(k):
                w.next("dT_ps")
                if k >= 2:
                    act.wait_ge(sem("mix_ps"), NT + k)
                if k < NT:
                    copy(dT[k % 2][:, 0:512], pb[k % 2 * 2][:, :])
                    copy(dT[k % 2][:, 512:1024], pb[k % 2 * 2 + 1][:, :], "dT_ready")
                else:
                    copy(dT[k % 2][:, 0:DC * NS], pb[k % 2 * 2][:, 0:DC * NS], "dT_ready")

            for u, (l, t) in enumerate(units):
                if t == 0:
                    if l:
                        copy_pooled(NT)
                    copy_hidden_T(u)
                    copy_queries(u, 0)
                    copy_queries_T(u, 0)
                    copy_scores(u, 0)
                    route(u, u, u + 1)
                if t < NT:
                    route(u + 1, u, u + 2 if t + 2 <= NT else None)
                else:
                    w.next("lane_ps")
                    for half in range(2):
                        copy(mod_ffn[:, 0, half * 512:(half + 1) * 512], pb[half][:, :], "lane_hidden" if half else None)
                    if l == 0:
                        for k in range(NT):
                            copy_pooled(k)
                    with act.Fori(0, SSTEPS) as r:
                        expert_turn(u, r)

        @block.gpsimd
        def _(pool):
            nc.gpsimd.memset(ones[:, :], 1.0).then_inc(sem("ones_set"), 1)
            for u, (l, t) in enumerate(units):
                if t == 0:
                    pool.wait_ge(sem("head_step"), (first_head(u, 0) + 1) * LINKS_HEAD)
                else:
                    pool.wait_ge(sem("expert_set"), u + 1)
                if u == 0:
                    pool.wait_ge(sem("mix_ps"), NT + 1)
                with pool.Fori(0, (before[u + 1] - before[u]) // 2) as r:
                    for half in range(2):
                        base = before[u] + half
                        pool.wait_ge(sem("u_used"), r * 2 * GRP + (base * GRP + GRP))
                        pool.sem_inc(sem("slot_turn"), 1)
                        pool.wait_ge(sem("v_used"), r * 2 * GRP + (base * GRP + GRP))
                        pool.sem_inc(sem("slot_turn"), 1)
                        src = expert[u % 2].bitcast(U32) if t < NT else e_lane
                        pool.tensor_copy(turn[:, half, :], src[:, bass.ds(r * 2 * GRP + half * GRP, GRP)]).then_inc(sem("turn_set"), 1)
                        pool.wait_ge(sem("turn_set"), r * 2 + (base + 1))
                        pool.sem_inc(sem("slot_turn"), 1)
                        for kind, table, used in (("u", T["peer_u"].rearrange("l e d -> (l e) d"), "u_used"),
                                                  ("v", T["peer_v"].rearrange("l e d -> (l e) d"), "v_used")):
                            for j in range(GRP):
                                pool.wait_ge(sem(used), r * 2 * GRP + (base * GRP + GRP + j + 1))
                                pool.sem_inc(sem("slot_turn"), 1)
                                pool.indirect_dma_start(ring[:, (GRP if kind == "v" else 0) + j, :], None, table,
                                                        bass.IndirectOffsetOnAxis(turn[:, half, j:j + 1], 0))\
                                    .then_inc(sem(f"{kind}_in{j}"), 16)

        @block.vector
        def _(dve):
            w = Turns(dve, "dve_step")
            d = w.done
            tt, ts, stt = dve.tensor_tensor, dve.tensor_scalar, dve.scalar_tensor_tensor

            w.next("c_exp")
            d(ts(hbuf[:, 1, 0:DC * NC], hbuf[:, 1, 0:DC * NC], 1.0, None, ALU.add))
            d(dve.reciprocal(hbuf[:, 1, 0:DC * NC], hbuf[:, 1, 0:DC * NC]))
            d(tt(cact.rearrange("p c n -> p (c n)"), hbuf[:, 0, 0:DC * NC], hbuf[:, 1, 0:DC * NC], ALU.mult), "c_act")
            w.next("b_in", 16, 2)
            for i in range(2 * ADA // 512):
                l, j = divmod(i, ADA // 512)
                w.next("ada_ps")
                if i >= 2:
                    dve.wait_ge(sem(f"ada_out{i % 2}"), 16 * (i // 2))
                bias = ada_bias(l)
                d(tt(ada_stage[:, i % 2, :], pb[i % 2][0:NC, :], bias[:, j * 512:(j + 1) * 512], ALU.add), "ada_row")

            def inverse_root(y, v, t, link):
                link(ts(y.bitcast(I32), v.bitcast(I32), -0.5, float(0x5F3759DF), ALU.mult, ALU.add))
                for _ in range(3):
                    link(tt(t, y, y, ALU.mult))
                    link(stt(t, t, -0.5, v, ALU.mult, ALU.mult))
                    link(stt(y, t, 1.5, y, ALU.add, ALU.mult))

            def set_mods(m, n, gain_=hT, loads=("mods_in", 16, 4)):
                w.next(*loads)
                d(stt(m[0:n, 0, :], m[0:n, 0, :], 1.0, gain_[0:n, :], ALU.add, ALU.mult), "mods_set" if loads[0] == "mods_in" else "smp_mods_set")

            def norm(xt, hb, m, n):
                d(stt(hb[0:n, :], xt[0:n, :], 1.0, xt[0:n, :], ALU.mult, ALU.mult, accum_out=tiny[0:n, 0:1]))
                d(ts(tiny[0:n, 1:2], tiny[0:n, 0:1], 1.0 / D, EPS, ALU.mult, ALU.add))
                inverse_root(tiny[0:n, 2:3], tiny[0:n, 1:2], newton[0:n, 0:1], d)
                d(stt(hb[0:n, :], xt[0:n, :], tiny[0:n, 2:3], m[0:n, 0, :], ALU.mult, ALU.mult))
                d(tt(hb[0:n, :], hb[0:n, :], m[0:n, 1, :], ALU.add), "h_ready")

            def add_mixed(t, gate_, name="x_mixed", banks=None, tmp=hT):
                n = tokens(t)
                for b, bank in enumerate(banks or pb[6:8]):
                    part = slice(b * 512, (b + 1) * 512)
                    d(tt(tmp[0:n, part], bank[0:n, :], gate_[0:n, part], ALU.mult))
                    d(tt(x_tok[0:n, t, part], x_tok[0:n, t, part], tmp[0:n, part], ALU.add), name if b else None)

            w.next("x_in", 16, NT + 1)
            w.next("consts_in", 16)
            set_mods(mod_mix, P)
            set_mods(mod_smp, NS, loads=("smp_mods_in", 16, 3))
            gq, gkv, gkr = gain_all[:, 0:QL], gain_all[:, QL:QL + KL], gain_all[:, QL + KL:ZW]
            gqn, gqr, gkn = (gain_all[:, ZW:ZW + NOPE], gain_all[:, ZW + NOPE:ZW + QH], gain_all[:, ZW + QH:ZW + QH + NOPE])

            def rotate(out1, out2, m1, m2):
                half = ROPE // 2
                d(tt(out1, m1[..., 0:half], m2[..., half:ROPE], ALU.subtract))
                return tt(out2, m2[..., 0:half], m1[..., half:ROPE], ALU.add)

            for i, t in enumerate(mla_order):
                n = tokens(t)
                if i == 0:
                    norm(x_tok[:, t, :], hbuf[:, 0, :], mod_smp, n)
                    w.next("gains_in", 16, 6)
                    d(stt(gqn, gqn, SCALE, gkn, ALU.mult, ALU.mult))
                    d(ts(gqr, gqr, SCALE, None, ALU.mult))
                w.next("z_ready")
                for k, (a, b) in enumerate(((0, QL), (QL, QL + KL), (QL + KL, ZW))):
                    d(stt(sq[0:n, a:b], z[0:n, a:b], 1.0, z[0:n, a:b], ALU.mult, ALU.mult, accum_out=tiny[0:n, 4 + k:5 + k]))
                    d(ts(newton[0:n, 24 + k:25 + k], tiny[0:n, 4 + k:5 + k], 1.0 / (b - a), EPS, ALU.mult, ALU.add))
                inverse_root(tiny[0:n, 4:7], newton[0:n, 24:27], newton[0:n, 0:3], d)
                d(stt(z[0:n, 0:QL], z[0:n, 0:QL], tiny[0:n, 4:5], gq[0:n], ALU.mult, ALU.mult))
                d(stt(rows[0:n, t, 0:KL], z[0:n, QL:QL + KL], tiny[0:n, 5:6], gkv[0:n], ALU.mult, ALU.mult))
                d(stt(z[0:n, QL + KL:ZW], z[0:n, QL + KL:ZW], tiny[0:n, 6:7], gkr[0:n], ALU.mult, ALU.mult))
                w.next("rot_in", 16)
                for k in range(2):
                    d(tt(sq[0:n, k * ROPE:(k + 1) * ROPE], z[0:n, QL + KL:ZW], rot[0:n, k, :], ALU.mult))
                d(rotate(rows[0:n, t, KL:KL + ROPE // 2], rows[0:n, t, KL + ROPE // 2:ROW], sq[0:n, 0:ROPE], sq[0:n, ROPE:2 * ROPE]), "row_ready")
                w.next("qk_ready")
                if i < NT:
                    norm(x_tok[:, mla_order[i + 1], :], hbuf[:, 0, :], mod_mix, P)
                q3 = qs[0:n, :].rearrange("p (h d) -> p h d", h=NH)
                s3 = sq[0:n, :].rearrange("p (h d) -> p h d", h=NH)
                k3 = ks[0:n, :].rearrange("p (h d) -> p h d", h=NH)
                d(tt(sq[0:n, :], qs[0:n, :], qs[0:n, :], ALU.mult))
                d(dve.tensor_reduce(tiny[0:n, 8:16], s3[:, :, 0:NOPE], AX_X, ALU.add))
                d(dve.tensor_reduce(tiny[0:n, 16:24], s3[:, :, NOPE:QH], AX_X, ALU.add))
                d(tt(sq[0:n, 0:D], ks[0:n, :], ks[0:n, :], ALU.mult))
                d(dve.tensor_reduce(tiny[0:n, 24:32], sq[0:n, 0:D].rearrange("p (h d) -> p h d", h=NH), AX_X, ALU.add))
                for a, width in ((8, NOPE), (16, ROPE), (24, NOPE)):
                    d(ts(newton[0:n, a + 16:a + 24], tiny[0:n, a:a + 8], 1.0 / width, EPS, ALU.mult, ALU.add))
                inverse_root(tiny[0:n, 8:32], newton[0:n, 24:48], newton[0:n, 0:24], d)

                def heads(a, width):
                    return tiny[0:n, a:a + 8].unsqueeze(2).to_broadcast([n, NH, width])

                def over_heads(g, width):
                    return g[0:n, :].unsqueeze(1).to_broadcast([n, NH, width])

                d(tt(q3[:, :, 0:NOPE], q3[:, :, 0:NOPE], heads(8, NOPE), ALU.mult))
                d(tt(q3[:, :, 0:NOPE], q3[:, :, 0:NOPE], over_heads(gqn, NOPE), ALU.mult))
                d(tt(q3[:, :, NOPE:QH], q3[:, :, NOPE:QH], heads(16, ROPE), ALU.mult))
                d(tt(q3[:, :, NOPE:QH], q3[:, :, NOPE:QH], over_heads(gqr, ROPE), ALU.mult))
                m = [sq[0:n, k * 512:(k + 1) * 512].rearrange("p (h d) -> p h d", h=NH) for k in range(2)]
                for k in range(2):
                    d(tt(m[k], q3[:, :, NOPE:QH], rot[0:n, k, :].unsqueeze(1).to_broadcast([n, NH, ROPE]), ALU.mult))
                d(rotate(q3[:, :, NOPE:NOPE + 32], q3[:, :, NOPE + 32:QH], m[0], m[1]))
                d(tt(k3, k3, heads(24, NOPE), ALU.mult), "qk_norm")
                if t == NT:
                    d(tt(sq[0:n, 0:D].rearrange("p (h d) -> p h d", h=NH), q3[:, :, 0:NOPE], k3, ALU.mult))
                    d(dve.tensor_reduce(tiny[0:n, 32:40], sq[0:n, 0:D].rearrange("p (h d) -> p h d", h=NH), AX_X, ALU.add))
                    d(tt(sq[0:n, 0:512].rearrange("p (h d) -> p h d", h=NH), q3[:, :, NOPE:QH],
                         rows[0:n, NT, KL:ROW].unsqueeze(1).to_broadcast([n, NH, ROPE]), ALU.mult))
                    d(dve.tensor_reduce(tiny[0:n, 40:48], sq[0:n, 0:512].rearrange("p (h d) -> p h d", h=NH), AX_X, ALU.add))
                    d(tt(tiny[0:n, 40:48], tiny[0:n, 40:48], tiny[0:n, 32:40], ALU.add), "own_ready")
                    continue
                keys = (t + 1) * P
                def row_max(h):
                    w.next("s_ps")
                    b = pb[h % 2]
                    d(tt(b[:, t * P:keys], b[:, t * P:keys], causal, ALU.add))
                    d(dve.tensor_reduce(tiny[:, 60:61], b[:, 0:keys], AX_X, ALU.max))
                    d(ts(tiny[:, 56 + h % 2:57 + h % 2], tiny[:, 60:61], -1.0, None, ALU.mult), "s_neg")
                row_max(0)
                for h in range(NH):
                    w.next("p_ready")
                    d(dve.reciprocal(tiny[:, 61:62], tiny[:, 58 + h % 2:59 + h % 2]))
                    d(ts(probs[:, h % 2, 0:keys], probs[:, h % 2, 0:keys], tiny[:, 61:62], None, ALU.mult), "p_norm")
                    if h + 1 < NH:
                        row_max(h + 1)
                w.next("mix_ps")
                add_mixed(t, mod_mix[:, 2, :])

            d(dve.memset(sc_s[:, :, :], LOWEST))
            for b in range(2):
                d(dve.memset(cached[:, b, NPG, :], 0.0), "smp_clear" if b else None)
            w.next("own_in", 16)
            d(dve.memset(zero, 0.0), "zero_set")
            LINKS = 14

            def chain(r, start):
                at = [start]

                def e(ins, name=None):
                    if name is None:
                        at[0] += 1
                        ins.then_inc(sem("smp_step"), 1)
                        dve.wait_ge(sem("smp_step"), r * LINKS + at[0])
                    else:
                        ins.then_inc(sem(name), 1)
                        dve.wait_ge(sem(name), r + 1)
                return e, at

            def final_scores(r, b):
                dve.wait_ge(sem("k_sums"), r * NPG + NPG)
                e, at = chain(r, 0)
                e(ts(kss[:, :], kss[:, :], 1.0 / NOPE, EPS, ALU.mult, ALU.add))
                inverse_root(krn[:, :], kss[:, :], krt[:, :], e)
                dve.wait_ge(sem("kk_ps"), r * NPG + NPG)
                both = pb[4 + b][:, 0:256].rearrange("p (g a h) -> p g a h", g=NPG, a=2)
                e(tt(sc_s[:, 0:NPG, :], both[:, :, 0, :], krn[:, :].rearrange("p (g h) -> p g h", g=NPG), ALU.mult))
                e(tt(sc_s[:, 0:NPG, :], sc_s[:, 0:NPG, :], both[:, :, 1, :], ALU.add))
                e(ts(sc_s[0:1, NPG, :], s_own[:, bass.ds(r * NH, NH)], 1.0, None, ALU.mult))
                e(dve.tensor_reduce(tiny[:, 0:NH], sc_s[:, :, :].rearrange("p g h -> p h g"), AX_X, ALU.max), "s_max")
                assert at[0] == LINKS

            def top(r, b):
                dve.wait_ge(sem("max_ps"), r + 1)
                dve.tensor_reduce(tiny[0:NH, 8:9], pb[4 + b][0:NH, 0:P], AX_X, ALU.max).then_inc(sem("smp_tail"), 1)
                dve.wait_ge(sem("smp_tail"), r * 2 + 1)
                ts(tiny[0:NH, 16:24], ident[0:NH, 0:NH], tiny[0:NH, 8:9], None, ALU.mult).then_inc(sem("max_diag"), 1)

            def shift(r, b):
                dve.wait_ge(sem("maxb_ps"), r + 1)
                tt(sc_s[:, :, :], sc_s[:, :, :], pb[4 + b][:, P:P + NH].unsqueeze(1).to_broadcast([P, NPG + 1, NH]), ALU.subtract)\
                    .then_inc(sem("s_shift"), 1)

            def sums(r, b):
                dve.wait_ge(sem("ps_ready"), r + 1)
                dve.tensor_reduce(tiny[:, 24:24 + NH], ps_s[:, :, :].rearrange("p g h -> p h g"), AX_X, ALU.add).then_inc(sem("p_sum"), 1)

            def contexts(r, b):
                dve.wait_ge(sem("ctx_ps"), r + 1)
                dve.reciprocal(tiny[0:NH, 32:33], pb[4 + b][0:NH, 144:145]).then_inc(sem("smp_tail"), 1)
                dve.wait_ge(sem("smp_tail"), r * 2 + 2)
                ts(ctx_n[0:NH, :], pb[4 + b][0:NH, 160:160 + KL], tiny[0:NH, 32:33], None, ALU.mult).then_inc(sem("ctx_norm"), 1)

            def keep_context(r, b):
                dve.wait_ge(sem("ctx_cols"), r + 1)
                ts(ctx_s[:, :, :, bass.ds(r, 1)].rearrange("p c h s -> p c (h s)"), pb[4 + b][:, 432:432 + 2 * NH].rearrange("p (c h) -> p c h", c=KLC),
                   1.0, None, ALU.mult).then_inc(sem("ctx_ready"), 1)

            tail_steps = {4: top, 6: shift, 8: sums, 11: contexts, 14: keep_context}

            def sequence(r, b):
                for g in range(NPG):
                    dve.wait_ge(sem("k_squares"), r * NPG + (g + 1))
                    dve.tensor_reduce(kss[:, g * NH:(g + 1) * NH], ksq[:, g % 2, :].rearrange("p (h d) -> p h d", h=NH), AX_X, ALU.add)\
                        .then_inc(sem("k_sums"), 1)
                    if g in tail_steps and not (isinstance(r, int) and r == 0):
                        tail_steps[g](r - 1, 1 - b)
                final_scores(r, b)

            dve.sem_inc(sem("ctx_ready"), 1)
            sequence(0, 0)
            with dve.Fori(0, NS // 2 - 1) as i:
                sequence(i * 2 + 1, 1)
                sequence(i * 2 + 2, 0)
            sequence(NS - 1, 1)
            for step in tail_steps.values():
                step(NS - 1, 1)
            dve.wait_ge(sem("ctx_ready"), NS + 1)
            w.next("mods_in", 16)
            set_mods(mod_ffn, P, gain)
            norm(x_tok[:, 0, :], hbuf[:, 0, :], mod_ffn, P)
            w.next("mix_ps")
            add_mixed(NT, mod_smp[:, 2, :], tmp=mixed)

            def rank(v, h, last, nxt):
                l, t = units[v]
                n = tokens(t)
                G = first_head(v, h)
                at = [0]

                def e(ins, name=None):
                    if name is None:
                        at[0] += 1
                        ins.then_inc(sem("head_step"), 1)
                        dve.wait_ge(sem("head_step"), G * LINKS_HEAD + at[0])
                    else:
                        ins.then_inc(sem(name), 1)
                        dve.wait_ge(sem(name), G + (2 if name == "sides_done" else 1))

                def need(step, plain=False):
                    dve.wait_ge(sem("head_step"), G * LINKS_HEAD + step)
                    if plain:
                        dve.sem_inc(sem("link_done"), 1)

                def step(ins):
                    at[0] += 1
                    ins.then_inc(sem("head_step"), 1)
                    return at[0]

                def top_first(src, rest, v8, i8):
                    m = [step(dve.max(v[:, 0:8], a)) for a, v in zip(src, v8)]
                    for a, r, v, i_, m_ in zip(src, rest, v8, i8, m):
                        need(m_, True)
                        dve.max_index(i_[:, 0:8], v[:, 0:8], a)
                        step(dve.match_replace(r, v[:, 0:8], a, LOWEST))

                def top_second(rest, v8, i8):
                    c, k = at[0], len(rest)
                    for j, (r, v) in enumerate(zip(rest, v8)):
                        need(c - k + j + 1, True)
                        step(dve.max(v[:, 8:16], r))
                    for j, (r, v, i_) in enumerate(zip(rest, v8, i8)):
                        need(c + j + 1, True)
                        step(dve.max_index(i_[:, 8:16], v[:, 8:16], r))

                sides = range(2)
                side_src = [sco[0:n, k * NK:(k + 1) * NK] for k in sides]
                side_rest = [cand[0:n, k * NK:(k + 1) * NK] for k in sides]
                side_v = [vals[0:n, k * TOPK:(k + 1) * TOPK] for k in sides]
                side_i = [idx[0:n, k * TOPK:(k + 1) * TOPK] for k in sides]

                def part0():
                    if last and nxt is not None:
                        norm(x_tok[:, units[nxt][1], :], hbuf[:, nxt % 3, :], mod_smp if units[nxt][1] == NT else mod_ffn, tokens(units[nxt][1]))
                    dve.wait_ge(sem("sco_ready"), G + 1)
                    dve.sem_inc(sem("link_done"), 1)
                    top_first(side_src, side_rest, side_v, side_i)

                def part1():
                    top_second(side_rest, side_v, side_i)
                    need(at[0])
                    e(dve.tensor_copy(idxf[0:n, :], idx[0:n, :]), "sides_done")

                def part2():
                    e(tt(cand[0:n, :].rearrange("p (i j) -> p i j", i=TOPK), vals[0:n, 0:TOPK].unsqueeze(2).to_broadcast([n, TOPK, TOPK]),
                         vals[0:n, TOPK:2 * TOPK].unsqueeze(1).to_broadcast([n, TOPK, TOPK]), ALU.add))
                    dve.sem_inc(sem("link_done"), 1)
                    top_first([cand[0:n, :]], [hits[0:n, :]], [best[0:n, :]], [flat[0:n, :]])
                    top_second([hits[0:n, :]], [best[0:n, :]], [flat[0:n, :]])
                    need(at[0])
                    e(ts(soft_n[0:n, 0:1], best[0:n, 0:1], -1.0, None, ALU.mult), "best_ready")

                def part3():
                    for k, (amount, op) in enumerate(((4, ALU.logical_shift_right), (TOPK - 1, ALU.bitwise_and))):
                        step(ts(place[0:n, k * TOPK:(k + 1) * TOPK].bitcast(U32), flat[0:n, :], amount, None, op))
                    need(at[0])
                    e(dve.tensor_copy(place[0:n, 2 * TOPK:4 * TOPK], place[0:n, 0:2 * TOPK].bitcast(U32)))
                    hot = [a[0:n, :].rearrange("p (m k) -> p m k", m=TOPK) for a in (hits, cand)]
                    first = at[0]
                    for k in sides:
                        step(tt(hot[k], place[0:n, (2 + k) * TOPK:(3 + k) * TOPK].unsqueeze(2).to_broadcast([n, TOPK, TOPK]),
                                iota[0:n, :].unsqueeze(1).to_broadcast([n, TOPK, TOPK]), ALU.is_equal))
                    for k in sides:
                        need(first + 1 + k)
                        step(tt(hot[k], hot[k], idxf[0:n, k * TOPK:(k + 1) * TOPK].unsqueeze(1).to_broadcast([n, TOPK, TOPK]), ALU.mult))
                    for k in sides:
                        need(first + 3 + k)
                        step(dve.tensor_reduce(e_side[0:n, k * TOPK:(k + 1) * TOPK], hot[k], AX_X, ALU.add))
                    need(first + 5)
                    e(ts(e_side[0:n, 0:TOPK], e_side[0:n, 0:TOPK], float(NK), float(l * NK * NK), ALU.mult, ALU.add))
                    dst = expert[v % 2] if t == NT else expert[v % 2].bitcast(U32)
                    e(tt(dst[0:n, bass.ds(h * TOPK, TOPK)], e_side[0:n, 0:TOPK], e_side[0:n, TOPK:2 * TOPK], ALU.add))
                    dve.wait_ge(sem("soft_ready"), G + 1)
                    e(dve.reciprocal(soft_n[0:n, 2:3], soft_n[0:n, 1:2]))
                    e(ts(gate[v % 2][0:n, bass.ds(h * TOPK, TOPK)], soft[0:n, :], soft_n[0:n, 2:3], None, ALU.mult))
                    assert at[0] == LINKS_HEAD, at[0]

                return part0, part1, part2, part3

            def expert_turn(u, k):
                t = units[u][1]
                hb = hbuf[:, u % 3, :] if t < NT else mod_ffn[:, 0, :]
                for j in range(GRP):
                    dve.wait_ge(sem(f"u_in{j}"), k * 16 + (before[u] + 1) * 16)
                    if j == 0:
                        dve.wait_ge(sem("acts_set"), k + (before[u] + 1))
                    dve.tensor_tensor_reduce(ring[:, j, :], ring[:, j, :], hb, 1.0, 0.0, ALU.mult, ALU.add, dots[:, j:j + 1])\
                        .then_inc(sem("u_used"), 1)
                dve.wait_ge(sem("u_used"), k * GRP + (before[u] * GRP + FREE + GRP))
                dve.sem_inc(sem("dots_set"), 1)

            def turn_weights(u, k):
                g_all = gate[u % 2] if units[u][1] < NT else g_lane
                dve.wait_ge(sem("acts_set"), k + (before[u] + 2))
                dve.wait_ge(sem("diag_set"), k * GRP + (before[u] * GRP + GRP))
                tt(wts[:, :], acts[:, :], g_all[:, bass.ds(k * GRP, GRP)], ALU.mult).then_inc(sem("wts_set"), 1)

            def route(v, u, nxt):
                def head(h, last, turns):
                    for k, part in enumerate(rank(v, h, last, nxt)):
                        if turns[k] is not None:
                            expert_turn(u, turns[k])
                        if units[u][1]:
                            turn_weights(u, turns[k])
                        part()
                        if not units[u][1] and turns[k] is not None:
                            turn_weights(u, turns[k])

                own = v == u
                if own:
                    head(0, False, [None] * 4)
                with dve.Fori(1 if own else 0, PH - 1) as h:
                    head(h, False, turns_of(v, u, h))
                head(PH - 1, True, turns_of(v, u, PH - 1))
                if own:
                    for k in range(STEPS // 2 - 2, STEPS // 2):
                        expert_turn(u, k)
                        turn_weights(u, k)
                if units[v][1] < NT:
                    dve.sem_inc(sem("expert_set"), 1)
                else:
                    dve.sem_inc(sem("route_done"), 1)

            dve.sem_inc(sem("u_used"), FREE)
            dve.sem_inc(sem("acts_set"), 1)
            dve.sem_inc(sem("diag_set"), GRP)
            dve.sem_inc(sem("sides_done"), 1)
            for u, (l, t) in enumerate(units):
                if t == 0:
                    if l:
                        set_mods(mod_smp, NS, gain, ("smp_mods_in", 16, 3))
                        norm(x_tok[:, NT, :], hbuf[:, NT % 3, :], mod_smp, NS)
                        w.next("gain_s_in", 16)
                        d(tt(mod_smp[0:NS, 2, :], mod_smp[0:NS, 2, :], pool_gain_s[0:NS], ALU.mult))
                        w.next("mix_ps")
                        add_mixed(NT, mod_smp[:, 2, :], "x_mixed", ybank(NT))
                        set_mods(mod_ffn, P, gain)
                        w.next("hbuf_free")
                        norm(x_tok[:, t, :], hbuf[:, u % 3, :], mod_ffn, P)
                    set_mods(mod_smp, NS, gain, ("smp_mods_in", 16, 3))
                    if not l:
                        set_mods(mod_mix, P, gain)
                        w.next("pool_gain_in", 16)
                        d(tt(mod_mix[:, 2, :], mod_mix[:, 2, :], pool_gain, ALU.mult))
                    route(u, u, u + 1)
                if t < NT:
                    route(u + 1, u, u + 2 if t + 2 <= NT else None)
                else:
                    w.next("lane_ps")
                    pick = lane_pick[:, :].rearrange("p (a h k) -> p a h k", a=2, h=PH)
                    d(tt(pick, pb[2][:, 0:2 * KK].rearrange("p (a h k) -> p a h k", a=2, h=PH), lane.unsqueeze(1).unsqueeze(1).to_broadcast([P, 2, PH, TOPK]), ALU.mult))
                    d(dve.tensor_reduce(g_lane[:, :], pick[:, 1], AX_X, ALU.add))
                    d(dve.tensor_reduce(e_pick[:, :], pick[:, 0], AX_X, ALU.add))
                    d(ts(e_lane[:, :], e_pick[:, :], 1.0, None, ALU.mult), "expert_set")
                    w.next("lane_hidden")
                    if l == 0:
                        norm(x_tok[:, 0, :], hbuf[:, 0, :], mod_mix, P)
                        for k in range(NT):
                            if k + 1 < NT:
                                norm(x_tok[:, k + 1, :], hbuf[:, (k + 1) % 3, :], mod_mix, P)
                            w.next("mix_ps")
                            add_mixed(k, mod_mix[:, 2, :], "x_mixed", ybank(k))
                    with dve.Fori(0, SSTEPS) as r:
                        expert_turn(u, r)
                        turn_weights(u, r)
                w.next("y_ps")
                add_mixed(t, (mod_smp if t == NT else mod_ffn)[:, 2, :], "x_routed", ybank(u), mixed)


_INS = ["x_prompt", "x_sample", "cache_mla", "state_pool", "page_table", "norm_mix", "norm_ffn", "w_ada", "b_ada", "w_mla_in",
        "g_q_lat", "g_kv_lat", "w_uq", "w_uk", "w_uv", "g_qn_nope", "g_qn_rope", "g_kn_nope", "g_kn_rope", "w_mla_out",
        "w_pool", "pool_scale", "w_peer_q", "peer_u", "peer_v"]
_OUTS = [("y_p", (1, SEQ, D)), ("y_s", (NS, 1, D)), ("rows_p", (1, 1, SEQ, ROW)), ("rows_s", (1, NS, 1, ROW)),
         ("pst_p", (1, 1, STATE, D)), ("pst_s", (1, NS, STATE, D))]


def kernel(**inputs):
    import concourse.bacc as bacc
    from concourse.bass_utils import run_bass_kernel_spmd

    nc = bacc.Bacc("TRN2", target_bir_lowering=False, num_devices=1)
    host = {name: np.ascontiguousarray(inputs[name]) for name in _INS}
    host["cT"] = np.ascontiguousarray(np.concatenate([inputs["c_sample"], inputs["c_prompt"]], axis=0).T)
    host["w_ukT"] = np.ascontiguousarray(np.transpose(inputs["w_uk"][0], (2, 1, 0)))
    keys = np.transpose(inputs["peer_subkeys"], (0, 4, 1, 2, 3))
    host["subkeysT"] = np.ascontiguousarray(keys.reshape(DEPTH, PEER_HALF, NQ, NK))
    host.update(shape_constants())
    arrays, T, O = {}, {}, {}
    for name, a in host.items():
        arrays["in_" + name] = a
        T[name] = nc.dram_tensor("in_" + name, a.shape, mybir.dt.from_np(a.dtype), kind="ExternalInput").ap()
    for name, shape in _OUTS:
        O[name] = nc.dram_tensor("out_" + name, shape, F32, kind="ExternalOutput").ap()
    decoder_step(nc, T, O)
    r = run_bass_kernel_spmd(nc, [arrays], core_ids=[0])
    return tuple(r.results[0]["out_" + name] for name, _ in _OUTS)
```
